# Optimizing a Trainium2 kernel written in Bass

```python
import numpy as np
import jax, jax.numpy as jnp
from jax import lax

D_MODEL = 1024
BATCH = 1
SEQ = 256
DEPTH = 2

N_A_LAYERS = DEPTH // 2
N_B_LAYERS = DEPTH - N_A_LAYERS
EPS = 1e-6
NEG_INF = -1e30
ROPE_THETA = 10000.0

GLA_HEADS = 4
GLA_DK = D_MODEL // (2 * GLA_HEADS)
GLA_DV = D_MODEL // GLA_HEADS
GLA_GATE_RANK = 16
GLA_TAU = 16.0
GLA_CHUNK = 64
GLA_IN = 2 * GLA_HEADS * GLA_DK + 2 * GLA_HEADS * GLA_DV + GLA_GATE_RANK

NSA_HEADS = 16
NSA_KV_HEADS = 4
NSA_GROUP = NSA_HEADS // NSA_KV_HEADS
NSA_HEAD_DIM = D_MODEL // NSA_HEADS
CMP_BLOCK = 32
CMP_STRIDE = 16
CMP_HIDDEN = 4 * NSA_HEAD_DIM
SEL_BLOCK = 64
SEL_TOPK = 16
WINDOW = 512
NSA_QCHUNK = 32
NSA_IN = NSA_HEADS * NSA_HEAD_DIM + 3 * NSA_HEADS
NSA_KV_OUT = 6 * NSA_KV_HEADS * NSA_HEAD_DIM
FORCE_SCORE = 1e4

FFN_DIM = 2816
CONV_WIDTH = 3


def rmsnorm(x, g):
    x32 = x.astype(jnp.float32)
    y = x32 * lax.rsqrt(jnp.mean(x32 * x32, axis=-1, keepdims=True) + EPS)
    return (y * g).astype(x.dtype)

def rope(x, pos):
    half = x.shape[-1] // 2
    inv = ROPE_THETA ** (-jnp.arange(half, dtype=jnp.float32) / half)
    ang = pos.astype(jnp.float32)[:, None] * inv[None, :]
    cos, sin = jnp.cos(ang), jnp.sin(ang)
    x1 = x[..., :half].astype(jnp.float32)
    x2 = x[..., half:].astype(jnp.float32)
    return jnp.concatenate([x1 * cos - x2 * sin, x1 * sin + x2 * cos], axis=-1).astype(x.dtype)

def masked_softmax(s, mask):
    s = jnp.where(mask, s.astype(jnp.float32), NEG_INF)
    return jnp.where(mask, jax.nn.softmax(s, axis=-1), 0.0)

def conv_ffn(h, w_up, conv_w, conv_b, w_down):
    S = h.shape[1]
    u = h @ w_up
    up = jnp.pad(u, ((0, 0), (CONV_WIDTH - 1, 0), (0, 0)))
    u = conv_b + up[:, 0:S] * conv_w[0]
    for j in range(1, CONV_WIDTH):
        u = u + up[:, j:j + S] * conv_w[j]
    gate, val = jnp.split(u, 2, axis=-1)
    return (jax.nn.silu(gate) * val) @ w_down

def gla_mixer(h, w_in, w_alpha_up, b_alpha, g_out, w_o):
    Bsz, S, _ = h.shape
    H, DK, DV, C = GLA_HEADS, GLA_DK, GLA_DV, GLA_CHUNK
    NC = S // C
    proj = h @ w_in
    splits = [H * DK, 2 * H * DK, 2 * H * DK + H * DV, 2 * H * DK + 2 * H * DV]
    q, k, v, r, a_low = jnp.split(proj, splits, axis=-1)
    log_a = jax.nn.log_sigmoid((a_low @ w_alpha_up + b_alpha).astype(jnp.float32)) / GLA_TAU

    def to_chunks(t, d):
        return t.astype(jnp.float32).reshape(Bsz, NC, C, H, d).transpose(1, 0, 3, 2, 4)

    qc = to_chunks(q, DK) * DK ** -0.5
    kc = to_chunks(k, DK)
    vc = to_chunks(v, DV)
    gc = to_chunks(log_a, DK)
    causal = jnp.tril(jnp.ones((C, C), dtype=bool))[:, :, None]

    def step(state, inp):
        q_, k_, v_, g_ = inp
        b = jnp.cumsum(g_, axis=2)
        o_inter = jnp.einsum('bhtk,bhkv->bhtv', q_ * jnp.exp(b), state)
        diff = b[:, :, :, None, :] - b[:, :, None, :, :]
        decay = jnp.where(causal, jnp.exp(jnp.minimum(diff, 0.0)), 0.0)
        att = jnp.einsum('bhtk,bhsk,bhtsk->bhts', q_, k_, decay)
        o_intra = jnp.einsum('bhts,bhsv->bhtv', att, v_)
        b_last = b[:, :, -1:, :]
        new_state = state * jnp.exp(b_last[:, :, 0, :, None]) + jnp.einsum(
            'bhsk,bhsv->bhkv', k_ * jnp.exp(b_last - b), v_)
        return new_state, o_inter + o_intra

    state0 = jnp.zeros((Bsz, H, DK, DV), jnp.float32)
    _, o = lax.scan(step, state0, (qc, kc, vc, gc))
    o = o.transpose(1, 0, 3, 2, 4).reshape(Bsz, S, H, DV)
    o = o * lax.rsqrt(jnp.mean(o * o, axis=-1, keepdims=True) + EPS) * g_out
    o = o.reshape(Bsz, S, H * DV).astype(h.dtype) * jax.nn.silu(r)
    return o @ w_o

def compress_blocks(t_raw, pe, w1, w2):
    Bsz, Hk, S, Dh = t_raw.shape
    n_cmp = (S - CMP_BLOCK) // CMP_STRIDE + 1
    idx = np.arange(n_cmp)[:, None] * CMP_STRIDE + np.arange(CMP_BLOCK)[None, :]
    blocks = (t_raw[:, :, idx, :] + pe).reshape(Bsz, Hk, n_cmp, CMP_BLOCK * Dh)
    return jax.nn.gelu(blocks @ w1) @ w2

def cmp_to_sel_weights(S):
    n_cmp = (S - CMP_BLOCK) // CMP_STRIDE + 1
    n_sel = S // SEL_BLOCK
    c0 = np.arange(n_cmp)[:, None] * CMP_STRIDE
    s0 = np.arange(n_sel)[None, :] * SEL_BLOCK
    ov = np.clip(np.minimum(c0 + CMP_BLOCK, s0 + SEL_BLOCK) - np.maximum(c0, s0), 0, None)
    return (ov / CMP_BLOCK).astype(np.float32)

def nsa_shared_kv(x, g_kv, w_kv, pe_k, pe_v, wk1, wk2, wv1, wv2):
    Bsz, S, _ = x.shape
    hn = rmsnorm(x, g_kv)
    kv = (hn @ w_kv).reshape(Bsz, S, 6, NSA_KV_HEADS, NSA_HEAD_DIM).transpose(2, 0, 3, 1, 4)
    pos = jnp.arange(S)
    k_cmp = compress_blocks(kv[0], pe_k, wk1, wk2)
    v_cmp = compress_blocks(kv[1], pe_v, wv1, wv2)
    k_sel = rope(kv[2], pos)
    k_win = rope(kv[4], pos)
    return k_cmp, v_cmp, k_sel, kv[3], k_win, kv[5]

gather_blocks = jax.vmap(jax.vmap(lambda blocks, ix: blocks[ix]))

def nsa_mixer(h, w_in, w_o, k_cmp, v_cmp, k_sel, v_sel, k_win, v_win):
    Bsz, S, _ = h.shape
    Hk, G, Dh, SB, QC = NSA_KV_HEADS, NSA_GROUP, NSA_HEAD_DIM, SEL_BLOCK, NSA_QCHUNK
    n_cmp = k_cmp.shape[2]
    n_sel = S // SB
    top = min(SEL_TOPK, n_sel)
    scale = Dh ** -0.5
    pos = jnp.arange(S)
    proj = h @ w_in
    q = proj[..., :NSA_HEADS * Dh].reshape(Bsz, S, Hk, G, Dh).transpose(0, 2, 3, 1, 4)
    gates = jax.nn.sigmoid(proj[..., NSA_HEADS * Dh:].astype(jnp.float32))
    gates = gates.reshape(Bsz, S, 3, Hk, G).transpose(2, 0, 3, 4, 1)[..., None]

    cmp_end = jnp.arange(n_cmp) * CMP_STRIDE + CMP_BLOCK - 1
    p_cmp = masked_softmax(jnp.einsum('bkgsd,bknd->bkgsn', q, k_cmp) * scale,
                           cmp_end[None, :] <= pos[:, None])
    o_cmp = jnp.einsum('bkgsn,bknd->bkgsd', p_cmp, v_cmp)

    imp = jnp.einsum('bkgsn,nj->bksj', p_cmp, jnp.asarray(cmp_to_sel_weights(S)))
    blk = jnp.arange(n_sel)[None, :]
    cur = (pos // SB)[:, None]
    forced = (blk == 0) | (blk == cur) | (blk == cur - 1)
    imp = jnp.where(blk > cur, -1.0, jnp.where(forced, FORCE_SCORE, imp))
    _, sel_idx = lax.top_k(imp, top)

    q_rot = rope(q, pos)
    k_blocks = k_sel.reshape(Bsz, Hk, n_sel, SB, Dh)
    v_blocks = v_sel.reshape(Bsz, Hk, n_sel, SB, Dh)
    pad = ((0, 0), (0, 0), (WINDOW, 0), (0, 0))
    k_win_pad = jnp.pad(k_win, pad)
    v_win_pad = jnp.pad(v_win, pad)

    def chunk(c):
        t0 = c * QC
        qc = lax.dynamic_slice_in_dim(q_rot, t0, QC, axis=3)
        qpos = t0 + jnp.arange(QC)
        idx = lax.dynamic_slice_in_dim(sel_idx, t0, QC, axis=2)
        ks = gather_blocks(k_blocks, idx).reshape(Bsz, Hk, QC, top * SB, Dh)
        vs = gather_blocks(v_blocks, idx).reshape(Bsz, Hk, QC, top * SB, Dh)
        kpos = (idx[..., None] * SB + jnp.arange(SB)).reshape(Bsz, Hk, 1, QC, top * SB)
        p_sel = masked_softmax(jnp.einsum('bkgqd,bkqmd->bkgqm', qc, ks) * scale,
                               kpos <= qpos[:, None])
        o_sel = jnp.einsum('bkgqm,bkqmd->bkgqd', p_sel, vs)
        kw = lax.dynamic_slice_in_dim(k_win_pad, t0, WINDOW + QC, axis=2)
        vw = lax.dynamic_slice_in_dim(v_win_pad, t0, WINDOW + QC, axis=2)
        kwpos = t0 - WINDOW + jnp.arange(WINDOW + QC)
        dist = qpos[:, None] - kwpos[None, :]
        win_mask = (kwpos[None, :] >= 0) & (dist >= 0) & (dist < WINDOW)
        p_win = masked_softmax(jnp.einsum('bkgqd,bknd->bkgqn', qc, kw) * scale, win_mask)
        o_win = jnp.einsum('bkgqn,bknd->bkgqd', p_win, vw)
        return o_sel, o_win

    o_sel, o_win = lax.map(chunk, jnp.arange(S // QC))
    o_sel = jnp.moveaxis(o_sel, 0, 3).reshape(Bsz, Hk, G, S, Dh)
    o_win = jnp.moveaxis(o_win, 0, 3).reshape(Bsz, Hk, G, S, Dh)
    o = gates[0] * o_cmp + gates[1] * o_sel + gates[2] * o_win
    o = o.transpose(0, 3, 1, 2, 4).reshape(Bsz, S, NSA_HEADS * Dh).astype(h.dtype)
    return o @ w_o

def first_inputs(seed: int = 0) -> dict:
    key = jax.random.key(seed)
    ks = jax.random.split(key, 32)
    f32 = jnp.float32

    def nrm(k, shape, fan_in):
        return jax.random.normal(k, shape, f32) * fan_in ** -0.5

    def gain(k, shape):
        return 1.0 + 0.02 * jax.random.normal(k, shape, f32)

    two_f = 2 * FFN_DIM
    return {
        'x': jax.random.normal(ks[0], (BATCH, SEQ, D_MODEL), f32),
        'norm_mix': gain(ks[1], (DEPTH, D_MODEL)),
        'norm_ffn': gain(ks[2], (DEPTH, D_MODEL)),
        'gla_w_in': nrm(ks[3], (N_A_LAYERS, D_MODEL, GLA_IN), D_MODEL),
        'gla_w_alpha_up': nrm(ks[4], (N_A_LAYERS, GLA_GATE_RANK, GLA_HEADS * GLA_DK), GLA_GATE_RANK),
        'gla_b_alpha': 0.1 * jax.random.normal(ks[5], (N_A_LAYERS, GLA_HEADS * GLA_DK), f32),
        'gla_norm': gain(ks[6], (N_A_LAYERS, GLA_HEADS, GLA_DV)),
        'gla_w_o': nrm(ks[7], (N_A_LAYERS, GLA_HEADS * GLA_DV, D_MODEL), GLA_HEADS * GLA_DV),
        'kv_norm': gain(ks[8], (D_MODEL,)),
        'nsa_w_kv': nrm(ks[9], (D_MODEL, NSA_KV_OUT), D_MODEL),
        'cmp_pe_k': 0.02 * jax.random.normal(ks[10], (CMP_BLOCK, NSA_HEAD_DIM), f32),
        'cmp_pe_v': 0.02 * jax.random.normal(ks[11], (CMP_BLOCK, NSA_HEAD_DIM), f32),
        'cmp_k_w1': nrm(ks[12], (CMP_BLOCK * NSA_HEAD_DIM, CMP_HIDDEN), CMP_BLOCK * NSA_HEAD_DIM),
        'cmp_k_w2': nrm(ks[13], (CMP_HIDDEN, NSA_HEAD_DIM), CMP_HIDDEN),
        'cmp_v_w1': nrm(ks[14], (CMP_BLOCK * NSA_HEAD_DIM, CMP_HIDDEN), CMP_BLOCK * NSA_HEAD_DIM),
        'cmp_v_w2': nrm(ks[15], (CMP_HIDDEN, NSA_HEAD_DIM), CMP_HIDDEN),
        'nsa_w_in': nrm(ks[16], (N_B_LAYERS, D_MODEL, NSA_IN), D_MODEL),
        'nsa_w_o': nrm(ks[17], (N_B_LAYERS, NSA_HEADS * NSA_HEAD_DIM, D_MODEL), NSA_HEADS * NSA_HEAD_DIM),
        'ffn_w_up': nrm(ks[18], (DEPTH, D_MODEL, two_f), D_MODEL),
        'ffn_conv_w': nrm(ks[19], (DEPTH, CONV_WIDTH, two_f), CONV_WIDTH),
        'ffn_conv_b': 0.02 * jax.random.normal(ks[20], (DEPTH, two_f), f32),
        'ffn_w_down': nrm(ks[21], (DEPTH, FFN_DIM, D_MODEL), FFN_DIM),
        'norm_final': gain(ks[22], (D_MODEL,)),
    }

def first_block(x, norm_mix, norm_ffn, gla_w_in, gla_w_alpha_up, gla_b_alpha, gla_norm, gla_w_o,
              kv_norm, nsa_w_kv, cmp_pe_k, cmp_pe_v, cmp_k_w1, cmp_k_w2, cmp_v_w1, cmp_v_w2,
              nsa_w_in, nsa_w_o, ffn_w_up, ffn_conv_w, ffn_conv_b, ffn_w_down, norm_final):
    shared = None
    for layer in range(DEPTH):
        if layer < N_A_LAYERS:
            hn = rmsnorm(x, norm_mix[layer])
            x = x + gla_mixer(hn, gla_w_in[layer], gla_w_alpha_up[layer], gla_b_alpha[layer],
                              gla_norm[layer], gla_w_o[layer])
        else:
            if layer == N_A_LAYERS:
                shared = nsa_shared_kv(x, kv_norm, nsa_w_kv, cmp_pe_k, cmp_pe_v,
                                       cmp_k_w1, cmp_k_w2, cmp_v_w1, cmp_v_w2)
            b = layer - N_A_LAYERS
            hn = rmsnorm(x, norm_mix[layer])
            x = x + nsa_mixer(hn, nsa_w_in[b], nsa_w_o[b], *shared)
        hn = rmsnorm(x, norm_ffn[layer])
        x = x + conv_ffn(hn, ffn_w_up[layer], ffn_conv_w[layer], ffn_conv_b[layer], ffn_w_down[layer])
    return rmsnorm(x, norm_final)


DEPTH_2 = 1

CHUNK = 64
N_META = 16

D_MIX = D_MODEL
M_HEADS = 4
M_HEAD_DIM = (D_MIX // 2) // M_HEADS
M_WIDTH = M_HEADS * M_HEAD_DIM
CONV_W = 4
F_HEADS = 8
F_HEAD_DIM = (D_MIX - M_WIDTH) // F_HEADS
F_WIDTH = F_HEADS * F_HEAD_DIM
Q_BLOCK = 128

PROJ_SIZES = (M_WIDTH, M_WIDTH, M_WIDTH, M_WIDTH, M_HEADS, M_HEADS, F_WIDTH, F_WIDTH, F_WIDTH, F_HEADS)
PROJ_DIM = 4 * M_WIDTH + 2 * M_HEADS + 3 * F_WIDTH + F_HEADS

PEER_HEADS = 8
N_KEYS = 128
N_EXPERTS = N_KEYS * N_KEYS
PEER_TOPK = 16
PEER_QDIM = 256
PEER_HALF = PEER_QDIM // 2
PEER_TOKEN_BLOCK = 128


def _rmsnorm(x, g):
    xf = x.astype(jnp.float32)
    y = xf * lax.rsqrt(jnp.mean(xf * xf, axis=-1, keepdims=True) + EPS)
    return (y * g.astype(jnp.float32)).astype(x.dtype)

def _proj_splits():
    out, acc = [], 0
    for s in PROJ_SIZES[:-1]:
        acc += s
        out.append(acc)
    return out

def _causal_dwconv(x, w):
    c = x.shape[-1]
    return lax.conv_general_dilated(
        x, w.astype(x.dtype)[:, None, :], window_strides=(1,),
        padding=[(CONV_W - 1, 0)], dimension_numbers=("NWC", "WIO", "NWC"),
        feature_group_count=c)

def _mlstm(q, k, v, o_pre, i_pre, f_pre, out_gain):
    f32 = jnp.float32
    B, L, _ = q.shape
    n_chunks = -(-L // CHUNK)
    pad = n_chunks * CHUNK - L

    def heads(t):
        t = jnp.pad(t.astype(f32), ((0, 0), (0, pad), (0, 0)))
        return t.reshape(B, n_chunks, CHUNK, M_HEADS, M_HEAD_DIM).transpose(1, 0, 3, 2, 4)

    def gates(t):
        t = jnp.pad(t.astype(f32), ((0, 0), (0, pad), (0, 0)))
        return t.reshape(B, n_chunks, CHUNK, M_HEADS).transpose(1, 0, 3, 2)

    qc = heads(q)
    kc = heads(k) * (M_HEAD_DIM ** -0.5)
    vc = heads(v)
    logi = gates(i_pre)
    logf = jax.nn.log_sigmoid(gates(f_pre))
    causal = jnp.asarray(np.tril(np.ones((CHUNK, CHUNK), dtype=bool)))

    def step(carry, inp):
        C, n, m = carry
        qb, kb, vb, li, lf = inp
        b = jnp.cumsum(lf, axis=-1)
        Dm = jnp.where(causal, b[..., :, None] - b[..., None, :] + li[..., None, :], -jnp.inf)
        m_inter = b + m[..., None]
        m_t = jnp.maximum(m_inter, jnp.max(Dm, axis=-1))
        S = jnp.einsum('bhtd,bhsd->bhts', qb, kb) * jnp.exp(Dm - m_t[..., None])
        w_inter = jnp.exp(m_inter - m_t)
        num = jnp.einsum('bhts,bhsd->bhtd', S, vb) + w_inter[..., None] * jnp.einsum('bhvk,bhtk->bhtv', C, qb)
        den = jnp.sum(S, axis=-1) + w_inter * jnp.einsum('bhk,bhtk->bht', n, qb)
        h = num / jnp.maximum(jnp.abs(den), jnp.exp(-m_t))[..., None]
        b_end = b[..., -1]
        g = b_end[..., None] - b + li
        m_new = jnp.maximum(b_end + m, jnp.max(g, axis=-1))
        decay = jnp.exp(b_end + m - m_new)
        wg = jnp.exp(g - m_new[..., None])
        C = decay[..., None, None] * C + jnp.einsum('bhs,bhsv,bhsk->bhvk', wg, vb, kb)
        n = decay[..., None] * n + jnp.einsum('bhs,bhsk->bhk', wg, kb)
        return (C, n, m_new), h

    init = (jnp.zeros((B, M_HEADS, M_HEAD_DIM, M_HEAD_DIM), f32),
            jnp.zeros((B, M_HEADS, M_HEAD_DIM), f32),
            jnp.zeros((B, M_HEADS), f32))
    _, h = lax.scan(step, init, (qc, kc, vc, logi, logf))
    h = h.transpose(1, 0, 3, 2, 4).reshape(B, n_chunks * CHUNK, M_HEADS, M_HEAD_DIM)[:, :L]
    h = _rmsnorm(h, out_gain.reshape(M_HEADS, M_HEAD_DIM)).reshape(B, L, M_WIDTH)
    h = h * jax.nn.sigmoid(o_pre.astype(f32))
    return h.astype(q.dtype)

def _forgetting_attention(q, k, v, f_pre, g_q, g_k):
    B, L, _ = q.shape

    def heads(t):
        return t.reshape(B, L, F_HEADS, F_HEAD_DIM).transpose(0, 2, 1, 3)

    qh = _rmsnorm(heads(q), g_q)
    kh = _rmsnorm(heads(k), g_k)
    vh = heads(v)
    c = jnp.cumsum(jax.nn.log_sigmoid(f_pre.astype(jnp.float32)), axis=1).transpose(0, 2, 1)
    scale = F_HEAD_DIM ** -0.5
    outs = []
    for start in range(0, L, Q_BLOCK):
        end = min(start + Q_BLOCK, L)
        logits = jnp.einsum('bhtd,bhsd->bhts', qh[:, :, start:end], kh[:, :, :end]).astype(jnp.float32) * scale
        logits = logits + c[:, :, start:end, None] - c[:, :, None, :end]
        mask = np.arange(start, end)[:, None] >= np.arange(end)[None, :]
        logits = jnp.where(mask, logits, -jnp.inf)
        p = jax.nn.softmax(logits, axis=-1).astype(vh.dtype)
        outs.append(jnp.einsum('bhts,bhsd->bhtd', p, vh[:, :, :end]))
    out = jnp.concatenate(outs, axis=2)
    return out.transpose(0, 2, 1, 3).reshape(B, L, F_WIDTH)

def _peer(x, w_query, sub_keys, u_emb, v_emb):
    B, L, D = x.shape
    T = B * L
    Tp = -(-T // PEER_TOKEN_BLOCK) * PEER_TOKEN_BLOCK
    xt = jnp.pad(x.reshape(T, D), ((0, Tp - T), (0, 0))).reshape(-1, PEER_TOKEN_BLOCK, D)
    keys32 = sub_keys.astype(jnp.float32)

    def block(xb):
        tb = xb.shape[0]
        qh = (xb @ w_query).astype(jnp.float32).reshape(tb, PEER_HEADS, 2, PEER_HALF)
        scores = jnp.einsum('thpc,hpnc->thpn', qh, keys32)
        val, idx = lax.top_k(scores, PEER_TOPK)
        cand = (val[:, :, 0, :, None] + val[:, :, 1, None, :]).reshape(tb, PEER_HEADS, PEER_TOPK * PEER_TOPK)
        cand_id = (idx[:, :, 0, :, None] * N_KEYS + idx[:, :, 1, None, :]).reshape(tb, PEER_HEADS, PEER_TOPK * PEER_TOPK)
        top_s, pos = lax.top_k(cand, PEER_TOPK)
        ids = jnp.take_along_axis(cand_id, pos, axis=-1).reshape(tb, PEER_HEADS * PEER_TOPK)
        gate = jax.nn.softmax(top_s, axis=-1).reshape(tb, PEER_HEADS * PEER_TOPK)
        u = u_emb[ids]
        act = jax.nn.gelu(jnp.einsum('ted,td->te', u, xb).astype(jnp.float32), approximate=False)
        w = (gate * act).astype(xb.dtype)
        return jnp.einsum('te,ted->td', w, v_emb[ids])

    out = lax.map(block, xt)
    return out.reshape(Tp, D)[:T].reshape(B, L, D)

def second_inputs(seed: int = 0) -> dict:
    key = jax.random.key(seed)
    ks = jax.random.split(key, 20)
    f32 = jnp.float32
    nrm = lambda k, shape, s: jax.random.normal(k, shape, f32) * s
    fbias_m = jnp.broadcast_to(jnp.linspace(3.0, 6.0, M_HEADS, dtype=f32), (DEPTH_2, M_HEADS))
    fbias_f = jnp.broadcast_to(jnp.linspace(2.0, 6.0, F_HEADS, dtype=f32), (DEPTH_2, F_HEADS))
    return {
        "x": nrm(ks[0], (BATCH, SEQ, D_MODEL), 1.0),
        "meta_tokens": nrm(ks[1], (N_META, D_MODEL), 1.0),
        "norm_mix": 1.0 + nrm(ks[2], (DEPTH_2, D_MODEL), 0.02),
        "w_in": nrm(ks[3], (DEPTH_2, D_MODEL, PROJ_DIM), D_MODEL ** -0.5),
        "conv_qk": nrm(ks[4], (DEPTH_2, CONV_W, 2 * M_WIDTH), CONV_W ** -0.5),
        "b_igate": nrm(ks[5], (DEPTH_2, M_HEADS), 0.1),
        "b_fgate_m": fbias_m + nrm(ks[6], (DEPTH_2, M_HEADS), 0.1),
        "m_out_norm": 1.0 + nrm(ks[7], (DEPTH_2, M_WIDTH), 0.02),
        "b_fgate_f": fbias_f + nrm(ks[8], (DEPTH_2, F_HEADS), 0.1),
        "f_q_norm": 1.0 + nrm(ks[9], (DEPTH_2, F_HEAD_DIM), 0.02),
        "f_k_norm": 1.0 + nrm(ks[10], (DEPTH_2, F_HEAD_DIM), 0.02),
        "w_out": nrm(ks[11], (DEPTH_2, D_MIX, D_MODEL), D_MIX ** -0.5),
        "norm_ffn": 1.0 + nrm(ks[12], (DEPTH_2, D_MODEL), 0.02),
        "peer_query": nrm(ks[13], (DEPTH_2, D_MODEL, PEER_HEADS * PEER_QDIM), D_MODEL ** -0.5),
        "peer_sub_keys": nrm(ks[14], (DEPTH_2, PEER_HEADS, 2, N_KEYS, PEER_HALF), PEER_HALF ** -0.5),
        "peer_u": nrm(ks[15], (DEPTH_2, N_EXPERTS, D_MODEL), D_MODEL ** -0.5),
        "peer_v": nrm(ks[16], (DEPTH_2, N_EXPERTS, D_MODEL), 0.1),
    }

def second_block(x, meta_tokens, norm_mix, w_in, conv_qk, b_igate, b_fgate_m, m_out_norm,
              b_fgate_f, f_q_norm, f_k_norm, w_out, norm_ffn, peer_query, peer_sub_keys,
              peer_u, peer_v):
    B = x.shape[0]
    meta = jnp.broadcast_to(meta_tokens.astype(x.dtype)[None], (B, N_META, D_MODEL))
    h_res = jnp.concatenate([meta, x], axis=1)
    splits = _proj_splits()
    for layer in range(DEPTH_2):
        hn = _rmsnorm(h_res, norm_mix[layer])
        z = hn @ w_in[layer]
        mq, mk, mv, mo, mi, mf, fq, fk, fv, ff = jnp.split(z, splits, axis=-1)
        qk = jax.nn.silu(_causal_dwconv(jnp.concatenate([mq, mk], axis=-1), conv_qk[layer]))
        mq, mk = jnp.split(qk, 2, axis=-1)
        y_m = _mlstm(mq, mk, mv, mo, mi + b_igate[layer], mf + b_fgate_m[layer], m_out_norm[layer])
        y_f = _forgetting_attention(fq, fk, fv, ff + b_fgate_f[layer], f_q_norm[layer], f_k_norm[layer])
        h_res = h_res + jnp.concatenate([y_m, y_f], axis=-1) @ w_out[layer]
        if layer == DEPTH_2 - 1:
            h_res = h_res[:, N_META:]
        h_res = h_res + _peer(_rmsnorm(h_res, norm_ffn[layer]), peer_query[layer],
                              peer_sub_keys[layer], peer_u[layer], peer_v[layer])
    return h_res


def setup_inputs(seed=0):
    out = dict(first_inputs(seed))
    for name, value in second_inputs(seed + 1).items():
        if name != "x":
            out[name + "_2"] = value
    return out


def reference(
    x, norm_mix, norm_ffn, gla_w_in, gla_w_alpha_up, gla_b_alpha, gla_norm, gla_w_o, kv_norm,
    nsa_w_kv, cmp_pe_k, cmp_pe_v, cmp_k_w1, cmp_k_w2, cmp_v_w1, cmp_v_w2, nsa_w_in, nsa_w_o,
    ffn_w_up, ffn_conv_w, ffn_conv_b, ffn_w_down, norm_final, meta_tokens_2, norm_mix_2, w_in_2,
    conv_qk_2, b_igate_2, b_fgate_m_2, m_out_norm_2, b_fgate_f_2, f_q_norm_2, f_k_norm_2,
    w_out_2, norm_ffn_2, peer_query_2, peer_sub_keys_2, peer_u_2, peer_v_2,
):
    x = first_block(
        x, norm_mix, norm_ffn, gla_w_in, gla_w_alpha_up, gla_b_alpha, gla_norm, gla_w_o,
        kv_norm, nsa_w_kv, cmp_pe_k, cmp_pe_v, cmp_k_w1, cmp_k_w2, cmp_v_w1, cmp_v_w2, nsa_w_in,
        nsa_w_o, ffn_w_up, ffn_conv_w, ffn_conv_b, ffn_w_down, norm_final,
    )
    return second_block(
        x, meta_tokens_2, norm_mix_2, w_in_2, conv_qk_2, b_igate_2, b_fgate_m_2, m_out_norm_2,
        b_fgate_f_2, f_q_norm_2, f_k_norm_2, w_out_2, norm_ffn_2, peer_query_2, peer_sub_keys_2,
        peer_u_2, peer_v_2,
    )


_drawn_inputs = setup_inputs


def setup_inputs(seed=0):
    import zlib

    import numpy as np

    out = dict(_drawn_inputs(seed))
    spreads = {}
    factors = {'gla_norm': 3.693,
     'kv_norm': 8.0,
     'cmp_pe_k': 8.0,
     'cmp_pe_v': 6.925,
     'norm_mix_2': 4.118,
     'b_igate_2': 64.0,
     'm_out_norm_2': 21.805,
     'f_q_norm_2': 8.0,
     'f_k_norm_2': 8.0,
     'norm_ffn_2': 22.996}
    for name, (base, spread) in spreads.items():
        noise = np.random.default_rng([zlib.crc32(name.encode()), seed]).standard_normal(out[name].shape)
        drawn = base * np.exp(spread * noise) if base else spread * noise
        out[name] = __import__('jax').numpy.asarray(drawn.astype(out[name].dtype))
    for name, factor in factors.items():
        out[name] = (out[name] * factor).astype(out[name].dtype)
    return out
```

```python
from contextlib import ExitStack

import numpy as np
import concourse.bass as bass
from concourse import mybir

F32 = mybir.dt.float32
F32R = mybir.dt.float32r
U32 = mybir.dt.uint32
ACT = mybir.ActivationFunctionType
ALU = mybir.AluOpType
AX = mybir.AxisListType

P = 128
D = 1024
KC = D // P
SEQ = 256
TT = SEQ // P
META = 16
L2 = SEQ + META
EPS = 1e-6
NEG = -1e30

GH, GDK, GDV, GC, GSUB = 4, 128, 256, 64, 16
GTAU = 16.0
GRANK = 16
CLAMP = 60.0
NCH = SEQ // GC

NH, NKV, NG, ND = 16, 4, 4, 64
CB, CS = 32, 16
NCMP = (SEQ - CB) // CS + 1
CHID = 4 * ND

FF = 2816
FT = FF // P

MH, MD = 4, 128
FH, FD = 8, 64
MCONV = 4

PH, PK, PQ = 8, 16, 128
NKEY = 128

RING = 6
HI = 3


def stream_plan():
    plan, at = {}, 0
    def add(name, count):
        nonlocal at
        plan[name] = (at, count)
        at += count
    add("gla_q", 4), add("gla_k", 4), add("gla_v", 8), add("gla_r", 8), add("gla_o", 8)
    add("ffn0", 3 * FT)
    add("nsa_raw", 4), add("nsa_rot_k", 4), add("nsa_q", 8), add("nsa_v", 4), add("cmp_k", 4), add("cmp_v", 4)
    add("nsa_o", 8)
    add("ffn1", 3 * FT)
    add("mix_q", 4), add("mix_k", 4), add("mix_og", 4), add("mix_fq", 4), add("mix_fk", 4), add("mix_v", 8)
    add("mix_o", 8)
    add("peer_q", 2 * PH)
    add("peer", 2 * NKEY)
    return plan, at


def param_plan():
    plan, at = {}, 0
    for name, width in (
        ("g_mix0", KC), ("g_ffn0", KC), ("g_kv", KC), ("g_mix1", KC), ("g_ffn1", KC), ("g_mix2", KC), ("g_ffn2", KC),
        ("g_gla", KC), ("b_alpha", GH), ("conv0", 2 * FT * 4), ("conv1", 2 * FT * 4), ("conv_m", 2 * MH * MCONV),
        ("g_m", MH), ("g_fq", 1), ("g_fk", 1), ("b_forget", 1), ("b_input", 1), ("pe_k", CB // 2), ("pe_v", CB // 2),
        ("w2_k", 2 * P), ("w2_v", 2 * ND), ("w_alow", KC * GRANK), ("w_aup", GH * GDK), ("w_gates", KC * 3 * NH),
        ("w_gates2", KC * 36),
    ):
        plan[name] = (at, width)
        at += width
    return plan, at


def const_plan():
    plan, at = {}, 0
    for name, width in (
        ("ident", P), ("ones", P), ("ones64", P), ("turn", P), ("cos", SEQ), ("sin", SEQ), ("tril", GC),
        ("reset", SEQ), ("mask1", SEQ), ("mask0", P), ("cmask", TT * NCMP), ("cvalid", TT), ("mask2", TT * L2),
        ("maskT", SEQ), ("iota", P),
    ):
        plan[name] = (at, width)
        at += width
    return plan, at


def constants():
    plan, width = const_plan()
    c = np.zeros((P, width), np.float32)
    def put(name, a):
        at, w = plan[name]
        c[: a.shape[0], at:at + w] = a.reshape(a.shape[0], -1)
    i = np.arange(P)
    put("ident", np.eye(P))
    put("ones", np.ones((P, P)))
    put("ones64", (i[:, None] // 64 == i[None, :] // 64).astype(np.float32))
    turn = np.zeros((P, P))
    for b in (0, 64):
        for d in range(32):
            turn[b + 32 + d, b + d] = -1.0
            turn[b + d, b + 32 + d] = 1.0
    put("turn", turn)
    half = ND // 2
    inv = np.float32(10000.0) ** (-np.arange(half, dtype=np.float32) / np.float32(half))
    ang = np.arange(SEQ, dtype=np.float32)[None, :] * inv[:, None]
    put("cos", np.tile(np.cos(ang), (4, 1)))
    put("sin", np.tile(np.sin(ang), (4, 1)))
    put("tril", (i[:, None] % GC <= np.arange(GC)[None, :]).astype(np.float32))
    put("reset", np.tile((np.arange(SEQ) % GC != 0).astype(np.float32), (P, 1)))
    put("mask1", np.where(np.arange(SEQ)[None, :] <= i[:, None] + P, 0.0, NEG))
    put("mask0", np.where(i[None, :] <= i[:, None], 0.0, NEG))
    pos = i[:, None] + P * np.arange(TT)[None, :]
    end = np.arange(NCMP) * CS + CB - 1
    put("cmask", np.where(end[None, None, :] <= pos[:, :, None], 0.0, NEG))
    put("cvalid", (pos >= CB - 1).astype(np.float32))
    put("mask2", np.where(np.arange(L2)[None, None, :] <= META + pos[:, :, None], 0.0, NEG))
    put("maskT", np.where(i[:, None] <= np.arange(SEQ)[None, :], 0.0, NEG))
    put("iota", np.tile(np.arange(P, dtype=np.float32), (P, 1)))
    return c


def build(nc, stream, params, consts, keys, g_final, x_in, meta_in, out):
    plan, n_tiles = stream_plan()
    pplan, pwidth = param_plan()
    cplan, cwidth = const_plan()
    ctx = ExitStack()
    with ctx:
        slab_base = nc.sbuf_base
        slab_bytes = nc.sbuf_bytes_remaining // 32 * 32 - 32
        ctx.enter_context(nc.sbuf_tensor("slab", [P, slab_bytes // 4], F32))
        place = {"end": -(-slab_base // 32) * 32}

        def sb(name, shape, dt=F32):
            place[name] = place["end"]
            place["end"] += -(-4 * int(np.prod(shape[1:])) // 32) * 32
            assert place["end"] <= slab_base + slab_bytes, name
            return nc.alloc_sbuf_tensor_at(name, shape, dt, offset=place[name])

        def over(name, shape, host, at, dt=F32R):
            return nc.alloc_sbuf_tensor_at(name, shape, dt, offset=place[host] + 4 * at)

        def sem(name):
            return ctx.enter_context(nc.semaphore(name))

        ring = sb("ring", [P, RING, D])
        prm = sb("prm", [P, pwidth])
        cst = sb("cst", [P, cwidth])
        x = sb("x", [P, TT, D])
        xn = sb("xn", [P, KC, L2])
        hT_hi, hT_lo = sb("hT_hi", [P, 2, SEQ], F32R), sb("hT_lo", [P, 2, SEQ], F32R)
        stat = sb("stat", [P, 64])
        arena = sb("arena", [P, NKEY * SEQ])
        ps = ctx.enter_context(nc.psum_tensor("ps", [P, 8, 512], F32))

        def par(name):
            at, w = pplan[name]
            return prm[:, at:at + w]

        def con(name):
            at, w = cplan[name]
            return cst[:, at:at + w]

        def carve(start, *sizes):
            views = []
            for n in sizes:
                views.append(arena[:, start:start + n])
                start += n
            assert start <= NKEY * SEQ, start
            return views, start

        ident, iota = con("ident"), con("iota")

        (qT, kT, z, dec, bcum, qx, qb, ka, kd, kdT, vtok, rtok, att, state, ytok, yT), _ = carve(
            0, 1024, 1024, 1024, 1024, 1024, 1024, 1024, 4096, 1024, 1024, 2048, 2048, 512, 2048, 2048, 2048)
        (xs,), _ = carve(NKEY * SEQ - 3 * D, 3 * D)
        xs = xs.rearrange("p (t n) -> p t n", n=D)
        (cgate, cval, sgate, hfull), _ = carve(0, SEQ, SEQ, SEQ, SEQ)
        ring_lo = over("ring_lo", [P, RING, D], "ring", 0)
        ffn_hi = over("ffn_hi", [P, HI, D], "arena", 6144)
        ffn_w_hi = [ffn_hi[:, s, :] for s in range(HI)]
        ffn_x_hi = over("ffn_x_hi", [P, KC, SEQ], "arena", 9216)
        ffn_x_lo = over("ffn_x_lo", [P, KC, SEQ], "arena", 11264)
        (xkv, cmpraw, raw, rot, shifted, blk, hid, hidT, hvr, kcT, vcr, pc, pcT, vsw, gs, sc_a, sc_b, pt, csc), _ = carve(
            0, 2048, 1024, 3072, 3072, 2048, 1920, 512, 240, 1024, 64, 256, 1024, 1024, 1024, 96, 1024, 512, 1536, 512)
        oT = xkv
        (mqk, mo, fqk, fsq, v2, lin, wts, stm, sfx, bfx, ptf, y2T), _ = carve(
            0, 2176, 1088, 2176, 2176, 3072, 9 * L2, 2560, 2560, 1024, 448, 1280, 2048)
        (em, dn, hn), _ = carve(4 * 2176 - 1088 + 3072 + 9 * L2, 1024, 1024, 1024)
        (gfin, xm), _ = carve(NKEY * SEQ - 5 * D, D, D)
        xm = xm[0:META, :]
        gates_j = arena[:, :].rearrange("p (j t) -> p j t", t=SEQ)
        route = sb("route", [P, 3, SEQ])
        onehot = sb("onehot", [P, 2, 2, 4, P])
        (qhT, scs, tv, ti, cand, tops, topi, pa, pb, ix, eq, tmp2, keysT), _ = carve(
            0, 4096, 4096, 512, 512, 512, 256, 256, 256, 256, 1024, 4096, 512, 2048)
        keysT = keysT.rearrange("p (i n) -> p i n", n=NKEY)
        gbuf = sb("gbuf", [P, 2, SEQ])
        tmp = sb("tmp", [P, SEQ])
        colb = sb("colb", [P, 48])
        xpT = xn
        peer_x_hi = over("peer_x_hi", [P, KC, SEQ], "prm", 0)
        peer_x_lo = over("peer_x_lo", [P, KC, SEQ], "cst", P)
        assert pwidth >= KC * SEQ and P + KC * SEQ <= cplan["iota"][0]
        peer_hi_a, peer_hi_b = over("peer_hi_a", [P, 2, D], "xn", 0), over("peer_hi_b", [P, D], "onehot", 0)
        peer_w_hi = [peer_hi_a[:, 0, :], peer_hi_a[:, 1, :], peer_hi_b[:, :]]

        w_loaded = [sem(f"w_loaded{s}") for s in range(RING)]
        tile_done = sem("tile_done")
        prm_in, x_in_sem, meta_sem, fin_sem, keys_in = (sem(n) for n in ("prm_in", "x_in", "meta_in", "gfin_in", "keys_in"))
        x_ready = sem("x_ready")
        sq_done, var_done, sd_done = sem("sq_done"), sem("var_done"), sem("sd_done")
        tok_ready = sem("tok_ready")
        t_done = sem("t_done")
        t_copied = sem("t_copied")
        small_done, fm_free = sem("small_done"), sem("fm_free")
        dve_step, act_step = sem("dve_step"), sem("act_step")
        act_rows = sem("act_rows")
        rot_done, rot_free = sem("rot_done"), sem("rot_free")
        hi_ok, lo_ok = sem("hi_ok"), sem("lo_ok")
        xhi_ok, xlo_ok = sem("xhi_ok"), sem("xlo_ok")

        cnt = {"dve": 0, "act": 0}

        def dlink(dve, ins):
            cnt["dve"] += 1
            ins.then_inc(dve_step, 1)
            dve.wait_ge(dve_step, cnt["dve"])

        def alink(act, ins):
            cnt["act"] += 1
            ins.then_inc(act_step, 1)
            act.wait_ge(act_step, cnt["act"])

        def v3(ap, n):
            return ap.rearrange("p (a n) -> p a n", n=n)

        def bcast(ap, *shape):
            return ap.broadcast_to([ap.shape[0], *shape])

        TILES = {"mix0": 2, "ffn0": 2, "mix1": 2, "ffn1": 2, "final": 2, "mix2": 3, "ffn2": 2}
        NBASE, XNEED, base, xr = {}, {}, 0, 0
        for name, n in TILES.items():
            NBASE[name] = base
            base += n
        XNEED = {"mix0": 0, "ffn0": 2, "mix1": 4, "ffn1": 6, "final": 8, "mix2": 10, "ffn2": 12}
        NIDX = {name: i for i, name in enumerate(TILES)}
        TST, base = {}, 0
        for name, n in (("mix0", 2), ("gla", 2), ("ffn0", 2), ("mix1", 2), ("ffn1", 2), ("mix2", 3), ("ffn2", 2)):
            TST[name] = (base, n)
            base += n

        def norm_tiles(name):
            own = [(x[:, t, :], P) for t in range(TT)]
            return [(xm, META)] + own if name == "mix2" else own

        def act_norm(act, name):
            if XNEED[name]:
                act.wait_ge(x_ready, XNEED[name])
            else:
                act.wait_ge(x_in_sem, 16)
            if name == "mix2":
                act.wait_ge(meta_sem, 16)
            for i, (src, rows) in enumerate(norm_tiles(name)):
                nc.scalar.activation(xs[0:rows, i, :], src, ACT.Square,
                                     accum_out=stat[0:rows, i:i + 1]).then_inc(sq_done, 1)
            act.wait_ge(var_done, NIDX[name] + 1)
            n = TILES[name]
            nc.scalar.activation(stat[:, 16:16 + n], stat[:, 8:8 + n], ACT.Sqrt).then_inc(sd_done, 1)

        def dve_norm(dve, name, gain=None):
            n = TILES[name]
            dve.wait_ge(sq_done, NBASE[name] + n)
            nc.vector.tensor_scalar(stat[:, 8:8 + n], stat[:, 0:n], 1.0 / D, EPS, ALU.mult, ALU.add).then_inc(var_done, 1)
            dve.wait_ge(sd_done, NIDX[name] + 1)
            dlink(dve, nc.vector.reciprocal(stat[:, 24:24 + n], stat[:, 16:16 + n]))
            for i, (src, rows) in enumerate(norm_tiles(name)):
                if gain is None:
                    nc.vector.tensor_scalar(xs[0:rows, i, :], src, stat[0:rows, 24 + i:25 + i], None,
                                            ALU.mult).then_inc(tok_ready, 1)
                else:
                    nc.vector.scalar_tensor_tensor(src, src, stat[0:rows, 24 + i:25 + i], gain, ALU.mult,
                                                   ALU.mult).then_inc(x_ready, 1)

        def pe_transpose(pe, name, src, rows_of):
            first, n = TST[name]
            for i in range(n):
                pe.wait_ge(tok_ready, first + i + 1)
                rows = rows_of(i)
                for half in range(2):
                    k = 2 * (first + i) + half
                    if k >= 2:
                        pe.wait_ge(t_copied, k - 1)
                    for c in range(4):
                        last = nc.tensor.transpose(ps[:, 6 + k % 2, c * rows:(c + 1) * rows],
                                                   src[0:rows, i, (4 * half + c) * P:(4 * half + c + 1) * P],
                                                   ident[0:rows, 0:rows])
                    last.then_inc(t_done, 1)

        def dve_transpose(dve, name, cols_of, outs):
            first, n = TST[name]
            for i in range(n):
                c0, rows = cols_of(i)
                for half in range(2):
                    k = 2 * (first + i) + half
                    dve.wait_ge(t_done, k + 1)
                    got = ps[:, 6 + k % 2, 0:4 * rows].rearrange("p (c t) -> p c t", c=4)
                    for o, (dst, gain) in enumerate(outs):
                        last = nc.vector.tensor_tensor(
                            dst[:, 4 * half:4 * half + 4, c0:c0 + rows], got,
                            bcast(par(gain)[:, 4 * half:4 * half + 4].unsqueeze(2), 4, rows), ALU.mult)
                    last.then_inc(t_copied, 1)

        def t_all(name):
            first, n = TST[name]
            return 2 * (first + n)

        own_cols = lambda i: (i * P, P)
        CSB = (0, 1, 4, 5)
        meta_cols = lambda i: (0, META) if i == 0 else (META + (i - 1) * P, P)

        fmc = {"pe": 0, "dve": 0}

        def w_wait(pe, n):
            pe.wait_ge(w_loaded[n % RING], 16 * (n // RING + 1))

        def fm_begin(pe):
            k = fmc["pe"]
            fmc["pe"] += 1
            if k >= 2:
                pe.wait_ge(fm_free, k - 1)
            return k % 2

        def pe_column(pe, n, rhs, width):
            bank = fm_begin(pe)
            w_wait(pe, n)
            w = v3(ring[:, n % RING, :], P)
            for c in range(KC):
                last = nc.tensor.matmul(ps[:, bank, 0:width], w[:, c, :], rhs[:, c, 0:width],
                                        start=(c == 0), stop=(c == KC - 1))
            last.then_inc(tile_done, 1)

        FM = [("tile", plan["gla_q"][0] + j) for j in range(2 * GH)] + [("small", j) for j in range(1 + GH)]
        FM += [("tile", plan["nsa_raw"][0] + j) for j in range(16)] + [("small", 1 + GH)]
        FM += [("tile", plan["mix_q"][0] + j) for j in range(20)]
        FM += [("tile", plan["peer_q"][0] + j) for j in range(2 * PH)]

        def fm_wait(eng, k):
            kind, n = FM[k]
            eng.wait_ge(tile_done if kind == "tile" else small_done, n + 1)

        def fm_take(dve):
            k = fmc["dve"]
            fmc["dve"] += 1
            fm_wait(dve, k)
            return k % 2

        def rows_wait(eng, name):
            first, n = plan[name]
            eng.wait_ge(tile_done, first + n)

        def pe_rows(pe, first, lhs, banks, n=KC):
            for k in range(n):
                w_wait(pe, first + k)
                for t, pair in enumerate(banks):
                    for half in range(2):
                        a = lhs(k, t)
                        last = nc.tensor.matmul(ps[0:a.shape[1], pair[half], :], a,
                                                ring[:, (first + k) % RING, half * 512:(half + 1) * 512],
                                                start=(k == 0), stop=(k == n - 1))
                last.then_inc(tile_done, 1)
            return last

        ROWB = [(2, 3), (4, 5)]

        def dve_residual(dve, name):
            rows_wait(dve, name)
            for t in range(TT):
                for half in range(2):
                    part = x[:, t, half * 512:(half + 1) * 512]
                    last = nc.vector.tensor_tensor(part, ps[:, ROWB[t][half], :], part, ALU.add)
                last.then_inc(x_ready, 1)

        SPLIT0 = {"ffn0": 0, "ffn1": 3 * FT, "peer": 6 * FT}
        W_HI = {"ffn0": ffn_w_hi, "ffn1": ffn_w_hi, "peer": peer_w_hi}

        def split_hi(act, name, tile, it=None, turns=1):
            n = plan[name][0] + tile
            turn = 16 * (n // RING + 1)
            act.wait_ge(w_loaded[n % RING], turn if it is None else it * (16 * turns) + turn)
            nc.scalar.activation(W_HI[name][tile % HI], ring[:, n % RING, :], ACT.Copy).then_inc(hi_ok, 1)

        def split_lo(dve, name, tile, it=None, turns=1):
            n = plan[name][0] + tile
            need = SPLIT0[name] + tile + 1
            dve.wait_ge(hi_ok, need if it is None else it * (RING * turns) + need)
            nc.vector.tensor_tensor(ring_lo[:, n % RING, :], ring[:, n % RING, :], W_HI[name][tile % HI].bitcast(F32),
                                    ALU.subtract).then_inc(lo_ok, 1)

        def split_wait(pe, name, tile, it=None, turns=1):
            need = SPLIT0[name] + tile + 1
            pe.wait_ge(lo_ok, need if it is None else it * (RING * turns) + need)

        def split_columns(name, tile, bank, x_hi, x_lo):
            n = plan[name][0] + tile
            w_hi, w_lo = v3(W_HI[name][tile % HI], P), v3(ring_lo[:, n % RING, :], P)
            for c in range(KC):
                nc.tensor.matmul(ps[:, bank, 0:SEQ], w_hi[:, c, :], x_hi[:, c, :], start=(c == 0), stop=False)
                nc.tensor.matmul(ps[:, bank, 0:SEQ], w_hi[:, c, :], x_lo[:, c, :], start=False, stop=False)
                last = nc.tensor.matmul(ps[:, bank, 0:SEQ], w_lo[:, c, :], x_hi[:, c, :], start=False, stop=(c == KC - 1))
            last.then_inc(tile_done, 1)

        def split_rows(name, tile, buf, first, final):
            n = plan[name][0] + tile
            w_hi, w_lo = W_HI[name][tile % HI], ring_lo[:, n % RING, :]
            for t in range(TT):
                h_hi, h_lo = hT_hi[:, buf, t * P:(t + 1) * P], hT_lo[:, buf, t * P:(t + 1) * P]
                for a, w, st, sp_ in ((h_hi, w_hi, first, False), (h_hi, w_lo, False, False), (h_lo, w_hi, False, final)):
                    for half in range(2):
                        last = nc.tensor.matmul(ps[:, ROWB[t][half], :], a, w[:, half * 512:(half + 1) * 512],
                                                start=st, stop=sp_)
            last.then_inc(tile_done, 1)

        def split_hidden(dve, full, buf, step, done):
            nc.vector.tensor_copy(hT_hi[:, buf, :], full).then_inc(dve_step, 1)
            dve.wait_ge(dve_step, step)
            nc.vector.tensor_tensor(hT_lo[:, buf, :], full, hT_hi[:, buf, :].bitcast(F32), ALU.subtract).then_inc(done, 1)

        XCNT = {"ffn0": 1, "ffn1": 2, "ffn2": 3}

        def act_input(act, name, x_hi):
            act.wait_ge(t_copied, t_all(name))
            nc.scalar.activation(x_hi[:, :, :], xn[:, :, 0:SEQ], ACT.Copy).then_inc(xhi_ok, 1)

        def dve_input(dve, name, x_hi, x_lo):
            dve.wait_ge(xhi_ok, XCNT[name])
            nc.vector.tensor_tensor(x_lo[:, :, :], xn[:, :, 0:SEQ], x_hi[:, :, :].bitcast(F32), ALU.subtract).then_inc(xlo_ok, 1)

        abs_ok, ln_ok, dsub_ok, dexp_ok, dmul_ok = (sem(n) for n in ("abs_ok", "ln_ok", "dsub_ok", "dexp_ok", "dmul_ok"))
        att_done, att_ok, kdt_done, kdt_ok = (sem(n) for n in ("att_done", "att_ok", "kdt_done", "kdt_ok"))
        kv_done, state_ok, go_done, osq_ok, ovar_ok, osd_ok = (sem(n) for n in ("kv_done", "state_ok", "go_done", "osq_ok", "ovar_ok", "osd_ok"))
        c0_done, cg_done, cv_done, silu_done, h_ready = (sem(n) for n in ("c0_done", "cg_done", "cv_done", "silu_done", "h_ready"))
        shift_in, blk_ok, hid_ok, ht_done, ht_ok, kc_done, kc_ok, gate_done, gate_ok = (sem(n) for n in (
            "shift_in", "blk_ok", "hid_ok", "ht_done", "ht_ok", "kc_done", "kc_ok", "gate_done", "gate_ok"))
        cs_done, cs_ok, ce_ok, pc_ok, pct_done, pct_ok = (sem(n) for n in ("cs_done", "cs_ok", "ce_ok", "pc_ok", "pct_done", "pct_ok"))
        s_done, max_ok, exp_ok, p_ok, pt_done, pt_ok, pv_done, o_ok = (sem(n) for n in (
            "s_done", "max_ok", "exp_ok", "p_ok", "pt_done", "pt_ok", "pv_done", "o_ok"))
        mc0, msilu_ok, gab_ok, gln_ok, row_ok, col_done, col_ok = (sem(n) for n in (
            "mc0", "msilu_ok", "gab_ok", "gln_ok", "row_ok", "col_done", "col_ok"))
        fsq_ok, fss_done, fvar_ok, fsd_ok, fn_ok = (sem(n) for n in ("fsq_ok", "fss_done", "fvar_ok", "fsd_ok", "fn_ok"))
        ms_done, mw_ok, mexp_ok, mst_ok, mnum_done, mb_done, em_ok, hn_ok, hsq_ok, hss_done, hvar_ok, hsd_ok, y2_ok = (sem(n) for n in (
            "ms_done", "mw_ok", "mexp_ok", "mst_ok", "mnum_done", "mb_done", "em_ok", "hn_ok", "hsq_ok", "hss_done", "hvar_ok", "hsd_ok", "y2_ok"))
        qh_ok, sc_done, sc_ok, gsub_ok, gexp_ok, rt_ok, rt_done, route_ok, oh_ok, oh_used, g_done, g_ok = (sem(n) for n in (
            "qh_ok", "sc_done", "sc_ok", "gsub_ok", "gexp_ok", "rt_ok", "rt_done", "route_ok", "oh_ok", "oh_used", "g_done", "g_ok"))
        gelu_ok, ph_ok, fin_ok, out_sem = (sem(n) for n in ("gelu_ok", "ph_ok", "fin_ok", "out_sem"))
        block = ctx.enter_context(nc.Block())

        FM2 = GH * 3 + 1 + 4 + 12

        @block.sync
        def _(sp):
            for s in range(RING):
                sp.dma_start(ring[:, s, :], stream[s]).then_inc(w_loaded[s], 16)
            rounds = n_tiles // RING
            with sp.Fori(1, rounds) as i:
                for s in range(RING):
                    sp.wait_ge(tile_done, i * RING + (s + 1 - RING))
                    sp.dma_start(ring[:, s, :], stream[i * RING + s]).then_inc(w_loaded[s], 16)
            for n in range(rounds * RING, n_tiles):
                sp.wait_ge(tile_done, n + 1 - RING)
                sp.dma_start(ring[:, n % RING, :], stream[n]).then_inc(w_loaded[n % RING], 16)
            for t in range(TT):
                sp.wait_ge(fin_ok, t + 1)
                sp.dma_start(out[t * P:(t + 1) * P, :], x[:, t, :]).then_inc(out_sem, 16)
            sp.wait_ge(out_sem, 16 * TT)

        @block.tensor
        def _(pe):
            def pe_ffn(layer):
                name, h0 = f"ffn{layer}", FT * layer

                def up(tile, bank, need, it=None):
                    split_wait(pe, name, tile, it)
                    if need is not None:
                        pe.wait_ge((cg_done, cv_done)[bank], need)
                    split_columns(name, tile, bank, ffn_x_hi, ffn_x_lo)

                def down(tile, f_par, first, last_f, need, it=None):
                    split_wait(pe, name, tile, it)
                    pe.wait_ge(h_ready, need)
                    split_rows(name, tile, f_par, first, last_f)

                def pair(tile, f, it=None):
                    for s in range(2):
                        need = None
                        if it is not None:
                            need = it * 2 + (h0 + f)
                        elif h0 + f:
                            need = h0 + f
                        up(tile + s, s, need, it)

                pe.wait_ge(xlo_ok, XCNT[name])
                pair(0, 0)
                pair(2, 1)
                down(4, 0, True, False, h0 + 1)
                pair(5, 2)
                down(7, 1, False, False, h0 + 2)
                with pe.Fori(0, (FT - 4) // 2) as i:
                    pair(8, 3, i)
                    down(10, 0, False, False, i * 2 + (h0 + 3), i)
                    pair(11, 4, i)
                    down(13, 1, False, False, i * 2 + (h0 + 4), i)
                pair(8 + 3 * (FT - 4), FT - 1)
                down(10 + 3 * (FT - 4), 0, False, False, h0 + FT - 1)
                down(11 + 3 * (FT - 4), 1, False, True, h0 + FT)

            pe.wait_ge(prm_in, 32)
            pe_transpose(pe, "mix0", xs, lambda i: P)
            pe.wait_ge(t_copied, t_all("mix0"))
            for h in range(2 * GH):
                pe_column(pe, plan["gla_q"][0] + h, xn, SEQ)
            bank = fm_begin(pe)
            wl = v3(par("w_alow"), GRANK)
            for c in range(KC):
                last = nc.tensor.matmul(ps[0:GRANK, bank, 0:SEQ], wl[:, c, :], xn[:, c, 0:SEQ],
                                        start=(c == 0), stop=(c == KC - 1))
            last.then_inc(small_done, 1)
            pe_rows(pe, plan["gla_v"][0], lambda k, t: xn[:, k, t * P:(t + 1) * P], ROWB)
            pe.wait_ge(fm_free, 2 * GH + 1)
            for h in range(GH):
                bank = fm_begin(pe)
                nc.tensor.matmul(ps[:, bank, 0:SEQ], par("w_aup")[0:GRANK, h * GDK:(h + 1) * GDK], dec[0:GRANK, 0:SEQ],
                                 start=True, stop=True).then_inc(small_done, 1)
            pe.wait_ge(fm_free, fmc["pe"])
            RB = [(6, 7), (0, 1)]
            pe_rows(pe, plan["gla_r"][0], lambda k, t: xn[:, k, t * P:(t + 1) * P], RB)

            pe.wait_ge(dmul_ok, 2)
            pe.wait_ge(act_rows, 1)
            kav = ka.rearrange("p (a h t) -> p a h t", a=GC // GSUB, h=GH)
            qxv, qbv, kdv = v3(qx, SEQ), v3(qb, SEQ), v3(kd, SEQ)
            for h in range(GH):
                for c in range(NCH):
                    rows, col = 64 * (c % 2), (h * TT + c // 2) * GC
                    for a in range(GC // GSUB):
                        t0 = c * GC + a * GSUB
                        last = nc.tensor.matmul(ps[rows:rows + GC, 2, col + a * GSUB:col + (a + 1) * GSUB],
                                                kav[:, a, h, c * GC:(c + 1) * GC], qxv[:, h, t0:t0 + GSUB],
                                                start=True, stop=True)
            last.then_inc(att_done, 1)
            pe.wait_ge(dmul_ok, 3)
            for h in range(GH):
                for t in range(TT):
                    u = h * TT + t
                    last = nc.tensor.transpose(ps[:, 3 + u // 4, (u % 4) * P:(u % 4 + 1) * P],
                                               kdv[:, h, t * P:(t + 1) * P], ident)
            last.then_inc(kdt_done, 1)
            attv, vv = v3(att, GC), v3(vtok, D)
            kdTv = kdT.rearrange("p (h t k) -> p h t k", h=GH, t=TT)
            stv = state.rearrange("p (b h v) -> p b h v", b=2, h=GH)
            pe.wait_ge(att_ok, 1)
            pe.wait_ge(kdt_ok, 1)
            pe.wait_ge(act_rows, 2)
            pe.wait_ge(dmul_ok, 4)
            OB = [6, 7, 0, 1]
            for c in range(NCH):
                t, rows = c // 2, 64 * (c % 2)
                if c:
                    pe.wait_ge(state_ok, c)
                if c < NCH - 1:
                    for h in range(GH):
                        last = nc.tensor.matmul(ps[:, (2, 5)[h // 2], (h % 2) * GDV:(h % 2 + 1) * GDV],
                                                kdTv[rows:rows + GC, h, t, :], vv[rows:rows + GC, t, h * GDV:(h + 1) * GDV],
                                                start=True, stop=True)
                    last.then_inc(kv_done, 1)
                for h in range(GH):
                    o = ps[rows:rows + GC, OB[2 * t + h // 2], (h % 2) * GDV:(h % 2 + 1) * GDV]
                    last = nc.tensor.matmul(o, attv[rows:rows + GC, h * TT + t, :],
                                            vv[rows:rows + GC, t, h * GDV:(h + 1) * GDV], start=True, stop=(c == 0))
                    if c:
                        last = nc.tensor.matmul(o, qbv[:, h, c * GC:(c + 1) * GC], stv[:, c % 2, h, :],
                                                start=False, stop=True)
                last.then_inc(go_done, 1)
            pe_transpose(pe, "gla", v3(ytok, D), lambda i: P)
            pe.wait_ge(t_copied, t_all("gla"))
            pe_rows(pe, plan["gla_o"][0], lambda k, t: v3(yT, SEQ)[:, k, t * P:(t + 1) * P], ROWB)

            pe_transpose(pe, "ffn0", xs, lambda i: P)
            pe.wait_ge(t_copied, t_all("ffn0"))
            pe_ffn(0)

            pe_transpose(pe, "mix1", xs, lambda i: P)
            pe.wait_ge(t_copied, t_all("mix1"))
            xkvv = v3(xkv, SEQ)
            for j in range(4):
                pe_column(pe, plan["nsa_raw"][0] + j, xkvv, SEQ)
            rawv, rotv = v3(raw, SEQ), v3(rot, SEQ)
            for j in range(13):
                if j < 12:
                    pe_column(pe, plan["nsa_rot_k"][0] + j, xkvv if j < 4 else xn, SEQ)
                if j:
                    pe.wait_ge(fm_free, fmc["pe"] - (1 if j < 12 else 0))
                    if j >= 3:
                        pe.wait_ge(rot_free, j - 2)
                    nc.tensor.matmul(ps[:, 6 + (j - 1) % 2, 0:SEQ], con("turn"), rawv[:, j - 1, :],
                                     start=True, stop=True).then_inc(rot_done, 1)
            n = plan["nsa_v"][0]
            for k in range(4):
                w_wait(pe, n + k)
                for c in range(2):
                    for t in range(TT):
                        last = nc.tensor.matmul(ps[:, 2 + t, :], xkvv[:, 2 * k + c, t * P:(t + 1) * P],
                                                ring[:, (n + k) % RING, c * 512:(c + 1) * 512],
                                                start=(k == 0 and c == 0), stop=(k == 3 and c == 1))
                last.then_inc(tile_done, 1)
            wg = v3(par("w_gates"), 3 * NH)
            for t in range(TT):
                for c in range(KC):
                    last = nc.tensor.matmul(ps[:, 4, t * 64:t * 64 + 3 * NH], xn[:, c, t * P:(t + 1) * P], wg[:, c, :],
                                            start=(c == 0), stop=(c == KC - 1))
            last.then_inc(gate_done, 1)
            blkv = blk.rearrange("p (b l n) -> p b l n", b=2, l=CB // 2)
            NB = NKV * NCMP
            for b in range(2):
                pe.wait_ge(blk_ok, b + 1)
                n = plan["cmp_k"][0] + 4 * b
                for k in range(4):
                    w_wait(pe, n + k)
                    for c in range(4):
                        last = nc.tensor.matmul(ps[0:NB, 5, b * CHID:(b + 1) * CHID], blkv[:, b, 4 * k + c, 0:NB],
                                                ring[:, (n + k) % RING, c * CHID:(c + 1) * CHID],
                                                start=(k == 0 and c == 0), stop=(k == 3 and c == 3))
                    last.then_inc(tile_done, 1)
            pe.wait_ge(hid_ok, 1)
            pe.wait_ge(rot_free, 12)
            for u in range(4):
                last = nc.tensor.transpose(ps[:, 6, u * 64:u * 64 + NB], hid[0:NB, u * P:(u + 1) * P], ident[0:NB, 0:NB])
            last.then_inc(ht_done, 1)
            pe.wait_ge(ht_ok, 1)
            w2k, w2v = v3(par("w2_k"), P), v3(par("w2_v"), ND)
            hidTv, hvrv = v3(hidT, 2 * NB)[:, 0, :].rearrange("p (c n) -> p c n", c=2), hvr.rearrange("p (c g m) -> p c g m", c=2, g=NKV)
            for c in range(2):
                nc.tensor.matmul(ps[:, 7, 0:NB], w2k[:, c, :], hidTv[:, c, :], start=(c == 0), stop=(c == 1))
            for g in range(NKV):
                for c in range(2):
                    last = nc.tensor.matmul(ps[:, 7, 64 + g * ND:64 + (g + 1) * ND], hvrv[:, c, g, :], w2v[:, c, :],
                                            start=(c == 0), stop=(c == 1))
            last.then_inc(kc_done, 1)
            pe.wait_ge(kc_ok, 1)
            for t in range(TT):
                for g in range(NKV):
                    rows = 64 * (g % 2)
                    for r in range(NG):
                        j = 4 + (g // 2) * NG + r
                        col = 16 * (j - 4)
                        last = nc.tensor.matmul(ps[:, CSB[2 * t + g % 2], col:col + NCMP], rawv[rows:rows + ND, j, t * P:(t + 1) * P],
                                                kcT[rows:rows + ND, g * NCMP:(g + 1) * NCMP], start=True, stop=True)
                last.then_inc(cs_done, 1)
            pcv = pc.rearrange("p (t g m) -> p t g m", t=TT, g=NKV)
            pcTv = pcT.rearrange("p (g t m) -> p g t m", g=NKV, t=TT)
            pe.wait_ge(pc_ok, 1)
            pe.wait_ge(act_rows, 3)
            for g in range(NKV):
                for t in range(TT):
                    u = g * TT + t
                    last = nc.tensor.transpose(ps[:, 2 + u // 4, (u % 4) * P:(u % 4 + 1) * P], pcv[:, t, 2 * (g % 2) + g // 2, :], ident)
            last.then_inc(pct_done, 1)
            pe.wait_ge(pct_ok, 1)

            scav = sc_a.rearrange("p (b n) -> p b n", b=2)
            scbv = sc_b.rearrange("p (b n) -> p b n", b=2)
            ptv = pt.rearrange("p (b n) -> p b n", b=2)
            vswv = v3(vsw, 512)

            def scores(u):
                j, rows = u // 2, 64 * (u % 2)
                if u >= 2:
                    pe.wait_ge(max_ok, u - 1)
                for b in range(2):
                    key = rotv[rows:rows + ND, 2 * b + j // NG, :]
                    nc.tensor.matmul(ps[:, 2 * (u % 2), b * SEQ:(b + 1) * SEQ], rotv[rows:rows + ND, 4 + j, P:2 * P], key,
                                     start=True, stop=True)
                    last = nc.tensor.matmul(ps[:, 2 * (u % 2) + 1, b * P:(b + 1) * P], rotv[rows:rows + ND, 4 + j, 0:P],
                                            key[:, 0:P], start=True, stop=True)
                last.then_inc(s_done, 1)

            def turn_p(u):
                pe.wait_ge(p_ok, u + 1)
                if u:
                    pe.wait_ge(pt_ok, u)
                for b in range(2):
                    for s in range(2):
                        nc.tensor.transpose(ps[:, 4, (2 * b + s) * P:(2 * b + s + 1) * P],
                                            scav[:, u % 2, b * SEQ + s * P:b * SEQ + (s + 1) * P], ident)
                    last = nc.tensor.transpose(ps[:, 5, b * P:(b + 1) * P], scbv[:, u % 2, b * P:(b + 1) * P], ident)
                last.then_inc(pt_done, 1)

            def values(u):
                j, pr = u // 2, u % 2
                g, r = 2 * (j // NG) + pr, j % NG
                pe.wait_ge(pt_ok, u + 1)
                if j >= 2 and pr == 0:
                    pe.wait_ge(o_ok, j - 1)
                for t in range(TT):
                    o = ps[64 * pr:64 * pr + ND, 6 + j % 2, t * P:(t + 1) * P]
                    nc.tensor.matmul(o, vcr[32 * r:32 * r + 32, g * ND:(g + 1) * ND], pcTv[32 * r:32 * r + 32, g, t, :],
                                     start=True, stop=False, tile_position=(32 * r, 64 * pr))
                    for b in range(2):
                        for s in range(t + 1):
                            col = (2 * b + s) * P if t else 512 + b * P
                            last = nc.tensor.matmul(o, vswv[:, s, b * 256 + g * ND:b * 256 + (g + 1) * ND],
                                                    ptv[:, u % 2, col:col + P], start=False, stop=(b == 1 and s == t))
                last.then_inc(pv_done, 1)

            scores(0)
            for u in range(NH + 1):
                if u + 1 < NH:
                    scores(u + 1)
                if u < NH:
                    turn_p(u)
                if u:
                    values(u - 1)
            pe.wait_ge(o_ok, NH // 2)
            pe_rows(pe, plan["nsa_o"][0], lambda k, t: v3(oT, SEQ)[:, k, t * P:(t + 1) * P], ROWB)

            pe_transpose(pe, "ffn1", xs, lambda i: P)
            pe.wait_ge(t_copied, t_all("ffn1"))
            pe_ffn(1)

            pe_transpose(pe, "mix2", xs, lambda i: META if i == 0 else P)
            pe.wait_ge(t_copied, t_all("mix2"))
            bank = fm_begin(pe)
            wg2 = v3(par("w_gates2"), 36)
            for c in range(KC):
                last = nc.tensor.matmul(ps[0:36, bank, 0:L2], wg2[:, c, :], xn[:, c, :], start=(c == 0), stop=(c == KC - 1))
            last.then_inc(small_done, 1)
            for j in range(20):
                pe_column(pe, plan["mix_q"][0] + j, xn, L2)
            S0 = [(0, META), (META, P), (META + P, P)]
            VB = [(6, 7), (2, 3), (4, 5)]
            pe_rows(pe, plan["mix_v"][0], lambda k, t: xn[:, k, S0[t][0]:S0[t][0] + S0[t][1]], VB)
            linv = v3(lin, L2)
            pe.wait_ge(row_ok, 1)
            pe.wait_ge(fm_free, fmc["pe"])
            for s in range(3):
                c0, rows = S0[s]
                nc.tensor.transpose(ps[0:rows, 0, s * 16:s * 16 + 12], linv[0:12, 1, c0:c0 + rows], ident[0:12, 0:12])
                last = nc.tensor.transpose(ps[0:rows, 0, s * 16 + 12:s * 16 + 16], linv[0:4, 3, c0:c0 + rows], ident[0:4, 0:4])
            last.then_inc(col_done, 1)
            pe.wait_ge(fsq_ok, 1)
            pe.wait_ge(col_ok, 1)
            pe.wait_ge(act_rows, 4)
            fsqv = v3(fsq, L2)
            for j in range(8):
                last = nc.tensor.matmul(ps[:, j, 0:L2], con("ones64"), fsqv[:, j, :], start=True, stop=True)
            last.then_inc(fss_done, 1)
            mqkv, v2v, stmv = v3(mqk, L2), v3(v2, D), v3(stm, 640)
            pe.wait_ge(fvar_ok, 1)
            pe.wait_ge(msilu_ok, 1)
            for h in range(MH + 1):
                if h < MH:
                    if h >= 2:
                        pe.wait_ge(mst_ok, h - 1)
                    b0, b1 = 2 * (h % 2), 2 * (h % 2) + 1
                    k, q = mqkv[:, MH + h, :], mqkv[:, h, META:L2]
                    nc.tensor.matmul(ps[:, b0, 0:256], k[:, META:META + P], q, start=True, stop=True)
                    nc.tensor.matmul(ps[:, b0, 256:384], k[:, META + P:L2], q[:, P:2 * P], start=True, stop=True)
                    nc.tensor.matmul(ps[:, b1, 0:256], bcast(ident[0:4, h:h + 1], P), linv[0:4, 4, META:L2], start=True, stop=True)
                    nc.tensor.matmul(ps[0:META, b1, 256:512], k[:, 0:META], q, start=True, stop=True).then_inc(ms_done, 1)
                if h:
                    g = h - 1
                    pe.wait_ge(mst_ok, g + 1)
                    st = stmv[:, g, :]
                    for bank, lhs in ((4 + g // 2, lambda rows, s: v2v[0:rows, s, g * MD:(g + 1) * MD]),
                                      (6 + g // 2, lambda rows, s: con("ones")[0:rows, :])):
                        o = ps[:, bank, (g % 2) * 256:(g % 2 + 1) * 256]
                        nc.tensor.matmul(o, lhs(P, 1), st[:, 0:256], start=True, stop=False)
                        nc.tensor.matmul(o[:, P:2 * P], lhs(P, 2), st[:, 256:384], start=False, stop=False)
                        last = nc.tensor.matmul(o, lhs(META, 0), st[0:META, 384:640], start=False, stop=True)
                    last.then_inc(mnum_done, 1)
            for h in range(MH):
                last = nc.tensor.matmul(ps[:, h // 2, (h % 2) * 256:(h % 2 + 1) * 256], bcast(ident[0:4, h:h + 1], P),
                                        linv[0:4, 5, META:L2], start=True, stop=True)
            last.then_inc(mb_done, 1)
            pe.wait_ge(hsq_ok, 1)
            for h in range(MH):
                last = nc.tensor.matmul(ps[:, 2 + h // 2, (h % 2) * 256:(h % 2 + 1) * 256], con("ones"),
                                        v3(em, 256)[:, h, :], start=True, stop=True)
            last.then_inc(hss_done, 1)
            pe.wait_ge(fn_ok, 1)
            pe.wait_ge(hvar_ok, 1)
            pe.wait_ge(em_ok, 1)
            fqkv, sfxv, ptfv = v3(fqk, L2), v3(sfx, 512), v3(ptf, 640)

            def fscores(u):
                j, rows = u // 2, 64 * (u % 2)
                if u >= 2:
                    pe.wait_ge(max_ok, NH + u - 1)
                b0, b1 = 2 * (u % 2), 2 * (u % 2) + 1
                nc.tensor.matmul(ps[:, b0, 0:L2], bcast(ident[0:12, 4 + u:5 + u], P), linv[0:12, 6, :], start=True, stop=True)
                q, k = fqkv[rows:rows + FD, j, :], fqkv[rows:rows + FD, 4 + j, :]
                nc.tensor.matmul(ps[:, b1, 0:L2], q[:, META + P:L2], k, start=True, stop=True)
                nc.tensor.matmul(ps[:, b1, L2:L2 + META + P], q[:, META:META + P], k[:, 0:META + P],
                                 start=True, stop=True).then_inc(s_done, 1)

            def fturn(u):
                pe.wait_ge(p_ok, NH + u + 1)
                if u:
                    pe.wait_ge(pt_ok, NH + u)
                else:
                    pe.wait_ge(hn_ok, 1)
                p1, p0 = sfxv[:, u % 2, 0:L2], sfxv[:, u % 2, L2:L2 + META + P]
                nc.tensor.transpose(ps[:, 4, 0:P], p1[:, META:META + P], ident)
                nc.tensor.transpose(ps[:, 4, P:2 * P], p1[:, META + P:L2], ident)
                nc.tensor.transpose(ps[0:META, 4, 2 * P:3 * P], p1[:, 0:META], ident)
                nc.tensor.transpose(ps[:, 5, 0:P], p0[:, META:META + P], ident)
                nc.tensor.transpose(ps[0:META, 5, P:2 * P], p0[:, 0:META], ident).then_inc(pt_done, 1)

            def fvalues(u):
                j, pr = u // 2, u % 2
                pe.wait_ge(pt_ok, NH + u + 1)
                if j >= 2 and pr == 0:
                    pe.wait_ge(o_ok, NH // 2 + j - 1)
                ptu = ptfv[:, u % 2, :]
                for t in range(TT):
                    o = ps[64 * pr:64 * pr + FD, 6 + j % 2, t * P:(t + 1) * P]
                    v = lambda rows, s: v2v[0:rows, s, 512 + u * FD:512 + (u + 1) * FD]
                    if t == 0:
                        nc.tensor.matmul(o, v(P, 1), ptu[:, 384:512], start=True, stop=False)
                        nc.tensor.matmul(o, v(META, 0), ptu[0:META, 512:640], start=False, stop=True,
                                         tile_position=(0, 64 * pr))
                    else:
                        nc.tensor.matmul(o, v(P, 1), ptu[:, 0:P], start=True, stop=False)
                        nc.tensor.matmul(o, v(P, 2), ptu[:, P:2 * P], start=False, stop=False)
                        last = nc.tensor.matmul(o, v(META, 0), ptu[0:META, 2 * P:3 * P], start=False, stop=True,
                                                tile_position=(0, 64 * pr))
                last.then_inc(pv_done, 1)

            fscores(0)
            for u in range(FH + 1):
                if u + 1 < FH:
                    fscores(u + 1)
                if u < FH:
                    fturn(u)
                if u:
                    fvalues(u - 1)
            pe.wait_ge(o_ok, NH // 2 + FH // 2)
            pe.wait_ge(y2_ok, 1)
            pe_rows(pe, plan["mix_o"][0], lambda k, t: v3(y2T, SEQ)[:, k, t * P:(t + 1) * P], ROWB)

            pe_transpose(pe, "ffn2", xs, lambda i: P)
            pe.wait_ge(t_copied, t_all("ffn2"))
            pe.wait_ge(keys_in, 16)
            qhTv = v3(qhT, SEQ)
            for j in range(2 * PH + 1):
                if j < 2 * PH:
                    pe_column(pe, plan["peer_q"][0] + j, xpT, SEQ)
                if j:
                    i = j - 1
                    pe.wait_ge(fm_free, fmc["pe"] - (1 if j < 2 * PH else 0))
                    if i % 4 == 0 and i >= 8:
                        pe.wait_ge(sc_ok, i // 4 - 1)
                    for t in range(TT):
                        last = nc.tensor.matmul(ps[:, 2 + 2 * (i // 4 % 2) + t, (i % 4) * P:(i % 4 + 1) * P],
                                                qhTv[:, i, t * P:(t + 1) * P], keysT[:, i, :], start=True, stop=True)
                    if i % 4 == 3:
                        last.then_inc(sc_done, 1)
            ixv = ix.rearrange("p (a t n) -> p a t n", a=4, t=TT)
            pe.wait_ge(rt_ok, 1)
            for a in range(3):
                for t in range(TT):
                    last = nc.tensor.transpose(ps[:, 6 + a // 2, (a % 2) * SEQ + t * P:(a % 2) * SEQ + (t + 1) * P],
                                               ixv[:, a, t, :], ident)
            last.then_inc(rt_done, 1)
            pe.wait_ge(route_ok, 1)
            with pe.Fori(0, SEQ // 8) as i:
                for b in range(2):
                    pe.wait_ge(oh_ok, i * 2 + (b + 1))
                    pe.wait_ge(g_ok, i * 2 + (b + 1))
                    for q in range(4):
                        last = nc.tensor.matmul(ps[:, 6 + b, q * P:(q + 1) * P], onehot[:, b, 0, q, :],
                                                onehot[:, b, 1, q, :], start=True, stop=True)
                    last.then_inc(g_done, 1)
            def expert_u(tile, bank, need, it=None):
                split_wait(pe, "peer", tile, it, 2)
                if need is not None:
                    pe.wait_ge(gelu_ok, need)
                split_columns("peer", tile, bank, peer_x_hi, peer_x_lo)

            def expert_v(tile, buf, first, last_j, need, it=None):
                split_wait(pe, "peer", tile, it, 2)
                pe.wait_ge(ph_ok, need)
                split_rows("peer", tile, buf, first, last_j)

            def step(j):
                expert_u(2 * j - 1, j % 2, j - 1 if j >= 2 else None)
                expert_v(2 * j, (j - 1) % 2, j == 1, False, j)

            pe.wait_ge(xlo_ok, XCNT["ffn2"])
            expert_u(0, 0, None)
            for j in range(1, 4):
                step(j)
            LOOPS = (NKEY - 4) // 6
            with pe.Fori(0, LOOPS) as i:
                for k in range(6):
                    j = 4 + k
                    need_u, need_v = i * 6 + (j - 1), i * 6 + j
                    expert_u(2 * j - 1, j % 2, need_u, i)
                    expert_v(2 * j, (j - 1) % 2, False, False, need_v, i)
            for j in range(4 + 6 * LOOPS, NKEY):
                step(j)
            expert_v(2 * NKEY - 1, 1, False, True, NKEY)

        @block.scalar
        def _(act):
            act.dma_start(x[:, :, :], x_in.rearrange("(t p) d -> p t d", p=P)).then_inc(x_in_sem, 16)
            act.dma_start(prm[:, :], params).then_inc(prm_in, 16)
            act.dma_start(cst[:, :], consts).then_inc(prm_in, 16)
            act.wait_ge(dve_step, 1)

            def act_ffn(layer):
                cw = par(f"conv{layer}").rearrange("p (f s w) -> p f s w", s=2, w=4)
                n0, h0 = plan[f"ffn{layer}"][0], FT * layer

                name = f"ffn{layer}"

                def tile(f, k, need_u, need_h, need_c, it=None):
                    first = 3 * k - 1 if k else 0
                    for s, dst in enumerate((cgate, cval)):
                        act.wait_ge(tile_done, need_u + s)
                        if need_h is not None:
                            act.wait_ge((silu_done, h_ready)[s], need_h)
                        nc.scalar.activation(dst, ps[:, s, 0:SEQ], ACT.Identity, bias=cw[:, f, s, 3:4],
                                             scale=cw[:, f, s, 2:3]).then_inc(c0_done, 1)
                        if first + s + HI < 3 * FT:
                            split_hi(act, name, first + s + HI, it)
                    act.wait_ge(cg_done, need_c)
                    nc.scalar.activation(sgate, cgate, ACT.Silu).then_inc(silu_done, 1)
                    if 0 < k < FT - 1:
                        act.wait_ge(tile_done, need_u + 2)
                        split_hi(act, name, first + 2 + HI, it)

                act_input(act, name, ffn_x_hi)
                tile(0, 0, n0 + 1, h0 if h0 else None, h0 + 1)
                with act.Fori(0, (FT - 2) // 2) as i:
                    for k in (1, 2):
                        tile(i * 2 + k, k, i * 6 + (n0 + 3 * k), i * 2 + (h0 + k), i * 2 + (h0 + k + 1), i)
                f = FT - 1
                tile(f, f, 3 * f + n0, f + h0, f + h0 + 1)

            def act_ahead(name):
                for tile in range(HI):
                    split_hi(act, name, tile)

            act_norm(act, "mix0")
            act.wait_ge(abs_ok, 1)
            alink(act, nc.scalar.activation(dec, dec, ACT.Exp, scale=-1.0))
            nc.scalar.activation(dec, dec, ACT.Ln, bias=1.0).then_inc(ln_ok, 1)
            rows_wait(act, "gla_v")
            for t in range(TT):
                for half in range(2):
                    last = nc.scalar.activation(v3(vtok, D)[:, t, half * 512:(half + 1) * 512], ps[:, ROWB[t][half], :], ACT.Copy)
            last.then_inc(act_rows, 1)
            for buf, need in ((qx, 1), (ka, 2), (kd, 3)):
                act.wait_ge(dsub_ok, need)
                nc.scalar.activation(buf, buf, ACT.Exp, scale=1.0 / GTAU).then_inc(dexp_ok, 1)
            nc.scalar.activation(qb, bcum, ACT.Exp, scale=1.0 / GTAU).then_inc(dexp_ok, 1)
            rows_wait(act, "gla_r")
            RB = [(6, 7), (0, 1)]
            for t in range(TT):
                for half in range(2):
                    last = nc.scalar.activation(v3(rtok, D)[:, t, half * 512:(half + 1) * 512], ps[:, RB[t][half], :], ACT.Silu)
            last.then_inc(act_rows, 1)
            act.wait_ge(kdt_done, 1)
            for b in range(2):
                last = nc.scalar.activation(kdT[:, b * 512:(b + 1) * 512], ps[:, 3 + b, :], ACT.Copy)
            last.then_inc(kdt_ok, 1)
            OB = [6, 7, 0, 1]
            for t in range(TT):
                act.wait_ge(go_done, 2 * t + 2)
                for h in range(GH):
                    last = nc.scalar.activation(v3(ytok, D)[:, t, h * GDV:(h + 1) * GDV],
                                                ps[:, OB[2 * t + h // 2], (h % 2) * GDV:(h % 2 + 1) * GDV], ACT.Square,
                                                accum_out=stat[:, 32 + t * GH + h:33 + t * GH + h])
                last.then_inc(osq_ok, 1)
            act.wait_ge(ovar_ok, 1)
            nc.scalar.activation(stat[:, 40:48], stat[:, 48:56], ACT.Sqrt).then_inc(osd_ok, 1)

            act_ahead("ffn0")
            act_norm(act, "ffn0")
            act_ffn(0)

            act_norm(act, "mix1")
            act.wait_ge(fm_free, 3 * GH + 1 + 4)
            cr = cmpraw.rearrange("p (b g t) -> p b g t", b=2, g=2)
            sh = shifted.rearrange("p (b g r t) -> p b g r t", b=2, g=2, r=2)
            for b in range(2):
                for r in range(2):
                    act.dma_start(sh[0:64, b, :, r, :], cr[64 * r:64 * r + 64, b, :, :]).then_inc(shift_in, 16)
                    act.dma_start(sh[64:128, b, :, r, 0:SEQ - 1], cr[64 * r:64 * r + 64, b, :, 1:SEQ]).then_inc(shift_in, 16)
            rows_wait(act, "nsa_v")
            for t in range(TT):
                last = nc.scalar.activation(v3(vsw, 512)[:, t, :], ps[:, 2 + t, :], ACT.Copy)
            last.then_inc(act_rows, 1)
            act.wait_ge(gate_done, 1)
            nc.scalar.activation(v3(gs, 3 * NH), ps[:, 4, 0:128].rearrange("p (t n) -> p t n", t=TT)[:, :, 0:3 * NH],
                                 ACT.Sigmoid).then_inc(gate_ok, 1)
            rows_wait(act, "cmp_v")
            nc.scalar.activation(hid[0:NKV * NCMP, :], ps[0:NKV * NCMP, 5, :], ACT.Gelu_apprx_tanh).then_inc(hid_ok, 1)
            act.wait_ge(cs_ok, 1)
            nc.scalar.activation(csc[:, 0:480], csc[:, 0:480], ACT.Exp).then_inc(ce_ok, 1)
            act.wait_ge(pct_done, 1)
            for b in range(2):
                last = nc.scalar.activation(pcT[:, b * 512:(b + 1) * 512], ps[:, 2 + b, :], ACT.Copy)
            last.then_inc(pct_ok, 1)
            scav, scbv, ptv = v3(sc_a, 512), v3(sc_b, 256), v3(pt, 768)

            def copy_pt(u):
                act.wait_ge(pt_done, u + 1)
                if u >= 2:
                    act.wait_ge(pv_done, u - 1)
                nc.scalar.activation(ptv[:, u % 2, 0:512], ps[:, 4, :], ACT.Copy)
                nc.scalar.activation(ptv[:, u % 2, 512:768], ps[:, 5, 0:256], ACT.Copy).then_inc(pt_ok, 1)

            for u in range(NH + 1):
                if u < NH:
                    act.wait_ge(max_ok, u + 1)
                    c = 8 * (u % 2)
                    for b in range(2):
                        a = scav[:, u % 2, b * SEQ:(b + 1) * SEQ]
                        nc.scalar.activation(a, a, ACT.Exp, bias=stat[:, 32 + c + b:33 + c + b],
                                             accum_out=stat[:, 36 + c + b:37 + c + b])
                        a = scbv[:, u % 2, b * P:(b + 1) * P]
                        last = nc.scalar.activation(a, a, ACT.Exp, bias=stat[:, 34 + c + b:35 + c + b],
                                                    accum_out=stat[:, 38 + c + b:39 + c + b])
                    last.then_inc(exp_ok, 1)
                if u:
                    copy_pt(u - 1)

            act_ahead("ffn1")
            act_norm(act, "ffn1")
            act_ffn(1)

            act.wait_ge(x_ready, 8)
            act.dma_start(xm, meta_in).then_inc(meta_sem, 16)
            act.dma_start(gfin, g_final.partition_broadcast(P)).then_inc(fin_sem, 16)
            act_norm(act, "final")
            act_norm(act, "mix2")
            act.wait_ge(gab_ok, 1)
            linv = v3(lin, L2)
            mqkv = v3(mqk, L2)
            alink(act, nc.scalar.activation(linv[0:12, 2, :], linv[0:12, 2, :], ACT.Exp, scale=-1.0))
            nc.scalar.activation(linv[0:12, 2, :], linv[0:12, 2, :], ACT.Ln, bias=1.0).then_inc(gln_ok, 1)
            cm = v3(par("conv_m"), MCONV)
            for j in range(2 * MH):
                fm_wait(act, FM2 + 1 + j)
                nc.scalar.activation(mqkv[:, j, :], ps[:, (FM2 + 1 + j) % 2, 0:L2], ACT.Copy,
                                     scale=cm[:, j, 3:4]).then_inc(mc0, 1)
            act.wait_ge(fm_free, FM2 + 1 + 2 * MH)
            nc.scalar.activation(mqk, mqk, ACT.Silu).then_inc(msilu_ok, 1)
            act.wait_ge(fm_free, FM2 + 1 + 20)
            nc.scalar.activation(fsq, fqk, ACT.Square).then_inc(fsq_ok, 1)
            rows_wait(act, "mix_v")
            VB, ROWS = [(6, 7), (2, 3), (4, 5)], [META, P, P]
            for s in range(3):
                for half in range(2):
                    last = nc.scalar.activation(v3(v2, D)[0:ROWS[s], s, half * 512:(half + 1) * 512],
                                                ps[0:ROWS[s], VB[s][half], :], ACT.Copy)
            last.then_inc(act_rows, 1)
            act.wait_ge(fvar_ok, 1)
            nc.scalar.activation(fsq, fsq, ACT.Sqrt).then_inc(fsd_ok, 1)
            wv = v3(wts, 640)
            for h in range(MH):
                act.wait_ge(mw_ok, h + 1)
                nc.scalar.activation(wv[:, h, 0:384], wv[:, h, 0:384], ACT.Exp)
                nc.scalar.activation(wv[0:META, h, 384:640], wv[0:META, h, 384:640], ACT.Exp).then_inc(mexp_ok, 1)
            act.wait_ge(mb_done, 1)
            for b in range(2):
                last = nc.scalar.activation(em[:, b * 512:(b + 1) * 512], ps[:, b, :], ACT.Exp, scale=-1.0)
            last.then_inc(em_ok, 1)
            act.wait_ge(hn_ok, 1)
            nc.scalar.activation(em, hn, ACT.Square).then_inc(hsq_ok, 1)
            act.wait_ge(hvar_ok, 1)
            alink(act, nc.scalar.activation(dn, dn, ACT.Sqrt))
            nc.scalar.activation(mo, mo, ACT.Sigmoid).then_inc(hsd_ok, 1)
            sfxv, ptfv = v3(sfx, 512), v3(ptf, 640)
            for u in range(FH + 1):
                if u < FH:
                    act.wait_ge(max_ok, NH + u + 1)
                    c = 8 * (u % 2)
                    a = sfxv[:, u % 2, 0:L2]
                    nc.scalar.activation(a, a, ACT.Exp, bias=stat[:, 32 + c:33 + c], accum_out=stat[:, 34 + c:35 + c])
                    a = sfxv[:, u % 2, L2:L2 + META + P]
                    nc.scalar.activation(a, a, ACT.Exp, bias=stat[:, 33 + c:34 + c],
                                         accum_out=stat[:, 35 + c:36 + c]).then_inc(exp_ok, 1)
                if u:
                    w = u - 1
                    act.wait_ge(pt_done, NH + w + 1)
                    if w >= 2:
                        act.wait_ge(pv_done, NH + w - 1)
                    nc.scalar.activation(ptfv[:, w % 2, 0:256], ps[:, 4, 0:256], ACT.Copy)
                    nc.scalar.activation(ptfv[0:META, w % 2, 256:384], ps[0:META, 4, 256:384], ACT.Copy)
                    nc.scalar.activation(ptfv[:, w % 2, 384:512], ps[:, 5, 0:128], ACT.Copy)
                    nc.scalar.activation(ptfv[0:META, w % 2, 512:640], ps[0:META, 5, 128:256], ACT.Copy).then_inc(pt_ok, 1)

            act.wait_ge(x_ready, 12)
            act.dma_start(keysT, keys).then_inc(keys_in, 16)
            act_norm(act, "ffn2")
            act_input(act, "ffn2", peer_x_hi)
            scv = scs.rearrange("p (t i n) -> p t i n", t=TT, i=2 * PH)
            for i in range(4):
                act.wait_ge(sc_done, i + 1)
                for t in range(TT):
                    last = nc.scalar.activation(scv[:, t, 4 * i:4 * i + 4, :],
                                                ps[:, 2 + 2 * (i % 2) + t, :].rearrange("p (i n) -> p i n", n=NKEY), ACT.Copy)
                last.then_inc(sc_ok, 1)
            act.wait_ge(gsub_ok, 1)
            nc.scalar.activation(tops, tops, ACT.Exp).then_inc(gexp_ok, 1)
            act.wait_ge(route_ok, 1)
            act.sem_inc(g_ok, 2)
            with act.Fori(0, SEQ // 8) as i:
                for b in range(2):
                    act.wait_ge(g_done, i * 2 + (b + 1))
                    nc.scalar.activation(gates_j[:, :, bass.ds(i * 8 + 4 * b, 4)],
                                         ps[:, 6 + b, :].rearrange("p (t j) -> p j t", j=NKEY), ACT.Copy).then_inc(g_ok, 1)
            act.wait_ge(g_done, SEQ // 4)
            act_ahead("peer")

            def gelu(par_, need_a, need_h):
                act.wait_ge(tile_done, need_a)
                if need_h is not None:
                    act.wait_ge(ph_ok, need_h)
                nc.scalar.activation(gbuf[:, par_, :], ps[:, par_, 0:SEQ], ACT.Gelu).then_inc(gelu_ok, 1)

            n0 = plan["peer"][0]
            gelu(0, n0 + 1, None)
            split_hi(act, "peer", HI)
            with act.Fori(0, (NKEY - 2) // 6) as i:
                for j in range(1, 7):
                    gelu(j % 2, i * 12 + (n0 + 2 * j), i * 6 + (j - 1))
                    split_hi(act, "peer", 2 * j - 1 + HI, i, 2)
                    act.wait_ge(tile_done, i * 12 + (n0 + 2 * j + 1))
                    split_hi(act, "peer", 2 * j + HI, i, 2)
            j = NKEY - 1
            gelu(j % 2, n0 + 2 * j, j - 1)

        @block.vector
        def _(dve):
            def dve_ffn(layer):
                cw = par(f"conv{layer}").rearrange("p (f s w) -> p f s w", s=2, w=4)
                u0, h0 = 2 * FT * layer, FT * layer
                name = f"ffn{layer}"

                def tile(f, k, c0, step, need_s, it=None):
                    first = 3 * k - 1 if k else 0
                    for s, dst in enumerate((cgate, cval)):
                        dve.wait_ge(c0_done, c0 + s)
                        nc.vector.scalar_tensor_tensor(dst[:, 1:SEQ], ps[:, s, 0:SEQ - 1], cw[:, f, s, 1:2], dst[:, 1:SEQ],
                                                       ALU.mult, ALU.add).then_inc(dve_step, 1)
                        dve.wait_ge(dve_step, step + (s + 1))
                        last = nc.vector.scalar_tensor_tensor(dst[:, 2:SEQ], ps[:, s, 0:SEQ - 2], cw[:, f, s, 0:1], dst[:, 2:SEQ],
                                                              ALU.mult, ALU.add)
                        last.then_inc((cg_done, cv_done)[s], 1)
                        if s == 0 and first + HI < 3 * FT:
                            split_lo(dve, name, first + HI, it)
                    dve.wait_ge(cv_done, need_s)
                    dve.wait_ge(silu_done, need_s)
                    nc.vector.tensor_tensor(hfull, sgate, cval, ALU.mult).then_inc(dve_step, 1)
                    dve.wait_ge(dve_step, step + 3)
                    split_hidden(dve, hfull, k % 2, step + 4, h_ready)
                    if k < FT - 1:
                        split_lo(dve, name, first + 1 + HI, it)
                        if k:
                            split_lo(dve, name, first + 2 + HI, it)

                dve_input(dve, name, ffn_x_hi, ffn_x_lo)
                d0 = cnt["dve"]
                tile(0, 0, u0 + 1, d0, h0 + 1)
                with dve.Fori(0, (FT - 2) // 2) as i:
                    for k in (1, 2):
                        tile(i * 2 + k, k, i * 4 + (u0 + 2 * k + 1), i * 8 + (d0 + 4 * k), i * 2 + (h0 + k + 1), i)
                f = FT - 1
                tile(f, f, u0 + 2 * f + 1, d0 + 4 * f, h0 + f + 1)
                cnt["dve"] = d0 + 4 * FT

            def dve_ahead(name):
                for tile in range(HI):
                    split_lo(dve, name, tile)

            dlink(dve, nc.vector.memset(stat[:, :], 1.0))
            dve.wait_ge(prm_in, 32)
            dve_norm(dve, "mix0")
            dve_transpose(dve, "mix0", own_cols, [(xn, "g_mix0")])
            for h in range(2 * GH):
                bank = fm_take(dve)
                dst = v3(qT if h < GH else kT, SEQ)[:, h % GH, :]
                nc.vector.tensor_copy(dst, ps[:, bank, 0:SEQ]).then_inc(fm_free, 1)
            bank = fm_take(dve)
            nc.vector.tensor_copy(dec[0:GRANK, 0:SEQ], ps[0:GRANK, bank, 0:SEQ]).then_inc(fm_free, 1)
            for h in range(GH):
                bank = fm_take(dve)
                nc.vector.tensor_scalar(v3(z, SEQ)[:, h, :], ps[:, bank, 0:SEQ], par("b_alpha")[:, h:h + 1], None,
                                        ALU.add).then_inc(fm_free, 1)
            dve.wait_ge(fm_free, fmc["dve"])
            nc.vector.scalar_tensor_tensor(dec, z, -1.0, z, ALU.mult, ALU.max).then_inc(abs_ok, 1)
            dve.wait_ge(ln_ok, 1)
            dlink(dve, nc.vector.scalar_tensor_tensor(z, z, 0.0, dec, ALU.min, ALU.subtract))
            for h in range(GH):
                last = nc.vector.tensor_tensor_scan(v3(bcum, SEQ)[:, h, :], con("reset"), v3(z, SEQ)[:, h, :], 0.0,
                                                    ALU.mult, ALU.add)
            dlink(dve, last)
            GR = GH * NCH
            bg = bcum.rearrange("p (g t) -> p g t", t=GC)
            NS = GC // GSUB
            qg = qx.rearrange("p (g a t) -> p g a t", a=NS, t=GSUB)
            bs = bcum.rearrange("p (g a t) -> p g a t", a=NS, t=GSUB)
            nc.vector.tensor_copy(qg[:, :, 0, :], bs[:, :, 0, :])
            nc.vector.tensor_tensor(qg[:, :, 1:NS, :], bs[:, :, 1:NS, :],
                                    bcast(bs[:, :, 0:NS - 1, GSUB - 1:GSUB], GR, NS - 1, GSUB), ALU.subtract).then_inc(dsub_ok, 1)
            kg = ka.rearrange("p (a g t) -> p a g t", a=NS, t=GC)
            nc.vector.tensor_scalar(kg[:, 0], bg, -1.0, None, ALU.mult)
            for a in range(1, NS):
                last = nc.vector.tensor_tensor(kg[:, a], bcast(bg[:, :, a * GSUB - 1:a * GSUB], GR, GC), bg, ALU.subtract)
            dlink(dve, last)
            nc.vector.tensor_scalar(ka, ka, CLAMP * GTAU, None, ALU.min).then_inc(dsub_ok, 1)
            nc.vector.tensor_tensor(kd.rearrange("p (g t) -> p g t", t=GC), bcast(bg[:, :, GC - 1:GC], GR, GC), bg,
                                    ALU.subtract).then_inc(dsub_ok, 1)
            dve.wait_ge(dexp_ok, 1)
            nc.vector.scalar_tensor_tensor(qx, qx, GDK ** -0.5, qT, ALU.mult, ALU.mult).then_inc(dmul_ok, 1)
            dve.wait_ge(dexp_ok, 2)
            kav = ka.rearrange("p (a n) -> p a n", a=NS)
            nc.vector.tensor_tensor(kav, kav, bcast(kT.unsqueeze(1), NS, GH * SEQ), ALU.mult).then_inc(dmul_ok, 1)
            dve.wait_ge(dexp_ok, 3)
            nc.vector.tensor_tensor(kd, kd, kT, ALU.mult).then_inc(dmul_ok, 1)
            dve.wait_ge(dexp_ok, 4)
            dlink(dve, nc.vector.tensor_copy(stat[:, 16:32], qb.rearrange("p (g t) -> p g t", t=GC)[:, :, GC - 1]))
            nc.vector.scalar_tensor_tensor(qb, qb, GDK ** -0.5, qT, ALU.mult, ALU.mult).then_inc(dmul_ok, 1)
            dve.wait_ge(att_done, 1)
            nc.vector.tensor_tensor(v3(att, GC), v3(ps[:, 2, :], GC), bcast(con("tril").unsqueeze(1), GH * TT, GC),
                                    ALU.mult).then_inc(att_ok, 1)
            stv = state.rearrange("p (b h v) -> p b h v", b=2, h=GH)
            for c in range(NCH - 1):
                dve.wait_ge(kv_done, c + 1)
                if c:
                    dve.wait_ge(go_done, c)
                for h in range(GH):
                    got = ps[:, (2, 5)[h // 2], (h % 2) * GDV:(h % 2 + 1) * GDV]
                    new = stv[:, (c + 1) % 2, h, :]
                    if c == 0:
                        last = nc.vector.tensor_copy(new, got)
                    else:
                        last = nc.vector.scalar_tensor_tensor(new, stv[:, c % 2, h, :],
                                                              stat[:, 16 + h * NCH + c:17 + h * NCH + c], got,
                                                              ALU.mult, ALU.add)
                last.then_inc(state_ok, 1)
                dve.wait_ge(state_ok, c + 1)
            dve.wait_ge(osq_ok, TT)
            nc.vector.tensor_scalar(stat[:, 48:56], stat[:, 32:40], 1.0 / GDV, EPS, ALU.mult, ALU.add).then_inc(ovar_ok, 1)
            dve.wait_ge(osd_ok, 1)
            dlink(dve, nc.vector.reciprocal(stat[:, 56:64], stat[:, 40:48]))
            OB = [6, 7, 0, 1]
            dve.wait_ge(act_rows, 2)
            for t in range(TT):
                for h in range(GH):
                    cols = slice(h * GDV, (h + 1) * GDV)
                    last = nc.vector.scalar_tensor_tensor(v3(ytok, D)[:, t, cols],
                                                          ps[:, OB[2 * t + h // 2], (h % 2) * GDV:(h % 2 + 1) * GDV],
                                                          stat[:, 56 + t * GH + h:57 + t * GH + h],
                                                          v3(rtok, D)[:, t, cols], ALU.mult, ALU.mult)
                last.then_inc(tok_ready, 1)
            dve_transpose(dve, "gla", own_cols, [(v3(yT, SEQ), "g_gla")])
            dve_residual(dve, "gla_o")

            dve_ahead("ffn0")
            dve_norm(dve, "ffn0")
            dve_transpose(dve, "ffn0", own_cols, [(xn, "g_ffn0")])
            dve_ffn(0)
            dve_residual(dve, "ffn0")

            dve_norm(dve, "mix1")
            dve_transpose(dve, "mix1", own_cols, [(xn, "g_mix1"), (v3(xkv, SEQ), "g_kv")])
            for j in range(4):
                bank = fm_take(dve)
                last = nc.vector.tensor_copy(v3(cmpraw, SEQ)[:, j, :], ps[:, bank, 0:SEQ])
                last.then_inc(fm_free, 1)
            nc.vector.memset(hvr, 0.0)
            nc.vector.memset(pc, 0.0)
            rawv, rotv = v3(raw, SEQ), v3(rot, SEQ)
            for j in range(13):
                if j < 12:
                    bank = fm_take(dve)
                    nc.vector.tensor_copy(rawv[:, j, :], ps[:, bank, 0:SEQ]).then_inc(fm_free, 1)
                if j:
                    i = j - 1
                    dve.wait_ge(rot_done, i + 1)
                    nc.vector.tensor_tensor(rotv[:, i, :], ps[:, 6 + i % 2, 0:SEQ], con("sin"), ALU.mult).then_inc(rot_free, 1)
                    dlink(dve, nc.vector.tensor_tensor(tmp[:, 0:SEQ], rawv[:, i, :], con("cos"), ALU.mult))
                    dlink(dve, nc.vector.tensor_tensor(rotv[:, i, :], rotv[:, i, :], tmp[:, 0:SEQ], ALU.add))
            dve.wait_ge(shift_in, 16 * 8)
            blkv = blk.rearrange("p (b l g n) -> p b l g n", b=2, l=CB // 2, g=NKV)
            shv = shifted.rearrange("p (b g t) -> p b g t", b=2, g=NKV)
            for b, pe_ in ((0, "pe_k"), (1, "pe_v")):
                for g in range(NKV):
                    src = shv[:, b, g, :].rearrange("p (n l e) -> p l n e", l=CB // 4, e=2)
                    lo, hi = src[:, :, 0:NCMP, 0], src[:, :, 1:NCMP + 1, 0]
                    for q, half in enumerate((lo, hi)):
                        ls = slice(q * CB // 4, (q + 1) * CB // 4)
                        last = nc.vector.tensor_tensor(blkv[:, b, ls, g, :], half,
                                                       bcast(par(pe_)[:, ls].unsqueeze(2), CB // 4, NCMP), ALU.add)
                last.then_inc(blk_ok, 1)
            NB = NKV * NCMP
            dve.wait_ge(ht_done, 1)
            hb = v3(ps[:, 6, 0:256], 64)
            hvrv = hvr.rearrange("p (c g r n) -> p c g r n", c=2, g=NKV, r=NG)
            nc.vector.tensor_copy(hidT[:, 0:2 * NB].rearrange("p (c n) -> p c n", c=2), hb[:, 0:2, 0:NB])
            for c in range(2):
                last = nc.vector.tensor_copy(hvrv[:, c, :, :, 0:NCMP],
                                             bcast(hb[:, 2 + c, 0:NB].rearrange("p (g n) -> p g n", g=NKV).unsqueeze(2),
                                                   NKV, NG, NCMP))
            last.then_inc(ht_ok, 1)
            dve.wait_ge(kc_done, 1)
            nc.vector.tensor_copy(kcT[:, 0:NB], ps[:, 7, 0:NB])
            nc.vector.tensor_copy(vcr, ps[:, 7, 64:320]).then_inc(kc_ok, 1)
            csv = csc[:, 0:480].rearrange("p (t h n) -> p t h n", t=TT, h=NH)
            for t in range(TT):
                dve.wait_ge(cs_done, t + 1)
                mask = con("cmask")[:, t * NCMP:(t + 1) * NCMP]
                for b in range(2):
                    got = ps[:, CSB[2 * t + b], 0:128].rearrange("p (h n) -> p h n", n=16)[:, :, 0:NCMP]
                    last = nc.vector.scalar_tensor_tensor(csv[:, t, 8 * b:8 * b + 8], got, ND ** -0.5,
                                                          bcast(mask.unsqueeze(1), 8, NCMP), ALU.mult, ALU.add)
            dlink(dve, last)
            cflat = csc[:, 0:480].rearrange("p (h n) -> p h n", n=NCMP)
            dlink(dve, nc.vector.tensor_reduce(tmp[:, 0:32], cflat, AX.X, ALU.max))
            nc.vector.tensor_tensor(cflat, cflat, bcast(tmp[:, 0:32].unsqueeze(2), 32, NCMP), ALU.subtract).then_inc(cs_ok, 1)
            dve.wait_ge(ce_ok, 1)
            dlink(dve, nc.vector.tensor_reduce(tmp[:, 32:64], cflat, AX.X, ALU.add))
            dlink(dve, nc.vector.reciprocal(tmp[:, 64:96], tmp[:, 32:64]))
            dve.wait_ge(gate_ok, 1)
            gsv = gs.rearrange("p (t b h) -> p t b h", t=TT, b=3)
            for t in range(TT):
                for b in range(2):
                    c = t * NH + 8 * b
                    last = nc.vector.scalar_tensor_tensor(
                        v3(tmp[:, 96 + c:104 + c], NG), v3(tmp[:, 64 + c:72 + c], NG), con("cvalid")[:, t:t + 1],
                        gsv[:, t, 0, :].rearrange("p (g b r) -> p g b r", b=2, r=NG)[:, :, b, :], ALU.mult, ALU.mult)
            dlink(dve, last)
            pcv = pc.rearrange("p (h n) -> p h n", n=32)
            nc.vector.tensor_tensor(pcv[:, :, 0:NCMP], cflat, bcast(tmp[:, 96:128].unsqueeze(2), 32, NCMP),
                                    ALU.mult).then_inc(pc_ok, 1)
            scav, scbv = v3(sc_a, 512), v3(sc_b, 256)

            def logits(u):
                dve.wait_ge(s_done, u + 1)
                if u >= 2:
                    dve.wait_ge(pt_done, u - 1)
                a, b, c = v3(scav[:, u % 2, :], SEQ), v3(scbv[:, u % 2, :], P), 8 * (u % 2)
                nc.vector.scalar_tensor_tensor(a, v3(ps[:, 2 * (u % 2), :], SEQ), ND ** -0.5,
                                               bcast(con("mask1").unsqueeze(1), 2, SEQ), ALU.mult, ALU.add)
                dlink(dve, nc.vector.scalar_tensor_tensor(b, v3(ps[:, 2 * (u % 2) + 1, 0:256], P), ND ** -0.5,
                                                          bcast(con("mask0").unsqueeze(1), 2, P), ALU.mult, ALU.add))
                nc.vector.tensor_reduce(stat[:, 32 + c:34 + c], a, AX.X, ALU.max, negate=True)
                nc.vector.tensor_reduce(stat[:, 34 + c:36 + c], b, AX.X, ALU.max, negate=True).then_inc(max_ok, 1)

            def probs(u):
                j, c = u // 2, 8 * (u % 2)
                h = (2 * (j // NG) + u % 2) * NG + j % NG
                dve.wait_ge(exp_ok, u + 1)
                dlink(dve, nc.vector.reciprocal(tmp[:, 0:4], stat[:, 36 + c:40 + c]))
                nc.vector.tensor_tensor(tmp[:, 4:6], tmp[:, 0:2], gsv[:, 1, 1:3, h], ALU.mult)
                dlink(dve, nc.vector.tensor_tensor(tmp[:, 6:8], tmp[:, 2:4], gsv[:, 0, 1:3, h], ALU.mult))
                for b in range(2):
                    a = scav[:, u % 2, b * SEQ:(b + 1) * SEQ]
                    nc.vector.tensor_scalar(a, a, tmp[:, 4 + b:5 + b], None, ALU.mult)
                    a = scbv[:, u % 2, b * P:(b + 1) * P]
                    last = nc.vector.tensor_scalar(a, a, tmp[:, 6 + b:7 + b], None, ALU.mult)
                last.then_inc(p_ok, 1)

            def heads_out(j, need, dst, base):
                dve.wait_ge(pv_done, need)
                nc.vector.tensor_copy(dst, ps[:, 6 + j % 2, 0:SEQ]).then_inc(o_ok, 1)

            for u in range(NH + 2):
                if u < NH:
                    logits(u)
                if 1 <= u <= NH:
                    probs(u - 1)
                if u >= 3 and u % 2 == 1:
                    heads_out((u - 3) // 2, u - 1, v3(oT, SEQ)[:, (u - 3) // 2, :], 0)
            dve_residual(dve, "nsa_o")

            dve_ahead("ffn1")
            dve_norm(dve, "ffn1")
            dve_transpose(dve, "ffn1", own_cols, [(xn, "g_ffn1")])
            dve_ffn(1)
            dve_residual(dve, "ffn1")

            dve.wait_ge(fin_sem, 16)
            dve_norm(dve, "final", gain=gfin)
            dve_norm(dve, "mix2")
            dve_transpose(dve, "mix2", meta_cols, [(xn, "g_mix2")])
            linv, mqkv = v3(lin, L2), v3(mqk, L2)
            bank = fm_take(dve)
            nc.vector.tensor_scalar(linv[0:12, 0, :], ps[0:12, bank, 0:L2], par("b_forget")[0:12, :], None, ALU.add)
            nc.vector.tensor_scalar(linv[0:4, 7, :], ps[32:36, bank, 0:L2], par("b_input")[32:36, :], None,
                                    ALU.add).then_inc(fm_free, 1)
            dve.wait_ge(fm_free, fmc["dve"])
            last = nc.vector.scalar_tensor_tensor(linv[0:12, 2, :], linv[0:12, 0, :], -1.0, linv[0:12, 0, :], ALU.mult, ALU.max)
            last.then_inc(gab_ok, 1)
            cm = v3(par("conv_m"), MCONV)
            for j in range(2 * MH):
                bank = fm_take(dve)
                dve.wait_ge(mc0, j + 1)
                for tap in range(MCONV - 2, -1, -1):
                    d = MCONV - 1 - tap
                    last = nc.vector.scalar_tensor_tensor(mqkv[:, j, d:L2], ps[:, bank, 0:L2 - d], cm[:, j, tap:tap + 1],
                                                          mqkv[:, j, d:L2], ALU.mult, ALU.add)
                    if tap:
                        dlink(dve, last)
                last.then_inc(fm_free, 1)
            dve.wait_ge(gln_ok, 1)
            dlink(dve, nc.vector.scalar_tensor_tensor(linv[0:12, 0, :], linv[0:12, 0, :], 0.0, linv[0:12, 2, :], ALU.min, ALU.subtract))
            dlink(dve, nc.vector.tensor_tensor_scan(linv[0:12, 1, :], bcast(con("ones")[0:12, 0:1], L2), linv[0:12, 0, :], 0.0,
                                                    ALU.mult, ALU.add))
            dlink(dve, nc.vector.tensor_tensor(linv[0:4, 3, :], linv[0:4, 7, :], linv[0:4, 1, :], ALU.subtract))
            dlink(dve, nc.vector.tensor_tensor_scan(linv[0:4, 8, :], linv[0:4, 3, :], linv[0:4, 3, :], 0.0, ALU.max, ALU.max))
            nc.vector.tensor_tensor(linv[0:4, 5, :], linv[0:4, 8, :], linv[0:4, 1, :], ALU.add)
            nc.vector.tensor_scalar(linv[0:4, 4, :], linv[0:4, 8, :], -1.0, None, ALU.mult)
            nc.vector.tensor_scalar(linv[0:12, 6, :], linv[0:12, 1, :], -1.0, None, ALU.mult).then_inc(row_ok, 1)
            for j in range(12):
                bank = fm_take(dve)
                dst = v3(mo, L2)[:, j, :] if j < 4 else v3(fqk, L2)[:, j - 4, :]
                last = nc.vector.tensor_copy(dst, ps[:, bank, 0:L2])
                last.then_inc(fm_free, 1)
            dve.wait_ge(col_done, 1)
            cols = v3(colb[:, :], 16)
            for s, rows in ((0, META), (1, P), (2, P)):
                last = nc.vector.tensor_copy(cols[0:rows, s, :], ps[0:rows, 0, s * 16:(s + 1) * 16])
            last.then_inc(col_ok, 1)
            dve.wait_ge(col_ok, 1)
            dve.wait_ge(fss_done, 1)
            nc.vector.tensor_scalar(v3(fsq, L2), ps[:, :, 0:L2], 1.0 / FD, EPS, ALU.mult, ALU.add).then_inc(fvar_ok, 1)
            wv, stmv = v3(wts, 640), v3(stm, 640)
            mT = con("maskT")

            def weights(h):
                dve.wait_ge(ms_done, h + 1)
                b1 = 2 * (h % 2) + 1
                nc.vector.scalar_tensor_tensor(wv[:, h, 0:256], ps[:, b1, 0:256], cols[:, 1, 12 + h:13 + h], mT, ALU.add, ALU.add)
                nc.vector.scalar_tensor_tensor(wv[:, h, 256:384], ps[:, b1, P:256], cols[:, 2, 12 + h:13 + h], mT[:, 0:P],
                                               ALU.add, ALU.add)
                nc.vector.tensor_scalar(wv[0:META, h, 384:640], ps[0:META, b1, 0:256], cols[0:META, 0, 12 + h:13 + h], None,
                                        ALU.add).then_inc(mw_ok, 1)

            def weighted(h):
                dve.wait_ge(mexp_ok, h + 1)
                b0 = 2 * (h % 2)
                nc.vector.scalar_tensor_tensor(stmv[:, h, 0:384], ps[:, b0, 0:384], MD ** -0.5, wv[:, h, 0:384], ALU.mult, ALU.mult)
                nc.vector.scalar_tensor_tensor(stmv[0:META, h, 384:640], ps[0:META, b0 + 1, 256:512], MD ** -0.5,
                                               wv[0:META, h, 384:640], ALU.mult, ALU.mult).then_inc(mst_ok, 1)

            for h in range(MH + 1):
                if h < MH:
                    weights(h)
                if h:
                    weighted(h - 1)
            dve.wait_ge(fsd_ok, 1)
            dlink(dve, nc.vector.reciprocal(fsq, fsq))
            nc.vector.scalar_tensor_tensor(fqk[:, 0:1088], fqk[:, 0:1088], par("g_fq"), fsq[:, 0:1088], ALU.mult, ALU.mult)
            nc.vector.scalar_tensor_tensor(fqk[:, 1088:2176], fqk[:, 1088:2176], par("g_fk"), fsq[:, 1088:2176], ALU.mult,
                                           ALU.mult).then_inc(fn_ok, 1)
            dve.wait_ge(mnum_done, MH)
            dve.wait_ge(em_ok, 1)
            for sign, other in ((-1.0, em), (1.0, dn)):
                for b in range(2):
                    last = nc.vector.scalar_tensor_tensor(dn[:, b * 512:(b + 1) * 512], ps[:, 6 + b, :], sign,
                                                          other[:, b * 512:(b + 1) * 512], ALU.mult, ALU.max)
                dlink(dve, last)
            dlink(dve, nc.vector.reciprocal(dn, dn))
            for b in range(2):
                last = nc.vector.tensor_tensor(hn[:, b * 512:(b + 1) * 512], ps[:, 4 + b, :], dn[:, b * 512:(b + 1) * 512], ALU.mult)
            last.then_inc(hn_ok, 1)
            dve.wait_ge(hss_done, 1)
            for b in range(2):
                last = nc.vector.tensor_scalar(dn[:, b * 512:(b + 1) * 512], ps[:, 2 + b, :], 1.0 / MD, EPS, ALU.mult, ALU.add)
            last.then_inc(hvar_ok, 1)
            dve.wait_ge(hsd_ok, 1)
            dlink(dve, nc.vector.reciprocal(dn, dn))
            for h in range(MH):
                c = slice(h * 256, (h + 1) * 256)
                last = nc.vector.scalar_tensor_tensor(hn[:, c], hn[:, c], par("g_m")[:, h:h + 1], dn[:, c], ALU.mult, ALU.mult)
            dlink(dve, last)
            nc.vector.tensor_tensor(v3(y2T, SEQ)[:, 0:MH, :], v3(hn, SEQ), v3(mo, L2)[:, :, META:L2], ALU.mult).then_inc(y2_ok, 1)
            sfxv = v3(sfx, 512)
            m2 = v3(con("mask2"), L2)

            def flogits(u):
                dve.wait_ge(s_done, NH + u + 1)
                if u >= 2:
                    dve.wait_ge(pt_done, NH + u - 1)
                b0, b1, c = 2 * (u % 2), 2 * (u % 2) + 1, 8 * (u % 2)
                nc.vector.scalar_tensor_tensor(bfx[:, 0:L2], ps[:, b0, 0:L2], cols[:, 2, 4 + u:5 + u], m2[:, 1, :], ALU.add, ALU.add)
                dlink(dve, nc.vector.scalar_tensor_tensor(bfx[:, L2:416], ps[:, b0, 0:META + P], cols[:, 1, 4 + u:5 + u],
                                                          m2[:, 0, 0:META + P], ALU.add, ALU.add))
                a = sfxv[:, u % 2, 0:416]
                dlink(dve, nc.vector.scalar_tensor_tensor(a, ps[:, b1, 0:416], FD ** -0.5, bfx[:, 0:416], ALU.mult, ALU.add))
                nc.vector.tensor_reduce(stat[:, 32 + c:33 + c], a[:, 0:L2], AX.X, ALU.max, negate=True)
                nc.vector.tensor_reduce(stat[:, 33 + c:34 + c], a[:, L2:416], AX.X, ALU.max, negate=True).then_inc(max_ok, 1)

            def fprobs(u):
                c = 8 * (u % 2)
                dve.wait_ge(exp_ok, NH + u + 1)
                dlink(dve, nc.vector.reciprocal(tmp[:, 0:2], stat[:, 34 + c:36 + c]))
                a = sfxv[:, u % 2, 0:L2]
                nc.vector.tensor_scalar(a, a, tmp[:, 0:1], None, ALU.mult)
                a = sfxv[:, u % 2, L2:416]
                nc.vector.tensor_scalar(a, a, tmp[:, 1:2], None, ALU.mult).then_inc(p_ok, 1)

            for u in range(FH + 2):
                if u < FH:
                    flogits(u)
                if 1 <= u <= FH:
                    fprobs(u - 1)
                if u >= 3 and u % 2 == 1:
                    heads_out((u - 3) // 2, NH + u - 1, v3(y2T, SEQ)[:, 4 + (u - 3) // 2, :], 0)
            dve_residual(dve, "mix_o")

            dve_norm(dve, "ffn2")
            dve_transpose(dve, "ffn2", own_cols, [(xpT, "g_ffn2")])
            dve_input(dve, "ffn2", peer_x_hi, peer_x_lo)
            for j in range(2 * PH):
                bank = fm_take(dve)
                nc.vector.tensor_copy(v3(qhT, SEQ)[:, j, :], ps[:, bank, 0:SEQ]).then_inc(fm_free, 1)
            scv = scs.rearrange("p (l n) -> p l n", n=NKEY)
            NL = TT * 2 * PH
            tvv, tiv = v3(tv, PK), v3(ti.bitcast(U32), PK)
            dve.wait_ge(sc_ok, 4)

            def top16(lists, src, vals, idxs):
                for part in range(2):
                    for l in range(lists):
                        last = nc.vector.max(vals[:, l, 8 * part:8 * part + 8], src[:, l, :])
                    dlink(dve, last)
                    for l in range(lists):
                        last = nc.vector.max_index(idxs[:, l, 8 * part:8 * part + 8], vals[:, l, 8 * part:8 * part + 8], src[:, l, :])
                    dlink(dve, last)
                    if part == 0:
                        for l in range(lists):
                            last = nc.vector.match_replace(src[:, l, :], vals[:, l, 0:8], src[:, l, :], -3.0e38)
                        dlink(dve, last)

            top16(NL, scv, tvv, tiv)
            NT = TT * PH
            pairs = tv.rearrange("p (l h k) -> p l h k", h=2, k=PK)
            candv = v3(eq, PK * PK)
            for l in range(NT):
                last = nc.vector.tensor_tensor(candv[:, l, :].rearrange("p (a b) -> p a b", b=PK),
                                               bcast(pairs[:, l, 0, :].unsqueeze(2), PK, PK),
                                               bcast(pairs[:, l, 1, :].unsqueeze(1), PK, PK), ALU.add)
            dlink(dve, last)
            topv, topiv = v3(tops, PK), v3(topi.bitcast(U32), PK)
            top16(NT, candv, topv, topiv)
            dlink(dve, nc.vector.tensor_copy(tmp[:, 32:32 + NT], topv[:, :, 0]))
            nc.vector.tensor_tensor(topv, topv, bcast(tmp[:, 32:32 + NT].unsqueeze(2), NT, PK), ALU.subtract).then_inc(gsub_ok, 1)
            pau, pbu = pa.bitcast(U32), pb.bitcast(U32)
            nc.vector.tensor_scalar(pau, topi.bitcast(U32), 4, None, ALU.logical_shift_right)
            dlink(dve, nc.vector.tensor_scalar(pbu, topi.bitcast(U32), 15, None, ALU.bitwise_and))
            ixf = ix.rearrange("p (a n) -> p a n", a=4)
            ident_i = v3(cand, PK)
            nc.vector.tensor_copy(cand, ti.bitcast(U32))
            nc.vector.tensor_copy(tmp2[:, 0:256], pau)
            dlink(dve, nc.vector.tensor_copy(tmp2[:, 256:512], pbu))
            kf = cand.rearrange("p (l h k) -> p l h k", h=2, k=PK)
            eqv = eq.rearrange("p (l k c) -> p l k c", k=PK, c=PK)
            io = bcast(iota[:, 0:PK].unsqueeze(1).unsqueeze(1), NT, PK, PK)
            for a in range(2):
                place = tmp2[:, 256 * a:256 * (a + 1)].rearrange("p (l k) -> p l k", k=PK)
                dlink(dve, nc.vector.tensor_tensor(eqv, bcast(place.unsqueeze(3), NT, PK, PK), io, ALU.is_equal))
                dlink(dve, nc.vector.tensor_tensor(eqv, eqv, bcast(kf[:, :, a, :].unsqueeze(2), NT, PK, PK), ALU.mult))
                dlink(dve, nc.vector.tensor_reduce(ixf[:, a, :], eqv, AX.X, ALU.add))
            dve.wait_ge(gexp_ok, 1)
            dlink(dve, nc.vector.tensor_reduce(tmp[:, 0:NT], topv, AX.X, ALU.add))
            dlink(dve, nc.vector.reciprocal(tmp[:, 16:16 + NT], tmp[:, 0:NT]))
            nc.vector.tensor_tensor(ixf[:, 2, :].rearrange("p (l k) -> p l k", k=PK), topv,
                                    bcast(tmp[:, 16:16 + NT].unsqueeze(2), NT, PK), ALU.mult).then_inc(rt_ok, 1)
            dve.wait_ge(rt_done, 1)
            nc.vector.tensor_copy(route[:, 0:2, :], v3(ps[:, 6, :], SEQ))
            nc.vector.tensor_copy(route[:, 2, :], ps[:, 7, 0:SEQ]).then_inc(route_ok, 1)
            dve.wait_ge(route_ok, 1)
            d0 = cnt["dve"]

            def onehots(b, t, need, step):
                if need is not None:
                    dve.wait_ge(g_done, need)
                nc.vector.tensor_tensor(onehot[:, b, 0], bcast(iota.unsqueeze(1), 4, P),
                                        bcast(route[:, 0, bass.ds(t, 4)].unsqueeze(2), 4, P), ALU.is_equal)
                nc.vector.tensor_tensor(onehot[:, b, 1], bcast(iota.unsqueeze(1), 4, P),
                                        bcast(route[:, 1, bass.ds(t, 4)].unsqueeze(2), 4, P), ALU.is_equal).then_inc(dve_step, 1)
                dve.wait_ge(dve_step, step)
                nc.vector.tensor_tensor(onehot[:, b, 1], onehot[:, b, 1],
                                        bcast(route[:, 2, bass.ds(t, 4)].unsqueeze(2), 4, P), ALU.mult).then_inc(oh_ok, 1)

            for b in range(2):
                onehots(b, 4 * b, None, d0 + b + 1)
            with dve.Fori(1, SEQ // 8) as i:
                for b in range(2):
                    onehots(b, i * 8 + 4 * b, i * 2 + (b - 1), i * 2 + (d0 + b + 1))
            cnt["dve"] = d0 + SEQ // 4

            def gated(par_, j, need, step):
                g = gbuf[:, par_, :]
                dve.wait_ge(gelu_ok, need)
                nc.vector.tensor_tensor(g, g, gates_j[:, j, :], ALU.mult).then_inc(dve_step, 1)
                dve.wait_ge(dve_step, step + 1)
                split_hidden(dve, g, par_, step + 2, ph_ok)

            dve_ahead("peer")
            dve.wait_ge(g_ok, 2 + SEQ // 4)
            d0 = cnt["dve"]
            gated(0, 0, 1, d0)
            split_lo(dve, "peer", HI)
            with dve.Fori(0, (NKEY - 2) // 6) as i:
                for j in range(1, 7):
                    gated(j % 2, i * 6 + j, i * 6 + (j + 1), i * 12 + (d0 + 2 * j))
                    for tile in (2 * j - 1 + HI, 2 * j + HI):
                        split_lo(dve, "peer", tile, i, 2)
            j = NKEY - 1
            gated(j % 2, j, j + 1, d0 + 2 * j)
            rows_wait(dve, "peer")
            for t in range(TT):
                for half in range(2):
                    part = x[:, t, half * 512:(half + 1) * 512]
                    last = nc.vector.tensor_tensor(part, ps[:, ROWB[t][half], :], part, ALU.add)
                last.then_inc(fin_ok, 1)


def column_tiles(w, dst):
    k, n = w.shape
    dst[...] = w.reshape(k // P, P, n // P, P).transpose(2, 1, 0, 3).reshape(n // P, P, -1)


def pack_stream(a):
    plan, total = stream_plan()
    out = np.empty((total, P, D), np.float32)

    def part(name):
        at, n = plan[name]
        return out[at:at + n]

    w = a["gla_w_in"][0]
    column_tiles(w[:, 0:512], part("gla_q"))
    column_tiles(w[:, 512:1024], part("gla_k"))
    part("gla_v")[...] = w[:, 1024:2048].reshape(KC, P, D)
    part("gla_r")[...] = w[:, 2048:3072].reshape(KC, P, D)
    part("gla_o")[...] = a["gla_w_o"][0].reshape(KC, P, D)
    for layer in range(2):
        dst = part(f"ffn{layer}")
        up, down = a["ffn_w_up"][layer], a["ffn_w_down"][layer].reshape(FT, P, D)
        cols = np.empty((2 * FT, P, D), np.float32)
        column_tiles(up, cols)
        dst[0], dst[1] = cols[0], cols[FT]
        for f in range(1, FT):
            dst[3 * f - 1], dst[3 * f], dst[3 * f + 1] = cols[f], cols[FT + f], down[f - 1]
        dst[3 * FT - 1] = down[FT - 1]
    w = a["nsa_w_kv"]
    column_tiles(w[:, 0:512], part("nsa_raw"))
    column_tiles(np.concatenate([w[:, 512:768], w[:, 1024:1280]], 1), part("nsa_rot_k"))
    v = np.concatenate([w[:, 768:1024], w[:, 1280:1536]], 1)
    part("nsa_v")[...] = v.reshape(4, 2, P, 512).transpose(0, 2, 1, 3).reshape(4, P, D)
    w = a["nsa_w_in"][0][:, 0:D].reshape(D, 2, 2, NG, ND).transpose(0, 1, 3, 2, 4).reshape(D, D)
    column_tiles(w, part("nsa_q"))
    part("nsa_o")[...] = a["nsa_w_o"][0].reshape(2, 2, NG, ND, D).transpose(0, 2, 1, 3, 4).reshape(KC, P, D)
    for name, key in (("cmp_k", "cmp_k_w1"), ("cmp_v", "cmp_v_w1")):
        part(name)[...] = a[key].reshape(4, 4, P, CHID).transpose(0, 2, 1, 3).reshape(4, P, D)
    w = a["w_in_2"][0]
    column_tiles(w[:, 0:512], part("mix_q"))
    column_tiles(w[:, 512:1024], part("mix_k"))
    column_tiles(w[:, 1536:2048], part("mix_og"))
    column_tiles(w[:, 2056:2568], part("mix_fq"))
    column_tiles(w[:, 2568:3080], part("mix_fk"))
    part("mix_v")[:, :, 0:512] = w[:, 1024:1536].reshape(KC, P, 512)
    part("mix_v")[:, :, 512:1024] = w[:, 3080:3592].reshape(KC, P, 512)
    part("mix_o")[...] = a["w_out_2"][0].reshape(KC, P, D)
    column_tiles(a["peer_query_2"][0], part("peer_q"))
    dst = part("peer")
    u = a["peer_u_2"][0].reshape(NKEY, NKEY, KC, P).transpose(1, 3, 2, 0).reshape(NKEY, P, D)
    v = a["peer_v_2"][0].reshape(NKEY, NKEY, D).transpose(1, 0, 2)
    dst[0], dst[1::2][:NKEY - 1] = u[0], u[1:]
    dst[2::2], dst[2 * NKEY - 1] = v[:NKEY - 1], v[NKEY - 1]
    return out


def pack_params(a):
    plan, width = param_plan()
    out = np.zeros((P, width), np.float32)

    def put(name, v, row=0):
        at, w = plan[name]
        v = v.reshape(v.shape[0], -1)
        out[row:row + v.shape[0], at:at + v.shape[1]] = v

    def rows(v):
        return v.reshape(-1, P).T

    for name, v in (("g_mix0", a["norm_mix"][0]), ("g_ffn0", a["norm_ffn"][0]), ("g_kv", a["kv_norm"]),
                    ("g_mix1", a["norm_mix"][1]), ("g_ffn1", a["norm_ffn"][1]), ("g_mix2", a["norm_mix_2"][0]),
                    ("g_ffn2", a["norm_ffn_2"][0]), ("g_gla", a["gla_norm"][0]), ("b_alpha", a["gla_b_alpha"][0]),
                    ("g_m", a["m_out_norm_2"][0])):
        put(name, rows(v))
    for layer in range(2):
        taps = a["ffn_conv_w"][layer].reshape(3, 2, FT, P)
        bias = a["ffn_conv_b"][layer].reshape(1, 2, FT, P)
        put(f"conv{layer}", np.concatenate([taps, bias], 0).transpose(3, 2, 1, 0))
    put("conv_m", a["conv_qk_2"][0].reshape(MCONV, 2 * MH, P).transpose(2, 1, 0))
    put("g_fq", np.concatenate([a["f_q_norm_2"][0]] * 2)[:, None])
    put("g_fk", np.concatenate([a["f_k_norm_2"][0]] * 2)[:, None])
    put("b_forget", np.concatenate([a["b_fgate_m_2"][0], a["b_fgate_f_2"][0]])[:, None])
    put("b_input", a["b_igate_2"][0][:, None], row=32)
    put("pe_k", a["cmp_pe_k"].reshape(CB // 2, P).T)
    put("pe_v", a["cmp_pe_v"].reshape(CB // 2, P).T)
    w2 = a["cmp_k_w2"].reshape(2, P, ND).transpose(1, 0, 2)
    put("w2_k", np.concatenate([w2, w2], 2))
    put("w2_v", a["cmp_v_w2"].reshape(2, P, ND).transpose(1, 0, 2))

    def chunks(w):
        return w.reshape(KC, P, -1).transpose(1, 0, 2)

    put("w_alow", chunks(a["gla_w_in"][0][:, 3072:3088]))
    put("w_aup", a["gla_w_alpha_up"][0])
    put("w_gates", chunks(a["nsa_w_in"][0][:, D:D + 3 * NH]))
    g = np.zeros((D, 36), np.float32)
    w = a["w_in_2"][0]
    g[:, 0:4], g[:, 4:12], g[:, 32:36] = w[:, 2052:2056], w[:, 3592:3600], w[:, 2048:2052]
    put("w_gates2", chunks(g))
    return out


def kernel(**inputs):
    import concourse.bacc as bacc
    from concourse.bass_utils import run_bass_kernel_spmd

    a = {k: np.asarray(v) for k, v in inputs.items()}
    arrays = {
        "stream": pack_stream(a),
        "params": pack_params(a),
        "consts": constants(),
        "keys": np.ascontiguousarray(a["peer_sub_keys_2"][0].reshape(2 * PH, NKEY, PQ).transpose(2, 0, 1)),
        "g_final": np.ascontiguousarray(a["norm_final"]),
        "x_in": np.ascontiguousarray(a["x"][0]),
        "meta_in": np.ascontiguousarray(a["meta_tokens_2"]),
    }
    nc = bacc.Bacc("TRN2", target_bir_lowering=False, num_devices=1)
    args = [nc.dram_tensor(n, v.shape, F32, kind="ExternalInput").ap() for n, v in arrays.items()]
    out = nc.dram_tensor("out", (SEQ, D), F32, kind="ExternalOutput").ap()
    build(nc, *args, out)
    r = run_bass_kernel_spmd(nc, [arrays], core_ids=[0])
    return r.results[0]["out"].reshape(1, SEQ, D)
```

```python
from contextlib import ExitStack

import numpy as np
import concourse.bass as bass
from concourse import mybir

F32 = mybir.dt.float32
F32R = mybir.dt.float32r
U32 = mybir.dt.uint32
ACT = mybir.ActivationFunctionType
ALU = mybir.AluOpType
AX = mybir.AxisListType

P = 128
D = 1024
KC = D // P
SEQ = 256
TT = SEQ // P
META = 16
L2 = SEQ + META
EPS = 1e-6
NEG = -1e30

GH, GDK, GDV, GC, GSUB = 4, 128, 256, 64, 16
GTAU = 16.0
GRANK = 16
CLAMP = 60.0
NCH = SEQ // GC

NH, NKV, NG, ND = 16, 4, 4, 64
CB, CS = 32, 16
NCMP = (SEQ - CB) // CS + 1
CHID = 4 * ND

FF = 2816
FT = FF // P

MH, MD = 4, 128
FH, FD = 8, 64
MCONV = 4

PH, PK, PQ = 8, 16, 128
NKEY = 128

RING = 6
HI = 3


def stream_plan():
    plan, at = {}, 0
    def add(name, count):
        nonlocal at
        plan[name] = (at, count)
        at += count
    add("gla_q", 4), add("gla_k", 4), add("gla_v", 8), add("gla_r", 8), add("gla_o", 8)
    add("ffn0", 3 * FT)
    add("nsa_raw", 4), add("nsa_rot_k", 4), add("nsa_q", 8), add("nsa_v", 4), add("cmp_k", 4), add("cmp_v", 4)
    add("nsa_o", 8)
    add("ffn1", 3 * FT)
    add("mix_q", 4), add("mix_k", 4), add("mix_og", 4), add("mix_fq", 4), add("mix_fk", 4), add("mix_v", 8)
    add("mix_o", 8)
    add("peer_q", 2 * PH)
    add("peer_u", NKEY), add("peer_v", NKEY)
    return plan, at


def param_plan():
    plan, at = {}, 0
    for name, width in (
        ("g_mix0", KC), ("g_ffn0", KC), ("g_kv", KC), ("g_mix1", KC), ("g_ffn1", KC), ("g_mix2", KC), ("g_ffn2", KC),
        ("g_gla", KC), ("b_alpha", GH), ("conv0", 2 * FT * 4), ("conv1", 2 * FT * 4), ("conv_m", 2 * MH * MCONV),
        ("g_m", MH), ("g_fq", 1), ("g_fk", 1), ("b_forget", 1), ("b_input", 1), ("pe_k", CB // 2), ("pe_v", CB // 2),
        ("w2_k", 2 * P), ("w2_v", 2 * ND), ("w_alow", KC * GRANK), ("w_aup", GH * GDK), ("w_gates", KC * 3 * NH),
        ("w_gates2", KC * 36),
    ):
        plan[name] = (at, width)
        at += width
    return plan, at


def const_plan():
    plan, at = {}, 0
    for name, width in (
        ("ident", P), ("ones", P), ("ones64", P), ("turn", P), ("cos", SEQ), ("sin", SEQ), ("tril", GC),
        ("reset", SEQ), ("mask1", SEQ), ("mask0", P), ("cmask", TT * NCMP), ("cvalid", TT), ("mask2", TT * L2),
        ("maskT", SEQ), ("iota", P),
    ):
        plan[name] = (at, width)
        at += width
    return plan, at


def constants():
    plan, width = const_plan()
    c = np.zeros((P, width), np.float32)
    def put(name, a):
        at, w = plan[name]
        c[: a.shape[0], at:at + w] = a.reshape(a.shape[0], -1)
    i = np.arange(P)
    put("ident", np.eye(P))
    put("ones", np.ones((P, P)))
    put("ones64", (i[:, None] // 64 == i[None, :] // 64).astype(np.float32))
    turn = np.zeros((P, P))
    for b in (0, 64):
        for d in range(32):
            turn[b + 32 + d, b + d] = -1.0
            turn[b + d, b + 32 + d] = 1.0
    put("turn", turn)
    half = ND // 2
    inv = np.float32(10000.0) ** (-np.arange(half, dtype=np.float32) / np.float32(half))
    ang = np.arange(SEQ, dtype=np.float32)[None, :] * inv[:, None]
    put("cos", np.tile(np.cos(ang), (4, 1)))
    put("sin", np.tile(np.sin(ang), (4, 1)))
    put("tril", (i[:, None] % GC <= np.arange(GC)[None, :]).astype(np.float32))
    put("reset", np.tile((np.arange(SEQ) % GC != 0).astype(np.float32), (P, 1)))
    put("mask1", np.where(np.arange(SEQ)[None, :] <= i[:, None] + P, 0.0, NEG))
    put("mask0", np.where(i[None, :] <= i[:, None], 0.0, NEG))
    pos = i[:, None] + P * np.arange(TT)[None, :]
    end = np.arange(NCMP) * CS + CB - 1
    put("cmask", np.where(end[None, None, :] <= pos[:, :, None], 0.0, NEG))
    put("cvalid", (pos >= CB - 1).astype(np.float32))
    put("mask2", np.where(np.arange(L2)[None, None, :] <= META + pos[:, :, None], 0.0, NEG))
    put("maskT", np.where(i[:, None] <= np.arange(SEQ)[None, :], 0.0, NEG))
    put("iota", np.tile(np.arange(P, dtype=np.float32), (P, 1)))
    return c


def build(nc, stream, params, consts, keys, g_final, x_in, meta_in, out):
    plan, n_tiles = stream_plan()
    pplan, pwidth = param_plan()
    cplan, cwidth = const_plan()
    ctx = ExitStack()
    with ctx:
        slab_base = nc.sbuf_base
        slab_bytes = nc.sbuf_bytes_remaining // 32 * 32 - 32
        ctx.enter_context(nc.sbuf_tensor("slab", [P, slab_bytes // 4], F32))
        place = {"end": -(-slab_base // 32) * 32}

        def sb(name, shape, dt=F32):
            place[name] = place["end"]
            place["end"] += -(-4 * int(np.prod(shape[1:])) // 32) * 32
            assert place["end"] <= slab_base + slab_bytes, name
            return nc.alloc_sbuf_tensor_at(name, shape, dt, offset=place[name])

        def over(name, shape, host, at, dt=F32R):
            return nc.alloc_sbuf_tensor_at(name, shape, dt, offset=place[host] + 4 * at)

        def sem(name):
            return ctx.enter_context(nc.semaphore(name))

        ring = sb("ring", [P, RING, D])
        prm = sb("prm", [P, pwidth])
        cst = sb("cst", [P, cwidth])
        x = sb("x", [P, TT, D])
        xn = sb("xn", [P, KC, L2])
        hT_hi, hT_lo = sb("hT_hi", [P, 2, SEQ], F32R), sb("hT_lo", [P, 2, SEQ], F32R)
        stat = sb("stat", [P, 64])
        arena = sb("arena", [P, NKEY * SEQ])
        ps = ctx.enter_context(nc.psum_tensor("ps", [P, 8, 512], F32))

        def par(name):
            at, w = pplan[name]
            return prm[:, at:at + w]

        def con(name):
            at, w = cplan[name]
            return cst[:, at:at + w]

        def carve(start, *sizes):
            views = []
            for n in sizes:
                views.append(arena[:, start:start + n])
                start += n
            assert start <= NKEY * SEQ, start
            return views, start

        NGAIN = pplan["b_alpha"][0]
        ident, iota = con("ident"), con("iota")

        (qT, kT, z, dec, bcum, qx, qb, ka, kd, kdT, vtok, rtok, att, state, ytok, yT), gla_end = carve(
            0, 1024, 1024, 1024, 1024, 1024, 1024, 1024, 4096, 1024, 1024, 2048, 2048, 512, 2048, 2048, 2048)
        (xs,), _ = carve(NKEY * SEQ - 3 * D, 3 * D)
        xs = xs.rearrange("p (t n) -> p t n", n=D)
        (cgate, cval, sgate, hfull), _ = carve(0, SEQ, SEQ, SEQ, SEQ)
        ring_lo = over("ring_lo", [P, RING, D], "ring", 0)
        ffn_hi = over("ffn_hi", [P, HI, D], "arena", 6144)
        ffn_w_hi = [ffn_hi[:, s, :] for s in range(HI)]
        ffn_x_hi = over("ffn_x_hi", [P, KC, SEQ], "arena", 9216)
        ffn_x_lo = over("ffn_x_lo", [P, KC, SEQ], "arena", 11264)
        (xkv, cmpraw, raw, rot, shifted, blk, hid, hidT, hvr, kcT, vcr, pc, pcT, vsw, gs, sc_a, sc_b, pt, csc), nsa_end = carve(
            0, 2048, 1024, 3072, 3072, 2048, 1920, 512, 240, 1024, 64, 256, 1024, 1024, 1024, 96, 1024, 512, 1536, 512)
        oT = xkv
        (mqk, mo, fqk, fsq, v2, lin, wts, stm, sfx, bfx, ptf, y2T), _ = carve(
            0, 2176, 1088, 2176, 2176, 3072, 9 * L2, 2560, 2560, 1024, 448, 1280, 2048)
        (em, dn, hn), _ = carve(4 * 2176 - 1088 + 3072 + 9 * L2, 1024, 1024, 1024)
        (gfin, xm), _ = carve(NKEY * SEQ - 5 * D, D, D)
        xm = xm[0:META, :]
        acts = arena[:, :].rearrange("p (j t) -> p j t", t=SEQ)
        route = sb("route", [P, 3, SEQ])
        onehot = sb("onehot", [P, 2, 2, 4, P])
        (qhT, keysT, scs, tv, ti, cand, tops, topi, pa, pb, ix, tmp2, eq), _ = carve(
            NKEY * SEQ - 18432, 4096, 2048, 4096, 512, 512, 512, 256, 256, 256, 256, 1024, 512, 4096)
        keysT = keysT.rearrange("p (i n) -> p i n", n=NKEY)
        tmp = sb("tmp", [P, SEQ])
        colb = sb("colb", [P, 48])
        xpT = xn
        early_hi, early_hi_c = over("early_hi", [P, 2, D], "onehot", 0), over("early_hi_c", [P, D], "hT_hi", 0)
        early_w_hi = [early_hi[:, 0, :], early_hi[:, 1, :], early_hi_c[:, :]]
        assert gla_end + 4096 <= NKEY * SEQ - 3 * D
        gla_x_hi = over("gla_x_hi", [P, KC, SEQ], "arena", gla_end)
        gla_x_lo = over("gla_x_lo", [P, KC, SEQ], "arena", gla_end + 2048)
        assert nsa_end + 4 * KC * SEQ <= NKEY * SEQ
        kv_x_hi, kv_x_lo, nsa_x_hi, nsa_x_lo = (over(name, [P, KC, SEQ], "arena", nsa_end + i * KC * SEQ) for i, name in
                                                enumerate(("kv_x_hi", "kv_x_lo", "nsa_x_hi", "nsa_x_lo")))
        mix_x_hi = over("mix_x_hi", [P, KC, L2], "arena", NKEY * SEQ - 2 * KC * L2)
        mix_x_lo = over("mix_x_lo", [P, KC, L2], "arena", NKEY * SEQ - KC * L2)
        gla_y_hi, gla_y_lo = over("gla_y_hi", [P, KC, SEQ], "arena", 0), over("gla_y_lo", [P, KC, SEQ], "arena", 2048)
        peer_x_hi = over("peer_x_hi", [P, KC, SEQ], "prm", 0)
        peer_x_lo = over("peer_x_lo", [P, KC, SEQ], "cst", P)
        assert pwidth >= KC * SEQ and P + KC * SEQ <= cplan["iota"][0]
        peer_hi_a, peer_hi_u = over("peer_hi_a", [P, 2, D], "xn", 0), over("peer_hi_u", [P, D], "hT_hi", 0)
        peer_hi_v = over("peer_hi_v", [P, D], "onehot", 0)
        assert place["hT_lo"] == place["hT_hi"] + 8 * SEQ
        onehot_c = over("onehot_c", [P, 2, 2, 4, P], "prm", 0, F32)
        OH = 4
        oh_rows = [onehot[:, 0], onehot[:, 1], onehot_c[:, 0], onehot_c[:, 1]]
        OHB = (6, 7, 2, 3)
        u_w_hi = [peer_hi_u[:, :], peer_hi_a[:, 0, :], peer_hi_a[:, 1, :]]
        q_w_hi = [u_w_hi[(i - 2 * PH) % HI] for i in range(HI)]
        v_w_hi = [peer_hi_a[:, 1, :], peer_hi_a[:, 0, :], peer_hi_v[:, :]]

        w_loaded = [sem(f"w_loaded{s}") for s in range(RING)]
        tile_done = sem("tile_done")
        prm_in, x_in_sem, meta_sem, fin_sem, keys_in = (sem(n) for n in ("prm_in", "x_in", "meta_in", "gfin_in", "keys_in"))
        first_in = sem("first_in")
        x_ready = sem("x_ready")
        sq_done, var_done, sd_done = sem("sq_done"), sem("var_done"), sem("sd_done")
        tok_ready = sem("tok_ready")
        t_done = sem("t_done")
        t_copied = sem("t_copied")
        small_done, fm_free = sem("small_done"), sem("fm_free")
        dve_step, act_step = sem("dve_step"), sem("act_step")
        act_rows = sem("act_rows")
        rot_done, rot_free = sem("rot_done"), sem("rot_free")
        hi_ok, lo_ok = sem("hi_ok"), sem("lo_ok")
        xhi_ok, xlo_ok = sem("xhi_ok"), sem("xlo_ok")

        cnt = {"dve": 0, "act": 0}

        def dlink(dve, ins):
            cnt["dve"] += 1
            ins.then_inc(dve_step, 1)
            dve.wait_ge(dve_step, cnt["dve"])

        def alink(act, ins):
            cnt["act"] += 1
            ins.then_inc(act_step, 1)
            act.wait_ge(act_step, cnt["act"])

        def v3(ap, n):
            return ap.rearrange("p (a n) -> p a n", n=n)

        def bcast(ap, *shape):
            return ap.broadcast_to([ap.shape[0], *shape])

        TILES = {"mix0": 2, "ffn0": 2, "mix1": 2, "ffn1": 2, "final": 2, "mix2": 3, "ffn2": 2}
        NBASE, XNEED, base, xr = {}, {}, 0, 0
        for name, n in TILES.items():
            NBASE[name] = base
            base += n
        XNEED = {"mix0": 0, "ffn0": 2, "mix1": 4, "ffn1": 6, "final": 8, "mix2": 10, "ffn2": 12}
        NIDX = {name: i for i, name in enumerate(TILES)}
        TST, base = {}, 0
        for name, n in (("mix0", 2), ("gla", 2), ("ffn0", 2), ("mix1", 2), ("ffn1", 2), ("mix2", 3), ("ffn2", 2)):
            TST[name] = (base, n)
            base += n

        def norm_tiles(name):
            own = [(x[:, t, :], P) for t in range(TT)]
            return [(xm, META)] + own if name == "mix2" else own

        def act_norm(act, name):
            if XNEED[name]:
                act.wait_ge(x_ready, XNEED[name])
            else:
                act.wait_ge(x_in_sem, 16)
            if name == "mix2":
                act.wait_ge(meta_sem, 16)
            for i, (src, rows) in enumerate(norm_tiles(name)):
                nc.scalar.activation(xs[0:rows, i, :], src, ACT.Square,
                                     accum_out=stat[0:rows, i:i + 1]).then_inc(sq_done, 1)
            act.wait_ge(var_done, NIDX[name] + 1)
            n = TILES[name]
            nc.scalar.activation(stat[:, 16:16 + n], stat[:, 8:8 + n], ACT.Sqrt).then_inc(sd_done, 1)

        def dve_norm(dve, name, gain=None):
            n = TILES[name]
            dve.wait_ge(sq_done, NBASE[name] + n)
            nc.vector.tensor_scalar(stat[:, 8:8 + n], stat[:, 0:n], 1.0 / D, EPS, ALU.mult, ALU.add).then_inc(var_done, 1)
            dve.wait_ge(sd_done, NIDX[name] + 1)
            dlink(dve, nc.vector.reciprocal(stat[:, 24:24 + n], stat[:, 16:16 + n]))
            for i, (src, rows) in enumerate(norm_tiles(name)):
                if gain is None:
                    nc.vector.tensor_scalar(xs[0:rows, i, :], src, stat[0:rows, 24 + i:25 + i], None,
                                            ALU.mult).then_inc(tok_ready, 1)
                else:
                    nc.vector.scalar_tensor_tensor(src, src, stat[0:rows, 24 + i:25 + i], gain, ALU.mult,
                                                   ALU.mult).then_inc(x_ready, 1)

        def pe_transpose(pe, name, src, rows_of):
            first, n = TST[name]
            for i in range(n):
                pe.wait_ge(tok_ready, first + i + 1)
                rows = rows_of(i)
                for half in range(2):
                    k = 2 * (first + i) + half
                    if k >= 2:
                        pe.wait_ge(t_copied, k - 1)
                    for c in range(4):
                        last = nc.tensor.transpose(ps[:, 6 + k % 2, c * rows:(c + 1) * rows],
                                                   src[0:rows, i, (4 * half + c) * P:(4 * half + c + 1) * P],
                                                   ident[0:rows, 0:rows])
                    last.then_inc(t_done, 1)

        def dve_transpose(dve, name, cols_of, outs):
            first, n = TST[name]
            for i in range(n):
                c0, rows = cols_of(i)
                for half in range(2):
                    k = 2 * (first + i) + half
                    dve.wait_ge(t_done, k + 1)
                    got = ps[:, 6 + k % 2, 0:4 * rows].rearrange("p (c t) -> p c t", c=4)
                    for o, (dst, gain) in enumerate(outs):
                        last = nc.vector.tensor_tensor(
                            dst[:, 4 * half:4 * half + 4, c0:c0 + rows], got,
                            bcast(par(gain)[:, 4 * half:4 * half + 4].unsqueeze(2), 4, rows), ALU.mult)
                    last.then_inc(t_copied, 1)

        def t_all(name):
            first, n = TST[name]
            return 2 * (first + n)

        own_cols = lambda i: (i * P, P)
        CSB = (0, 1, 4, 5)
        meta_cols = lambda i: (0, META) if i == 0 else (META + (i - 1) * P, P)

        fmc = {"pe": 0, "dve": 0}

        def w_wait(pe, n):
            pe.wait_ge(w_loaded[n % RING], 16 * (n // RING + 1))

        def fm_begin(pe):
            k = fmc["pe"]
            fmc["pe"] += 1
            if k >= 2:
                pe.wait_ge(fm_free, k - 1)
            return k % 2

        tiles = [("tile", plan["gla_q"][0] + j) for j in range(2 * GH)]
        FM = [("small", 0)] + tiles[:2] + [("small", 1 + j) for j in range(GH)] + tiles[2:]
        FM += [("tile", plan["nsa_raw"][0] + j) for j in range(16)] + [("small", 1 + GH)]
        FM += [("tile", plan["mix_q"][0] + j) for j in range(20)]
        FM += [("tile", plan["peer_q"][0] + j) for j in range(2 * PH)]

        def fm_wait(eng, k):
            kind, n = FM[k]
            eng.wait_ge(tile_done if kind == "tile" else small_done, n + 1)

        def fm_take(dve):
            k = fmc["dve"]
            fmc["dve"] += 1
            fm_wait(dve, k)
            return k % 2

        def rows_wait(eng, name):
            first, n = plan[name]
            eng.wait_ge(tile_done, first + n)

        def pe_rows(pe, first, lhs, banks, n=KC):
            for k in range(n):
                w_wait(pe, first + k)
                for t, pair in enumerate(banks):
                    for half in range(2):
                        a = lhs(k, t)
                        last = nc.tensor.matmul(ps[0:a.shape[1], pair[half], :], a,
                                                ring[:, (first + k) % RING, half * 512:(half + 1) * 512],
                                                start=(k == 0), stop=(k == n - 1))
                last.then_inc(tile_done, 1)
            return last

        ROWB = [(2, 3), (4, 5)]

        def dve_residual(dve, name):
            rows_wait(dve, name)
            for t in range(TT):
                for half in range(2):
                    part = x[:, t, half * 512:(half + 1) * 512]
                    last = nc.vector.tensor_tensor(part, ps[:, ROWB[t][half], :], part, ALU.add)
                last.then_inc(x_ready, 1)

        plan["gla_in"] = (plan["gla_q"][0], 24)
        plan["nsa_in"] = (plan["nsa_raw"][0], 20)
        plan["mix_in"] = (plan["mix_q"][0], 28)
        SPLIT0, base = {}, 0
        W_HI = {"gla_in": early_w_hi, "gla_o": early_w_hi, "ffn0": ffn_w_hi, "nsa_in": early_w_hi, "ffn1": ffn_w_hi, "mix_in": early_w_hi,
                "peer_q": q_w_hi, "peer_u": u_w_hi, "peer_v": v_w_hi}
        for name in W_HI:
            SPLIT0[name] = base
            base += plan[name][1]
        UMID = 78
        assert UMID % RING == 0 and UMID * SEQ <= NKEY * SEQ - 18432 + 4096 + 2048

        def split_hi(act, name, tile, it=None):
            n = plan[name][0] + tile
            turn = 16 * (n // RING + 1)
            act.wait_ge(w_loaded[n % RING], turn if it is None else it * 16 + turn)
            nc.scalar.activation(W_HI[name][tile % HI], ring[:, n % RING, :], ACT.Copy).then_inc(hi_ok, 1)

        def split_lo(dve, name, tile, it=None):
            n = plan[name][0] + tile
            need = SPLIT0[name] + tile + 1
            dve.wait_ge(hi_ok, need if it is None else it * RING + need)
            nc.vector.tensor_tensor(ring_lo[:, n % RING, :], ring[:, n % RING, :], W_HI[name][tile % HI].bitcast(F32),
                                    ALU.subtract).then_inc(lo_ok, 1)

        def split_wait(pe, name, tile, it=None):
            need = SPLIT0[name] + tile + 1
            pe.wait_ge(lo_ok, need if it is None else it * RING + need)

        def split_columns(name, tile, bank, x_hi, x_lo, width=SEQ):
            n = plan[name][0] + tile
            w_hi, w_lo = v3(W_HI[name][tile % HI], P), v3(ring_lo[:, n % RING, :], P)
            for c in range(KC):
                nc.tensor.matmul(ps[:, bank, 0:width], w_hi[:, c, :], x_hi[:, c, :], start=(c == 0), stop=False)
                nc.tensor.matmul(ps[:, bank, 0:width], w_hi[:, c, :], x_lo[:, c, :], start=False, stop=False)
                last = nc.tensor.matmul(ps[:, bank, 0:width], w_lo[:, c, :], x_hi[:, c, :], start=False, stop=(c == KC - 1))
            last.then_inc(tile_done, 1)

        def split_rows(name, tile, buf, first, final):
            n = plan[name][0] + tile
            w_hi, w_lo = W_HI[name][tile % HI], ring_lo[:, n % RING, :]
            for t in range(TT):
                h_hi, h_lo = hT_hi[:, buf, t * P:(t + 1) * P], hT_lo[:, buf, t * P:(t + 1) * P]
                for a, w, st, sp_ in ((h_hi, w_hi, first, False), (h_hi, w_lo, False, False), (h_lo, w_hi, False, final)):
                    for half in range(2):
                        last = nc.tensor.matmul(ps[:, ROWB[t][half], :], a, w[:, half * 512:(half + 1) * 512],
                                                start=st, stop=sp_)
            last.then_inc(tile_done, 1)

        def split_hidden(dve, full, buf, step, done):
            nc.vector.tensor_copy(hT_hi[:, buf, :], full).then_inc(dve_step, 1)
            dve.wait_ge(dve_step, step)
            nc.vector.tensor_tensor(hT_lo[:, buf, :], full, hT_hi[:, buf, :].bitcast(F32), ALU.subtract).then_inc(done, 1)

        def pe_split_rows(pe, name, first, lhs, banks):
            for k in range(KC):
                n = plan[name][0] + first + k
                w_hi, w_lo = W_HI[name][(first + k) % HI], ring_lo[:, n % RING, :]
                split_wait(pe, name, first + k)
                for t, pair in enumerate(banks):
                    for part, w, i in ((0, w_hi, 0), (0, w_lo, 1), (1, w_hi, 2)):
                        for half in range(2):
                            a = lhs(part, k, t)
                            last = nc.tensor.matmul(ps[0:a.shape[1], pair[half], :], a, w[:, half * 512:(half + 1) * 512],
                                                    start=(k == 0 and i == 0), stop=(k == KC - 1 and i == 2))
                last.then_inc(tile_done, 1)

        def behind_hi(act, name, tiles):
            for tile in tiles:
                act.wait_ge(tile_done, plan[name][0] + tile + 1)
                split_hi(act, name, tile + HI)

        XCNT = {"mix0": 1, "gla": 2, "ffn0": 3, "kv": 4, "mix1": 5, "ffn1": 6, "mix2": 7, "ffn2": 8}

        def act_input(act, name, x_hi, src=None):
            act.wait_ge(t_copied, t_all("mix1" if name == "kv" else name))
            nc.scalar.activation(x_hi[:, :, :], xn[:, :, 0:SEQ] if src is None else src, ACT.Copy).then_inc(xhi_ok, 1)

        def dve_input(dve, name, x_hi, x_lo, src=None):
            dve.wait_ge(xhi_ok, XCNT[name])
            nc.vector.tensor_tensor(x_lo[:, :, :], xn[:, :, 0:SEQ] if src is None else src, x_hi[:, :, :].bitcast(F32),
                                    ALU.subtract).then_inc(xlo_ok, 1)

        abs_ok, ln_ok, dsub_ok, dexp_ok, dmul_ok = (sem(n) for n in ("abs_ok", "ln_ok", "dsub_ok", "dexp_ok", "dmul_ok"))
        att_done, att_ok, kdt_done, kdt_ok = (sem(n) for n in ("att_done", "att_ok", "kdt_done", "kdt_ok"))
        kv_done, state_ok, go_done, osq_ok, ovar_ok, osd_ok = (sem(n) for n in ("kv_done", "state_ok", "go_done", "osq_ok", "ovar_ok", "osd_ok"))
        c0_done, cg_done, cv_done, silu_done, h_ready = (sem(n) for n in ("c0_done", "cg_done", "cv_done", "silu_done", "h_ready"))
        shift_in, blk_ok, hid_ok, ht_done, ht_ok, kc_done, kc_ok, gate_done, gate_ok = (sem(n) for n in (
            "shift_in", "blk_ok", "hid_ok", "ht_done", "ht_ok", "kc_done", "kc_ok", "gate_done", "gate_ok"))
        cs_done, cs_ok, ce_ok, pc_ok, pct_done, pct_ok = (sem(n) for n in ("cs_done", "cs_ok", "ce_ok", "pc_ok", "pct_done", "pct_ok"))
        s_done, max_ok, exp_ok, p_ok, pt_done, pt_ok, pv_done, o_ok = (sem(n) for n in (
            "s_done", "max_ok", "exp_ok", "p_ok", "pt_done", "pt_ok", "pv_done", "o_ok"))
        mc0, msilu_ok, gab_ok, gln_ok, row_ok, col_done, col_ok = (sem(n) for n in (
            "mc0", "msilu_ok", "gab_ok", "gln_ok", "row_ok", "col_done", "col_ok"))
        fsq_ok, fss_done, fvar_ok, fsd_ok, fn_ok = (sem(n) for n in ("fsq_ok", "fss_done", "fvar_ok", "fsd_ok", "fn_ok"))
        ms_done, mw_ok, mexp_ok, mst_ok, mnum_done, mb_done, em_ok, hn_ok, hsq_ok, hss_done, hvar_ok, hsd_ok, y2_ok = (sem(n) for n in (
            "ms_done", "mw_ok", "mexp_ok", "mst_ok", "mnum_done", "mb_done", "em_ok", "hn_ok", "hsq_ok", "hss_done", "hvar_ok", "hsd_ok", "y2_ok"))
        qh_ok, sc_done, sc_ok, gsub_ok, gexp_ok, rt_ok, rt_done, route_ok, oh_ok, eq_ok, g_done, g_ok = (sem(n) for n in (
            "qh_ok", "sc_done", "sc_ok", "gsub_ok", "gexp_ok", "rt_ok", "rt_done", "route_ok", "oh_ok", "eq_ok", "g_done", "g_ok"))
        gelu_ok, ph_ok, fin_ok, out_sem = (sem(n) for n in ("gelu_ok", "ph_ok", "fin_ok", "out_sem"))
        block = ctx.enter_context(nc.Block())

        FM2 = GH * 3 + 1 + 4 + 12

        @block.sync
        def _(sp):
            for s in range(RING):
                sp.dma_start(ring[:, s, :], stream[s]).then_inc(w_loaded[s], 16)
            rounds = n_tiles // RING
            with sp.Fori(1, rounds) as i:
                for s in range(RING):
                    sp.wait_ge(tile_done, i * RING + (s + 1 - RING))
                    sp.dma_start(ring[:, s, :], stream[i * RING + s]).then_inc(w_loaded[s], 16)
            for n in range(rounds * RING, n_tiles):
                sp.wait_ge(tile_done, n + 1 - RING)
                sp.dma_start(ring[:, n % RING, :], stream[n]).then_inc(w_loaded[n % RING], 16)
            for t in range(TT):
                sp.wait_ge(fin_ok, t + 1)
                sp.dma_start(out[t * P:(t + 1) * P, :], x[:, t, :]).then_inc(out_sem, 16)
            sp.wait_ge(out_sem, 16 * TT)

        @block.tensor
        def _(pe):
            def pe_ffn(layer):
                name, h0 = f"ffn{layer}", FT * layer

                def up(tile, bank, need, it=None):
                    split_wait(pe, name, tile, it)
                    if need is not None:
                        pe.wait_ge((cg_done, cv_done)[bank], need)
                    split_columns(name, tile, bank, ffn_x_hi, ffn_x_lo)

                def down(tile, f_par, first, last_f, need, it=None):
                    split_wait(pe, name, tile, it)
                    pe.wait_ge(h_ready, need)
                    split_rows(name, tile, f_par, first, last_f)

                def pair(tile, f, it=None):
                    for s in range(2):
                        need = None
                        if it is not None:
                            need = it * 2 + (h0 + f)
                        elif h0 + f:
                            need = h0 + f
                        up(tile + s, s, need, it)

                pe.wait_ge(xlo_ok, XCNT[name])
                pair(0, 0)
                pair(2, 1)
                down(4, 0, True, False, h0 + 1)
                pair(5, 2)
                down(7, 1, False, False, h0 + 2)
                with pe.Fori(0, (FT - 4) // 2) as i:
                    pair(8, 3, i)
                    down(10, 0, False, False, i * 2 + (h0 + 3), i)
                    pair(11, 4, i)
                    down(13, 1, False, False, i * 2 + (h0 + 4), i)
                pair(8 + 3 * (FT - 4), FT - 1)
                down(10 + 3 * (FT - 4), 0, False, False, h0 + FT - 1)
                down(11 + 3 * (FT - 4), 1, False, True, h0 + FT)

            pe.wait_ge(first_in, 32)
            pe_transpose(pe, "mix0", xs, lambda i: P)
            pe.wait_ge(prm_in, 32)
            pe.wait_ge(t_copied, t_all("mix0"))
            pe.wait_ge(xlo_ok, XCNT["mix0"])
            bank = fm_begin(pe)
            wl = v3(par("w_alow"), GRANK)
            for c in range(KC):
                last = nc.tensor.matmul(ps[0:GRANK, bank, 0:SEQ], wl[:, c, :], xn[:, c, 0:SEQ],
                                        start=(c == 0), stop=(c == KC - 1))
            last.then_inc(small_done, 1)
            pe.wait_ge(xlo_ok, XCNT["mix0"])
            for h in range(2 * GH):
                if h == 2:
                    pe.wait_ge(fm_free, 1)
                    for g in range(GH):
                        bank = fm_begin(pe)
                        nc.tensor.matmul(ps[:, bank, 0:SEQ], par("w_aup")[0:GRANK, g * GDK:(g + 1) * GDK],
                                         dec[0:GRANK, 0:SEQ], start=True, stop=True).then_inc(small_done, 1)
                bank = fm_begin(pe)
                split_wait(pe, "gla_in", h)
                split_columns("gla_in", h, bank, gla_x_hi, gla_x_lo)
            own_tokens = lambda part, k, t: (gla_x_hi, gla_x_lo)[part][:, k, t * P:(t + 1) * P]
            pe_split_rows(pe, "gla_in", 8, own_tokens, ROWB)
            pe.wait_ge(fm_free, fmc["pe"])
            RB = [(6, 7), (0, 1)]
            pe_split_rows(pe, "gla_in", 16, own_tokens, RB)

            pe.wait_ge(dmul_ok, 2)
            pe.wait_ge(act_rows, 1)
            kav = ka.rearrange("p (a h t) -> p a h t", a=GC // GSUB, h=GH)
            qxv, qbv, kdv = v3(qx, SEQ), v3(qb, SEQ), v3(kd, SEQ)
            for h in range(GH):
                for c in range(NCH):
                    rows, col = 64 * (c % 2), (h * TT + c // 2) * GC
                    for a in range(GC // GSUB):
                        t0 = c * GC + a * GSUB
                        last = nc.tensor.matmul(ps[rows:rows + GC, 2, col + a * GSUB:col + (a + 1) * GSUB],
                                                kav[:, a, h, c * GC:(c + 1) * GC], qxv[:, h, t0:t0 + GSUB],
                                                start=True, stop=True)
            last.then_inc(att_done, 1)
            pe.wait_ge(dmul_ok, 3)
            for h in range(GH):
                for t in range(TT):
                    u = h * TT + t
                    last = nc.tensor.transpose(ps[:, 3 + u // 4, (u % 4) * P:(u % 4 + 1) * P],
                                               kdv[:, h, t * P:(t + 1) * P], ident)
            last.then_inc(kdt_done, 1)
            attv, vv = v3(att, GC), v3(vtok, D)
            kdTv = kdT.rearrange("p (h t k) -> p h t k", h=GH, t=TT)
            stv = state.rearrange("p (b h v) -> p b h v", b=2, h=GH)
            pe.wait_ge(att_ok, 1)
            pe.wait_ge(kdt_ok, 1)
            pe.wait_ge(act_rows, 2)
            pe.wait_ge(dmul_ok, 4)
            OB = [6, 7, 0, 1]
            for c in range(NCH):
                t, rows = c // 2, 64 * (c % 2)
                if c:
                    pe.wait_ge(state_ok, c)
                if c < NCH - 1:
                    for h in range(GH):
                        last = nc.tensor.matmul(ps[:, (2, 5)[h // 2], (h % 2) * GDV:(h % 2 + 1) * GDV],
                                                kdTv[rows:rows + GC, h, t, :], vv[rows:rows + GC, t, h * GDV:(h + 1) * GDV],
                                                start=True, stop=True)
                    last.then_inc(kv_done, 1)
                for h in range(GH):
                    o = ps[rows:rows + GC, OB[2 * t + h // 2], (h % 2) * GDV:(h % 2 + 1) * GDV]
                    last = nc.tensor.matmul(o, attv[rows:rows + GC, h * TT + t, :],
                                            vv[rows:rows + GC, t, h * GDV:(h + 1) * GDV], start=True, stop=(c == 0))
                    if c:
                        last = nc.tensor.matmul(o, qbv[:, h, c * GC:(c + 1) * GC], stv[:, c % 2, h, :],
                                                start=False, stop=True)
                last.then_inc(go_done, 1)
            pe_transpose(pe, "gla", v3(ytok, D), lambda i: P)
            pe.wait_ge(xlo_ok, XCNT["gla"])
            pe_split_rows(pe, "gla_o", 0, lambda part, k, t: (gla_y_hi, gla_y_lo)[part][:, k, t * P:(t + 1) * P], ROWB)

            pe_transpose(pe, "ffn0", xs, lambda i: P)
            pe.wait_ge(t_copied, t_all("ffn0"))
            pe_ffn(0)

            pe_transpose(pe, "mix1", xs, lambda i: P)
            pe.wait_ge(t_copied, t_all("mix1"))
            pe.wait_ge(xlo_ok, XCNT["kv"])
            for j in range(4):
                bank = fm_begin(pe)
                split_wait(pe, "nsa_in", j)
                split_columns("nsa_in", j, bank, kv_x_hi, kv_x_lo)
            rawv, rotv = v3(raw, SEQ), v3(rot, SEQ)
            for j in range(13):
                if j < 12:
                    if j == 4:
                        pe.wait_ge(xlo_ok, XCNT["mix1"])
                    bank = fm_begin(pe)
                    split_wait(pe, "nsa_in", 4 + j)
                    split_columns("nsa_in", 4 + j, bank, *((kv_x_hi, kv_x_lo) if j < 4 else (nsa_x_hi, nsa_x_lo)))
                if j:
                    pe.wait_ge(fm_free, fmc["pe"] - (1 if j < 12 else 0))
                    if j >= 3:
                        pe.wait_ge(rot_free, j - 2)
                    nc.tensor.matmul(ps[:, 6 + (j - 1) % 2, 0:SEQ], con("turn"), rawv[:, j - 1, :],
                                     start=True, stop=True).then_inc(rot_done, 1)
            n = plan["nsa_v"][0]
            for k in range(4):
                tile = 16 + k
                split_wait(pe, "nsa_in", tile)
                w_hi, w_lo = early_w_hi[tile % HI], ring_lo[:, (n + k) % RING, :]
                for c in range(2):
                    for t in range(TT):
                        for i, (x_, w) in enumerate(((kv_x_hi, w_hi), (kv_x_hi, w_lo), (kv_x_lo, w_hi))):
                            last = nc.tensor.matmul(ps[:, 2 + t, :], x_[:, 2 * k + c, t * P:(t + 1) * P],
                                                    w[:, c * 512:(c + 1) * 512],
                                                    start=(k == 0 and c == 0 and i == 0), stop=(k == 3 and c == 1 and i == 2))
                last.then_inc(tile_done, 1)
            wg = v3(par("w_gates"), 3 * NH)
            for t in range(TT):
                for c in range(KC):
                    last = nc.tensor.matmul(ps[:, 4, t * 64:t * 64 + 3 * NH], xn[:, c, t * P:(t + 1) * P], wg[:, c, :],
                                            start=(c == 0), stop=(c == KC - 1))
            last.then_inc(gate_done, 1)
            blkv = blk.rearrange("p (b l n) -> p b l n", b=2, l=CB // 2)
            NB = NKV * NCMP
            for b in range(2):
                pe.wait_ge(blk_ok, b + 1)
                n = plan["cmp_k"][0] + 4 * b
                for k in range(4):
                    w_wait(pe, n + k)
                    for c in range(4):
                        last = nc.tensor.matmul(ps[0:NB, 5, b * CHID:(b + 1) * CHID], blkv[:, b, 4 * k + c, 0:NB],
                                                ring[:, (n + k) % RING, c * CHID:(c + 1) * CHID],
                                                start=(k == 0 and c == 0), stop=(k == 3 and c == 3))
                    last.then_inc(tile_done, 1)
            pe.wait_ge(hid_ok, 1)
            pe.wait_ge(rot_free, 12)
            for u in range(4):
                last = nc.tensor.transpose(ps[:, 6, u * 64:u * 64 + NB], hid[0:NB, u * P:(u + 1) * P], ident[0:NB, 0:NB])
            last.then_inc(ht_done, 1)
            pe.wait_ge(ht_ok, 1)
            w2k, w2v = v3(par("w2_k"), P), v3(par("w2_v"), ND)
            hidTv, hvrv = v3(hidT, 2 * NB)[:, 0, :].rearrange("p (c n) -> p c n", c=2), hvr.rearrange("p (c g m) -> p c g m", c=2, g=NKV)
            for c in range(2):
                nc.tensor.matmul(ps[:, 7, 0:NB], w2k[:, c, :], hidTv[:, c, :], start=(c == 0), stop=(c == 1))
            for g in range(NKV):
                for c in range(2):
                    last = nc.tensor.matmul(ps[:, 7, 64 + g * ND:64 + (g + 1) * ND], hvrv[:, c, g, :], w2v[:, c, :],
                                            start=(c == 0), stop=(c == 1))
            last.then_inc(kc_done, 1)
            pe.wait_ge(kc_ok, 1)
            for t in range(TT):
                for g in range(NKV):
                    rows = 64 * (g % 2)
                    for r in range(NG):
                        j = 4 + (g // 2) * NG + r
                        col = 16 * (j - 4)
                        last = nc.tensor.matmul(ps[:, CSB[2 * t + g % 2], col:col + NCMP], rawv[rows:rows + ND, j, t * P:(t + 1) * P],
                                                kcT[rows:rows + ND, g * NCMP:(g + 1) * NCMP], start=True, stop=True)
                last.then_inc(cs_done, 1)
            pcv = pc.rearrange("p (t g m) -> p t g m", t=TT, g=NKV)
            pcTv = pcT.rearrange("p (g t m) -> p g t m", g=NKV, t=TT)
            pe.wait_ge(pc_ok, 1)
            pe.wait_ge(act_rows, 3)
            for g in range(NKV):
                for t in range(TT):
                    u = g * TT + t
                    last = nc.tensor.transpose(ps[:, 2 + u // 4, (u % 4) * P:(u % 4 + 1) * P], pcv[:, t, 2 * (g % 2) + g // 2, :], ident)
            last.then_inc(pct_done, 1)
            pe.wait_ge(pct_ok, 1)

            scav = sc_a.rearrange("p (b n) -> p b n", b=2)
            scbv = sc_b.rearrange("p (b n) -> p b n", b=2)
            ptv = pt.rearrange("p (b n) -> p b n", b=2)
            vswv = v3(vsw, 512)

            def scores(u):
                j, rows = u // 2, 64 * (u % 2)
                if u >= 2:
                    pe.wait_ge(max_ok, u - 1)
                for b in range(2):
                    key = rotv[rows:rows + ND, 2 * b + j // NG, :]
                    nc.tensor.matmul(ps[:, 2 * (u % 2), b * SEQ:(b + 1) * SEQ], rotv[rows:rows + ND, 4 + j, P:2 * P], key,
                                     start=True, stop=True)
                    last = nc.tensor.matmul(ps[:, 2 * (u % 2) + 1, b * P:(b + 1) * P], rotv[rows:rows + ND, 4 + j, 0:P],
                                            key[:, 0:P], start=True, stop=True)
                last.then_inc(s_done, 1)

            def turn_p(u):
                pe.wait_ge(p_ok, u + 1)
                if u:
                    pe.wait_ge(pt_ok, u)
                for b in range(2):
                    for s in range(2):
                        nc.tensor.transpose(ps[:, 4, (2 * b + s) * P:(2 * b + s + 1) * P],
                                            scav[:, u % 2, b * SEQ + s * P:b * SEQ + (s + 1) * P], ident)
                    last = nc.tensor.transpose(ps[:, 5, b * P:(b + 1) * P], scbv[:, u % 2, b * P:(b + 1) * P], ident)
                last.then_inc(pt_done, 1)

            def values(u):
                j, pr = u // 2, u % 2
                g, r = 2 * (j // NG) + pr, j % NG
                pe.wait_ge(pt_ok, u + 1)
                if j >= 2 and pr == 0:
                    pe.wait_ge(o_ok, j - 1)
                for t in range(TT):
                    o = ps[64 * pr:64 * pr + ND, 6 + j % 2, t * P:(t + 1) * P]
                    nc.tensor.matmul(o, vcr[32 * r:32 * r + 32, g * ND:(g + 1) * ND], pcTv[32 * r:32 * r + 32, g, t, :],
                                     start=True, stop=False, tile_position=(32 * r, 64 * pr))
                    for b in range(2):
                        for s in range(t + 1):
                            col = (2 * b + s) * P if t else 512 + b * P
                            last = nc.tensor.matmul(o, vswv[:, s, b * 256 + g * ND:b * 256 + (g + 1) * ND],
                                                    ptv[:, u % 2, col:col + P], start=False, stop=(b == 1 and s == t))
                last.then_inc(pv_done, 1)

            scores(0)
            for u in range(NH + 1):
                if u + 1 < NH:
                    scores(u + 1)
                if u < NH:
                    turn_p(u)
                if u:
                    values(u - 1)
            pe.wait_ge(o_ok, NH // 2)
            pe_rows(pe, plan["nsa_o"][0], lambda k, t: v3(oT, SEQ)[:, k, t * P:(t + 1) * P], ROWB)

            pe_transpose(pe, "ffn1", xs, lambda i: P)
            pe.wait_ge(t_copied, t_all("ffn1"))
            pe_ffn(1)

            pe_transpose(pe, "mix2", xs, lambda i: META if i == 0 else P)
            pe.wait_ge(t_copied, t_all("mix2"))
            bank = fm_begin(pe)
            wg2 = v3(par("w_gates2"), 36)
            for c in range(KC):
                last = nc.tensor.matmul(ps[0:36, bank, 0:L2], wg2[:, c, :], xn[:, c, :], start=(c == 0), stop=(c == KC - 1))
            last.then_inc(small_done, 1)
            pe.wait_ge(xlo_ok, XCNT["mix2"])
            for j in range(20):
                bank = fm_begin(pe)
                split_wait(pe, "mix_in", j)
                split_columns("mix_in", j, bank, mix_x_hi, mix_x_lo, L2)
            S0 = [(0, META), (META, P), (META + P, P)]
            VB = [(6, 7), (2, 3), (4, 5)]
            pe_split_rows(pe, "mix_in", 20, lambda part, k, t: (mix_x_hi, mix_x_lo)[part][:, k, S0[t][0]:S0[t][0] + S0[t][1]],
                          VB)
            linv = v3(lin, L2)
            pe.wait_ge(row_ok, 1)
            pe.wait_ge(fm_free, fmc["pe"])
            for s in range(3):
                c0, rows = S0[s]
                nc.tensor.transpose(ps[0:rows, 0, s * 16:s * 16 + 12], linv[0:12, 1, c0:c0 + rows], ident[0:12, 0:12])
                last = nc.tensor.transpose(ps[0:rows, 0, s * 16 + 12:s * 16 + 16], linv[0:4, 3, c0:c0 + rows], ident[0:4, 0:4])
            last.then_inc(col_done, 1)
            pe.wait_ge(fsq_ok, 1)
            pe.wait_ge(col_ok, 1)
            pe.wait_ge(act_rows, 4)
            fsqv = v3(fsq, L2)
            for j in range(8):
                last = nc.tensor.matmul(ps[:, j, 0:L2], con("ones64"), fsqv[:, j, :], start=True, stop=True)
            last.then_inc(fss_done, 1)
            mqkv, v2v, stmv = v3(mqk, L2), v3(v2, D), v3(stm, 640)
            pe.wait_ge(fvar_ok, 1)
            pe.wait_ge(msilu_ok, 1)
            for h in range(MH + 1):
                if h < MH:
                    if h >= 2:
                        pe.wait_ge(mst_ok, h - 1)
                    b0, b1 = 2 * (h % 2), 2 * (h % 2) + 1
                    k, q = mqkv[:, MH + h, :], mqkv[:, h, META:L2]
                    nc.tensor.matmul(ps[:, b0, 0:256], k[:, META:META + P], q, start=True, stop=True)
                    nc.tensor.matmul(ps[:, b0, 256:384], k[:, META + P:L2], q[:, P:2 * P], start=True, stop=True)
                    nc.tensor.matmul(ps[:, b1, 0:256], bcast(ident[0:4, h:h + 1], P), linv[0:4, 4, META:L2], start=True, stop=True)
                    nc.tensor.matmul(ps[0:META, b1, 256:512], k[:, 0:META], q, start=True, stop=True).then_inc(ms_done, 1)
                if h:
                    g = h - 1
                    pe.wait_ge(mst_ok, g + 1)
                    st = stmv[:, g, :]
                    for bank, lhs in ((4 + g // 2, lambda rows, s: v2v[0:rows, s, g * MD:(g + 1) * MD]),
                                      (6 + g // 2, lambda rows, s: con("ones")[0:rows, :])):
                        o = ps[:, bank, (g % 2) * 256:(g % 2 + 1) * 256]
                        nc.tensor.matmul(o, lhs(P, 1), st[:, 0:256], start=True, stop=False)
                        nc.tensor.matmul(o[:, P:2 * P], lhs(P, 2), st[:, 256:384], start=False, stop=False)
                        last = nc.tensor.matmul(o, lhs(META, 0), st[0:META, 384:640], start=False, stop=True)
                    last.then_inc(mnum_done, 1)
            for h in range(MH):
                last = nc.tensor.matmul(ps[:, h // 2, (h % 2) * 256:(h % 2 + 1) * 256], bcast(ident[0:4, h:h + 1], P),
                                        linv[0:4, 5, META:L2], start=True, stop=True)
            last.then_inc(mb_done, 1)
            pe.wait_ge(hsq_ok, 1)
            for h in range(MH):
                last = nc.tensor.matmul(ps[:, 2 + h // 2, (h % 2) * 256:(h % 2 + 1) * 256], con("ones"),
                                        v3(em, 256)[:, h, :], start=True, stop=True)
            last.then_inc(hss_done, 1)
            pe.wait_ge(fn_ok, 1)
            pe.wait_ge(hvar_ok, 1)
            pe.wait_ge(em_ok, 1)
            fqkv, sfxv, ptfv = v3(fqk, L2), v3(sfx, 512), v3(ptf, 640)

            def fscores(u):
                j, rows = u // 2, 64 * (u % 2)
                if u >= 2:
                    pe.wait_ge(max_ok, NH + u - 1)
                b0, b1 = 2 * (u % 2), 2 * (u % 2) + 1
                nc.tensor.matmul(ps[:, b0, 0:L2], bcast(ident[0:12, 4 + u:5 + u], P), linv[0:12, 6, :], start=True, stop=True)
                q, k = fqkv[rows:rows + FD, j, :], fqkv[rows:rows + FD, 4 + j, :]
                nc.tensor.matmul(ps[:, b1, 0:L2], q[:, META + P:L2], k, start=True, stop=True)
                nc.tensor.matmul(ps[:, b1, L2:L2 + META + P], q[:, META:META + P], k[:, 0:META + P],
                                 start=True, stop=True).then_inc(s_done, 1)

            def fturn(u):
                pe.wait_ge(p_ok, NH + u + 1)
                if u:
                    pe.wait_ge(pt_ok, NH + u)
                else:
                    pe.wait_ge(hn_ok, 1)
                p1, p0 = sfxv[:, u % 2, 0:L2], sfxv[:, u % 2, L2:L2 + META + P]
                nc.tensor.transpose(ps[:, 4, 0:P], p1[:, META:META + P], ident)
                nc.tensor.transpose(ps[:, 4, P:2 * P], p1[:, META + P:L2], ident)
                nc.tensor.transpose(ps[0:META, 4, 2 * P:3 * P], p1[:, 0:META], ident)
                nc.tensor.transpose(ps[:, 5, 0:P], p0[:, META:META + P], ident)
                nc.tensor.transpose(ps[0:META, 5, P:2 * P], p0[:, 0:META], ident).then_inc(pt_done, 1)

            def fvalues(u):
                j, pr = u // 2, u % 2
                pe.wait_ge(pt_ok, NH + u + 1)
                if j >= 2 and pr == 0:
                    pe.wait_ge(o_ok, NH // 2 + j - 1)
                ptu = ptfv[:, u % 2, :]
                for t in range(TT):
                    o = ps[64 * pr:64 * pr + FD, 6 + j % 2, t * P:(t + 1) * P]
                    v = lambda rows, s: v2v[0:rows, s, 512 + u * FD:512 + (u + 1) * FD]
                    if t == 0:
                        nc.tensor.matmul(o, v(P, 1), ptu[:, 384:512], start=True, stop=False)
                        nc.tensor.matmul(o, v(META, 0), ptu[0:META, 512:640], start=False, stop=True,
                                         tile_position=(0, 64 * pr))
                    else:
                        nc.tensor.matmul(o, v(P, 1), ptu[:, 0:P], start=True, stop=False)
                        nc.tensor.matmul(o, v(P, 2), ptu[:, P:2 * P], start=False, stop=False)
                        last = nc.tensor.matmul(o, v(META, 0), ptu[0:META, 2 * P:3 * P], start=False, stop=True,
                                                tile_position=(0, 64 * pr))
                last.then_inc(pv_done, 1)

            fscores(0)
            for u in range(FH + 1):
                if u + 1 < FH:
                    fscores(u + 1)
                if u < FH:
                    fturn(u)
                if u:
                    fvalues(u - 1)
            pe.wait_ge(o_ok, NH // 2 + FH // 2)
            pe.wait_ge(y2_ok, MH)
            pe_rows(pe, plan["mix_o"][0], lambda k, t: v3(y2T, SEQ)[:, k, t * P:(t + 1) * P], ROWB)

            pe_transpose(pe, "ffn2", xs, lambda i: P)
            pe.wait_ge(t_copied, t_all("ffn2"))
            pe.wait_ge(keys_in, 16)
            pe.wait_ge(xlo_ok, XCNT["ffn2"])
            qhTv = v3(qhT, SEQ)
            for j in range(2 * PH + 1):
                if j < 2 * PH:
                    bank = fm_begin(pe)
                    split_wait(pe, "peer_q", j)
                    split_columns("peer_q", j, bank, peer_x_hi, peer_x_lo)
                if j:
                    i = j - 1
                    pe.wait_ge(fm_free, fmc["pe"] - (1 if j < 2 * PH else 0))
                    if i % 4 == 0 and i >= 8:
                        pe.wait_ge(sc_ok, i // 4 - 1)
                    for t in range(TT):
                        last = nc.tensor.matmul(ps[:, 2 + 2 * (i // 4 % 2) + t, (i % 4) * P:(i % 4 + 1) * P],
                                                qhTv[:, i, t * P:(t + 1) * P], keysT[:, i, :], start=True, stop=True)
                    if i % 4 == 3:
                        last.then_inc(sc_done, 1)
            u0 = plan["peer_u"][0]

            def expert_u(tile, it=None):
                split_wait(pe, "peer_u", tile, it)
                if tile >= 2:
                    pe.wait_ge(gelu_ok, tile - 1 if it is None else it * RING + (tile - 1))
                split_columns("peer_u", tile, tile % 2, peer_x_hi, peer_x_lo)

            for tile in range(RING):
                expert_u(tile)
            with pe.Fori(0, UMID // RING - 1) as i:
                for k in range(RING):
                    expert_u(RING + k, i)
            ixv = ix.rearrange("p (a t n) -> p a t n", a=4, t=TT)
            pe.wait_ge(rt_ok, 1)
            for a in range(3):
                for t in range(TT):
                    last = nc.tensor.transpose(ps[:, 6 + a // 2, (a % 2) * SEQ + t * P:(a % 2) * SEQ + (t + 1) * P],
                                               ixv[:, a, t, :], ident)
            last.then_inc(rt_done, 1)
            rest = (NKEY - UMID) // RING
            with pe.Fori(0, rest) as i:
                for k in range(RING):
                    expert_u(UMID + k, i)
            for tile in range(UMID + rest * RING, NKEY):
                expert_u(tile)

            def token_gates(g, b):
                pe.wait_ge(oh_ok, g + 1)
                for q in range(4):
                    last = nc.tensor.matmul(ps[:, OHB[b], q * P:(q + 1) * P], oh_rows[b][:, 0, q, :],
                                            oh_rows[b][:, 1, q, :], start=True, stop=True)
                last.then_inc(g_done, 1)

            pe.wait_ge(route_ok, 1)
            for b in range(OH):
                token_gates(b, b)
            with pe.Fori(1, SEQ // (4 * OH)) as i:
                for b in range(OH):
                    pe.wait_ge(g_ok, i * OH + (b - OH + 1))
                    token_gates(i * OH + b, b)

            def expert_v(tile, it=None):
                split_wait(pe, "peer_v", tile, it)
                pe.wait_ge(ph_ok, tile + 1 if it is None else it * RING + (tile + 1))
                split_rows("peer_v", tile, tile % 2, tile == 0, tile == NKEY - 1)

            for tile in range(2):
                expert_v(tile)
            with pe.Fori(0, (NKEY - 2) // RING - 1) as i:
                for k in range(RING):
                    expert_v(2 + k, i)
            for tile in range(NKEY - RING, NKEY):
                expert_v(tile)

        @block.scalar
        def _(act):
            act.dma_start(x[:, :, :], x_in.rearrange("(t p) d -> p t d", p=P)).then_inc(x_in_sem, 16)
            act.dma_start(cst[:, 0:P], consts[:, 0:P]).then_inc(first_in, 16)
            act.dma_start(prm[:, 0:NGAIN], params[:, 0:NGAIN]).then_inc(first_in, 16)
            act.dma_start(prm[:, NGAIN:], params[:, NGAIN:]).then_inc(prm_in, 16)
            act.dma_start(cst[:, P:], consts[:, P:]).then_inc(prm_in, 16)
            act.wait_ge(dve_step, 1)

            def act_ffn(layer):
                cw = par(f"conv{layer}").rearrange("p (f s w) -> p f s w", s=2, w=4)
                n0, h0 = plan[f"ffn{layer}"][0], FT * layer

                name = f"ffn{layer}"

                def tile(f, k, need_u, need_h, need_c, it=None):
                    first = 3 * k - 1 if k else 0
                    for s, dst in enumerate((cgate, cval)):
                        act.wait_ge(tile_done, need_u + s)
                        if need_h is not None:
                            act.wait_ge((silu_done, h_ready)[s], need_h)
                        nc.scalar.activation(dst, ps[:, s, 0:SEQ], ACT.Identity, bias=cw[:, f, s, 3:4],
                                             scale=cw[:, f, s, 2:3]).then_inc(c0_done, 1)
                        if first + s + HI < 3 * FT:
                            split_hi(act, name, first + s + HI, it)
                    act.wait_ge(cg_done, need_c)
                    nc.scalar.activation(sgate, cgate, ACT.Silu).then_inc(silu_done, 1)
                    if 0 < k < FT - 1:
                        act.wait_ge(tile_done, need_u + 2)
                        split_hi(act, name, first + 2 + HI, it)

                act_input(act, name, ffn_x_hi)
                tile(0, 0, n0 + 1, h0 if h0 else None, h0 + 1)
                with act.Fori(0, (FT - 2) // 2) as i:
                    for k in (1, 2):
                        tile(i * 2 + k, k, i * 6 + (n0 + 3 * k), i * 2 + (h0 + k), i * 2 + (h0 + k + 1), i)
                f = FT - 1
                tile(f, f, 3 * f + n0, f + h0, f + h0 + 1)

            def act_ahead(name):
                for tile in range(HI):
                    split_hi(act, name, tile)

            act_norm(act, "mix0")
            act_ahead("gla_in")
            act_input(act, "mix0", gla_x_hi)
            behind_hi(act, "gla_in", (0, 1))
            act.wait_ge(abs_ok, 1)
            alink(act, nc.scalar.activation(dec, dec, ACT.Exp, scale=-1.0))
            nc.scalar.activation(dec, dec, ACT.Ln, bias=1.0).then_inc(ln_ok, 1)
            behind_hi(act, "gla_in", range(2, 9))
            for buf, need, tiles in ((qx, 1, (9, 10, 11)), (ka, 2, (12,)), (kd, 3, ())):
                act.wait_ge(dsub_ok, need)
                nc.scalar.activation(buf, buf, ACT.Exp, scale=1.0 / GTAU).then_inc(dexp_ok, 1)
                behind_hi(act, "gla_in", tiles)
            nc.scalar.activation(qb, bcum, ACT.Exp, scale=1.0 / GTAU).then_inc(dexp_ok, 1)
            behind_hi(act, "gla_in", range(13, 16))
            rows_wait(act, "gla_v")
            for t in range(TT):
                for half in range(2):
                    last = nc.scalar.activation(v3(vtok, D)[:, t, half * 512:(half + 1) * 512], ps[:, ROWB[t][half], :], ACT.Copy)
            last.then_inc(act_rows, 1)
            behind_hi(act, "gla_in", range(16, 21))
            rows_wait(act, "gla_r")
            RB = [(6, 7), (0, 1)]
            for t in range(TT):
                for half in range(2):
                    last = nc.scalar.activation(v3(rtok, D)[:, t, half * 512:(half + 1) * 512], ps[:, RB[t][half], :], ACT.Silu)
            last.then_inc(act_rows, 1)
            act_ahead("gla_o")
            act.wait_ge(kdt_done, 1)
            for b in range(2):
                last = nc.scalar.activation(kdT[:, b * 512:(b + 1) * 512], ps[:, 3 + b, :], ACT.Copy)
            last.then_inc(kdt_ok, 1)
            OB = [6, 7, 0, 1]
            for t in range(TT):
                act.wait_ge(go_done, 2 * t + 2)
                for h in range(GH):
                    last = nc.scalar.activation(v3(ytok, D)[:, t, h * GDV:(h + 1) * GDV],
                                                ps[:, OB[2 * t + h // 2], (h % 2) * GDV:(h % 2 + 1) * GDV], ACT.Square,
                                                accum_out=stat[:, 32 + t * GH + h:33 + t * GH + h])
                last.then_inc(osq_ok, 1)
            act.wait_ge(ovar_ok, 1)
            nc.scalar.activation(stat[:, 40:48], stat[:, 48:56], ACT.Sqrt).then_inc(osd_ok, 1)
            act_input(act, "gla", gla_y_hi, v3(yT, SEQ))
            behind_hi(act, "gla_o", range(0, KC - HI))

            act_ahead("ffn0")
            act_norm(act, "ffn0")
            act_ffn(0)

            act_norm(act, "mix1")
            act_ahead("nsa_in")
            act_input(act, "kv", kv_x_hi, v3(xkv, SEQ))
            act_input(act, "mix1", nsa_x_hi)
            behind_hi(act, "nsa_in", range(4))
            act.wait_ge(fm_free, 3 * GH + 1 + 4)
            cr = cmpraw.rearrange("p (b g t) -> p b g t", b=2, g=2)
            sh = shifted.rearrange("p (b g r t) -> p b g r t", b=2, g=2, r=2)
            for b in range(2):
                for r in range(2):
                    act.dma_start(sh[0:64, b, :, r, :], cr[64 * r:64 * r + 64, b, :, :]).then_inc(shift_in, 16)
                    act.dma_start(sh[64:128, b, :, r, 0:SEQ - 1], cr[64 * r:64 * r + 64, b, :, 1:SEQ]).then_inc(shift_in, 16)
            behind_hi(act, "nsa_in", range(4, 20 - HI))
            rows_wait(act, "nsa_v")
            for t in range(TT):
                last = nc.scalar.activation(v3(vsw, 512)[:, t, :], ps[:, 2 + t, :], ACT.Copy)
            last.then_inc(act_rows, 1)
            act.wait_ge(gate_done, 1)
            nc.scalar.activation(v3(gs, 3 * NH), ps[:, 4, 0:128].rearrange("p (t n) -> p t n", t=TT)[:, :, 0:3 * NH],
                                 ACT.Sigmoid).then_inc(gate_ok, 1)
            rows_wait(act, "cmp_v")
            nc.scalar.activation(hid[0:NKV * NCMP, :], ps[0:NKV * NCMP, 5, :], ACT.Gelu_apprx_tanh).then_inc(hid_ok, 1)
            act.wait_ge(cs_ok, 1)
            nc.scalar.activation(csc[:, 0:480], csc[:, 0:480], ACT.Exp).then_inc(ce_ok, 1)
            act.wait_ge(pct_done, 1)
            for b in range(2):
                last = nc.scalar.activation(pcT[:, b * 512:(b + 1) * 512], ps[:, 2 + b, :], ACT.Copy)
            last.then_inc(pct_ok, 1)
            scav, scbv, ptv = v3(sc_a, 512), v3(sc_b, 256), v3(pt, 768)

            def copy_pt(u):
                act.wait_ge(pt_done, u + 1)
                if u >= 2:
                    act.wait_ge(pv_done, u - 1)
                nc.scalar.activation(ptv[:, u % 2, 0:512], ps[:, 4, :], ACT.Copy)
                nc.scalar.activation(ptv[:, u % 2, 512:768], ps[:, 5, 0:256], ACT.Copy).then_inc(pt_ok, 1)

            for u in range(NH + 1):
                if u < NH:
                    act.wait_ge(max_ok, u + 1)
                    c = 8 * (u % 2)
                    for b in range(2):
                        a = scav[:, u % 2, b * SEQ:(b + 1) * SEQ]
                        nc.scalar.activation(a, a, ACT.Exp, bias=stat[:, 32 + c + b:33 + c + b],
                                             accum_out=stat[:, 36 + c + b:37 + c + b])
                        a = scbv[:, u % 2, b * P:(b + 1) * P]
                        last = nc.scalar.activation(a, a, ACT.Exp, bias=stat[:, 34 + c + b:35 + c + b],
                                                    accum_out=stat[:, 38 + c + b:39 + c + b])
                    last.then_inc(exp_ok, 1)
                if u:
                    copy_pt(u - 1)

            act_ahead("ffn1")
            act_norm(act, "ffn1")
            act_ffn(1)

            act.wait_ge(x_ready, 8)
            act.dma_start(xm, meta_in).then_inc(meta_sem, 16)
            act.dma_start(gfin, g_final.partition_broadcast(P)).then_inc(fin_sem, 16)
            act_norm(act, "final")
            act_norm(act, "mix2")
            act_ahead("mix_in")
            act_input(act, "mix2", mix_x_hi, xn[:, :, :])
            act.wait_ge(gab_ok, 1)
            linv = v3(lin, L2)
            mqkv = v3(mqk, L2)
            alink(act, nc.scalar.activation(linv[0:12, 2, :], linv[0:12, 2, :], ACT.Exp, scale=-1.0))
            nc.scalar.activation(linv[0:12, 2, :], linv[0:12, 2, :], ACT.Ln, bias=1.0).then_inc(gln_ok, 1)
            cm = v3(par("conv_m"), MCONV)
            for j in range(2 * MH):
                fm_wait(act, FM2 + 1 + j)
                nc.scalar.activation(mqkv[:, j, :], ps[:, (FM2 + 1 + j) % 2, 0:L2], ACT.Copy,
                                     scale=cm[:, j, 3:4]).then_inc(mc0, 1)
                split_hi(act, "mix_in", j + HI)
            act.wait_ge(fm_free, FM2 + 1 + 2 * MH)
            nc.scalar.activation(mqk, mqk, ACT.Silu).then_inc(msilu_ok, 1)
            behind_hi(act, "mix_in", range(2 * MH, 20))
            act.wait_ge(fm_free, FM2 + 1 + 20)
            nc.scalar.activation(fsq, fqk, ACT.Square).then_inc(fsq_ok, 1)
            behind_hi(act, "mix_in", range(20, 28 - HI))
            rows_wait(act, "mix_v")
            VB, ROWS = [(6, 7), (2, 3), (4, 5)], [META, P, P]
            for s in range(3):
                for half in range(2):
                    last = nc.scalar.activation(v3(v2, D)[0:ROWS[s], s, half * 512:(half + 1) * 512],
                                                ps[0:ROWS[s], VB[s][half], :], ACT.Copy)
            last.then_inc(act_rows, 1)
            act.wait_ge(fvar_ok, 1)
            nc.scalar.activation(fsq, fsq, ACT.Sqrt).then_inc(fsd_ok, 1)
            wv = v3(wts, 640)
            for h in range(MH):
                act.wait_ge(mw_ok, h + 1)
                nc.scalar.activation(wv[:, h, 0:384], wv[:, h, 0:384], ACT.Exp)
                nc.scalar.activation(wv[0:META, h, 384:640], wv[0:META, h, 384:640], ACT.Exp).then_inc(mexp_ok, 1)
            act.wait_ge(mb_done, 1)
            for b in range(2):
                last = nc.scalar.activation(em[:, b * 512:(b + 1) * 512], ps[:, b, :], ACT.Exp, scale=-1.0)
            last.then_inc(em_ok, 1)
            act.wait_ge(hn_ok, 1)
            nc.scalar.activation(em, hn, ACT.Square).then_inc(hsq_ok, 1)
            act.wait_ge(hvar_ok, 1)
            alink(act, nc.scalar.activation(dn, dn, ACT.Sqrt))
            nc.scalar.activation(mo, mo, ACT.Sigmoid).then_inc(hsd_ok, 1)
            sfxv, ptfv = v3(sfx, 512), v3(ptf, 640)
            for u in range(FH + 1):
                if u < FH:
                    act.wait_ge(max_ok, NH + u + 1)
                    c = 8 * (u % 2)
                    a = sfxv[:, u % 2, 0:L2]
                    nc.scalar.activation(a, a, ACT.Exp, bias=stat[:, 32 + c:33 + c], accum_out=stat[:, 34 + c:35 + c])
                    a = sfxv[:, u % 2, L2:L2 + META + P]
                    nc.scalar.activation(a, a, ACT.Exp, bias=stat[:, 33 + c:34 + c],
                                         accum_out=stat[:, 35 + c:36 + c]).then_inc(exp_ok, 1)
                if u:
                    w = u - 1
                    act.wait_ge(pt_done, NH + w + 1)
                    if w >= 2:
                        act.wait_ge(pv_done, NH + w - 1)
                    nc.scalar.activation(ptfv[:, w % 2, 0:256], ps[:, 4, 0:256], ACT.Copy)
                    nc.scalar.activation(ptfv[0:META, w % 2, 256:384], ps[0:META, 4, 256:384], ACT.Copy)
                    nc.scalar.activation(ptfv[:, w % 2, 384:512], ps[:, 5, 0:128], ACT.Copy)
                    nc.scalar.activation(ptfv[0:META, w % 2, 512:640], ps[0:META, 5, 128:256], ACT.Copy).then_inc(pt_ok, 1)

            act.wait_ge(x_ready, 12)
            act.dma_start(keysT, keys).then_inc(keys_in, 16)
            act_norm(act, "ffn2")
            act_input(act, "ffn2", peer_x_hi)
            scv = scs.rearrange("p (t i n) -> p t i n", t=TT, i=2 * PH)

            def scores(i):
                act.wait_ge(sc_done, i + 1)
                for t in range(TT):
                    last = nc.scalar.activation(scv[:, t, 4 * i:4 * i + 4, :],
                                                ps[:, 2 + 2 * (i % 2) + t, :].rearrange("p (i n) -> p i n", n=NKEY), ACT.Copy)
                last.then_inc(sc_ok, 1)

            act.wait_ge(xlo_ok, XCNT["ffn2"])
            for tile in range(HI):
                split_hi(act, "peer_q", tile)
            q0 = plan["peer_q"][0]
            for j in range(2 * PH):
                act.wait_ge(tile_done, q0 + j + 1)
                if j + HI < 2 * PH:
                    split_hi(act, "peer_q", j + HI)
                else:
                    split_hi(act, "peer_u", j + HI - 2 * PH)
                if j % 4 == 1 and j > 4:
                    scores(j // 4 - 1)
            scores(3)
            u0, v0 = plan["peer_u"][0], plan["peer_v"][0]

            def gelu(j, tile, it=None):
                need = u0 + tile + 1
                act.wait_ge(tile_done, need if it is None else it * RING + need)
                nc.scalar.activation(acts[:, j, :], ps[:, tile % 2, 0:SEQ], ACT.Gelu).then_inc(gelu_ok, 1)
                if tile + HI < NKEY:
                    split_hi(act, "peer_u", tile + HI, it)

            GEXP = 8 * RING
            with act.Fori(0, GEXP // RING) as i:
                for k in range(RING):
                    gelu(i * RING + k, k, i)
            act.wait_ge(gsub_ok, 1)
            nc.scalar.activation(tops, tops, ACT.Exp).then_inc(gexp_ok, 1)
            with act.Fori(0, (UMID - GEXP) // RING) as i:
                for k in range(RING):
                    gelu(i * RING + (GEXP + k), GEXP + k, i)
            act.wait_ge(route_ok, 1)
            rest = (NKEY - HI - UMID) // RING
            with act.Fori(0, rest) as i:
                for k in range(RING):
                    gelu(i * RING + (UMID + k), UMID + k, i)
            for tile in range(UMID + rest * RING, NKEY):
                gelu(tile, tile)
            for tile in range(2):
                split_hi(act, "peer_v", tile)
            with act.Fori(0, SEQ // (4 * OH)) as i:
                for b in range(OH):
                    act.wait_ge(eq_ok, i * OH + (b + 1))
                    for q in range(4):
                        rows = oh_rows[b][:, 1, q, :]
                        last = nc.scalar.activation(rows, rows, ACT.Copy,
                                                    scale=route[:, 2, bass.ds(i * (4 * OH) + (4 * b + q), 1)])
                    last.then_inc(oh_ok, 1)
            act.wait_ge(g_done, SEQ // 4)
            split_hi(act, "peer_v", 2)
            rest = (NKEY - HI) // RING
            with act.Fori(0, rest) as i:
                for k in range(RING):
                    act.wait_ge(tile_done, i * RING + (v0 + k + 1))
                    split_hi(act, "peer_v", k + HI, i)
            for tile in range(rest * RING, NKEY - HI):
                act.wait_ge(tile_done, v0 + tile + 1)
                split_hi(act, "peer_v", tile + HI)

        @block.vector
        def _(dve):
            def dve_ffn(layer):
                cw = par(f"conv{layer}").rearrange("p (f s w) -> p f s w", s=2, w=4)
                u0, h0 = 2 * FT * layer, FT * layer
                name = f"ffn{layer}"

                def tile(f, k, c0, step, need_s, it=None):
                    first = 3 * k - 1 if k else 0
                    for s, dst in enumerate((cgate, cval)):
                        dve.wait_ge(c0_done, c0 + s)
                        nc.vector.scalar_tensor_tensor(dst[:, 1:SEQ], ps[:, s, 0:SEQ - 1], cw[:, f, s, 1:2], dst[:, 1:SEQ],
                                                       ALU.mult, ALU.add).then_inc(dve_step, 1)
                        dve.wait_ge(dve_step, step + (s + 1))
                        last = nc.vector.scalar_tensor_tensor(dst[:, 2:SEQ], ps[:, s, 0:SEQ - 2], cw[:, f, s, 0:1], dst[:, 2:SEQ],
                                                              ALU.mult, ALU.add)
                        last.then_inc((cg_done, cv_done)[s], 1)
                        if s == 0 and first + HI < 3 * FT:
                            split_lo(dve, name, first + HI, it)
                    dve.wait_ge(cv_done, need_s)
                    dve.wait_ge(silu_done, need_s)
                    nc.vector.tensor_tensor(hfull, sgate, cval, ALU.mult).then_inc(dve_step, 1)
                    dve.wait_ge(dve_step, step + 3)
                    split_hidden(dve, hfull, k % 2, step + 4, h_ready)
                    if k < FT - 1:
                        split_lo(dve, name, first + 1 + HI, it)
                        if k:
                            split_lo(dve, name, first + 2 + HI, it)

                dve_input(dve, name, ffn_x_hi, ffn_x_lo)
                d0 = cnt["dve"]
                tile(0, 0, u0 + 1, d0, h0 + 1)
                with dve.Fori(0, (FT - 2) // 2) as i:
                    for k in (1, 2):
                        tile(i * 2 + k, k, i * 4 + (u0 + 2 * k + 1), i * 8 + (d0 + 4 * k), i * 2 + (h0 + k + 1), i)
                f = FT - 1
                tile(f, f, u0 + 2 * f + 1, d0 + 4 * f, h0 + f + 1)
                cnt["dve"] = d0 + 4 * FT

            def dve_ahead(name):
                for tile in range(HI):
                    split_lo(dve, name, tile)

            dlink(dve, nc.vector.memset(stat[:, :], 1.0))
            dve_norm(dve, "mix0")
            dve.wait_ge(first_in, 32)
            dve_transpose(dve, "mix0", own_cols, [(xn, "g_mix0")])
            split_lo(dve, "gla_in", 0)
            dve_input(dve, "mix0", gla_x_hi, gla_x_lo)
            for tile in range(1, HI):
                split_lo(dve, "gla_in", tile)
            dve.wait_ge(prm_in, 32)
            bank = fm_take(dve)
            nc.vector.tensor_copy(dec[0:GRANK, 0:SEQ], ps[0:GRANK, bank, 0:SEQ]).then_inc(fm_free, 1)

            def take_tile(h):
                bank = fm_take(dve)
                dst = v3(qT if h < GH else kT, SEQ)[:, h % GH, :]
                nc.vector.tensor_copy(dst, ps[:, bank, 0:SEQ]).then_inc(fm_free, 1)
                split_lo(dve, "gla_in", h + HI)

            take_tile(0)
            take_tile(1)
            for h in range(GH):
                bank = fm_take(dve)
                nc.vector.tensor_scalar(v3(z, SEQ)[:, h, :], ps[:, bank, 0:SEQ], par("b_alpha")[:, h:h + 1], None,
                                        ALU.add).then_inc(fm_free, 1)
            dve.wait_ge(fm_free, fmc["dve"])
            nc.vector.scalar_tensor_tensor(dec, z, -1.0, z, ALU.mult, ALU.max).then_inc(abs_ok, 1)
            take_tile(2)
            dve.wait_ge(ln_ok, 1)
            dlink(dve, nc.vector.scalar_tensor_tensor(z, z, 0.0, dec, ALU.min, ALU.subtract))
            for h in range(3, 2 * GH):
                take_tile(h)
            for h in range(GH):
                last = nc.vector.tensor_tensor_scan(v3(bcum, SEQ)[:, h, :], con("reset"), v3(z, SEQ)[:, h, :], 0.0,
                                                    ALU.mult, ALU.add)
            dlink(dve, last)
            GR = GH * NCH
            bg = bcum.rearrange("p (g t) -> p g t", t=GC)
            NS = GC // GSUB
            qg = qx.rearrange("p (g a t) -> p g a t", a=NS, t=GSUB)
            bs = bcum.rearrange("p (g a t) -> p g a t", a=NS, t=GSUB)
            nc.vector.tensor_copy(qg[:, :, 0, :], bs[:, :, 0, :])
            nc.vector.tensor_tensor(qg[:, :, 1:NS, :], bs[:, :, 1:NS, :],
                                    bcast(bs[:, :, 0:NS - 1, GSUB - 1:GSUB], GR, NS - 1, GSUB), ALU.subtract).then_inc(dsub_ok, 1)
            split_lo(dve, "gla_in", 11)
            kg = ka.rearrange("p (a g t) -> p a g t", a=NS, t=GC)
            nc.vector.tensor_scalar(kg[:, 0], bg, -1.0, None, ALU.mult)
            for a in range(1, NS):
                last = nc.vector.tensor_tensor(kg[:, a], bcast(bg[:, :, a * GSUB - 1:a * GSUB], GR, GC), bg, ALU.subtract)
                if a < NS - 1:
                    split_lo(dve, "gla_in", 11 + a)
            dlink(dve, last)
            nc.vector.tensor_scalar(ka, ka, CLAMP * GTAU, None, ALU.min).then_inc(dsub_ok, 1)
            split_lo(dve, "gla_in", 14)
            nc.vector.tensor_tensor(kd.rearrange("p (g t) -> p g t", t=GC), bcast(bg[:, :, GC - 1:GC], GR, GC), bg,
                                    ALU.subtract).then_inc(dsub_ok, 1)
            split_lo(dve, "gla_in", 15)
            dve.wait_ge(fm_free, fmc["dve"])
            dve.wait_ge(dexp_ok, 1)
            nc.vector.scalar_tensor_tensor(qx, qx, GDK ** -0.5, qT, ALU.mult, ALU.mult).then_inc(dmul_ok, 1)
            split_lo(dve, "gla_in", 16)
            dve.wait_ge(dexp_ok, 2)
            kav = ka.rearrange("p (a n) -> p a n", a=NS)
            for a in (0, NS // 2):
                part = kav[:, a:a + NS // 2]
                last = nc.vector.tensor_tensor(part, part, bcast(kT.unsqueeze(1), NS // 2, GH * SEQ), ALU.mult)
                if a:
                    last.then_inc(dmul_ok, 1)
                split_lo(dve, "gla_in", 17 + (a > 0))
            dve.wait_ge(dexp_ok, 3)
            nc.vector.tensor_tensor(kd, kd, kT, ALU.mult).then_inc(dmul_ok, 1)
            split_lo(dve, "gla_in", 19)
            dve.wait_ge(dexp_ok, 4)
            dlink(dve, nc.vector.tensor_copy(stat[:, 16:32], qb.rearrange("p (g t) -> p g t", t=GC)[:, :, GC - 1]))
            nc.vector.scalar_tensor_tensor(qb, qb, GDK ** -0.5, qT, ALU.mult, ALU.mult).then_inc(dmul_ok, 1)
            for tile in range(20, 24):
                split_lo(dve, "gla_in", tile)
            dve.wait_ge(att_done, 1)
            nc.vector.tensor_tensor(v3(att, GC), v3(ps[:, 2, :], GC), bcast(con("tril").unsqueeze(1), GH * TT, GC),
                                    ALU.mult).then_inc(att_ok, 1)
            stv = state.rearrange("p (b h v) -> p b h v", b=2, h=GH)
            for c in range(NCH - 1):
                dve.wait_ge(kv_done, c + 1)
                if c:
                    dve.wait_ge(go_done, c)
                for h in range(GH):
                    got = ps[:, (2, 5)[h // 2], (h % 2) * GDV:(h % 2 + 1) * GDV]
                    new = stv[:, (c + 1) % 2, h, :]
                    if c == 0:
                        last = nc.vector.tensor_copy(new, got)
                    else:
                        last = nc.vector.scalar_tensor_tensor(new, stv[:, c % 2, h, :],
                                                              stat[:, 16 + h * NCH + c:17 + h * NCH + c], got,
                                                              ALU.mult, ALU.add)
                last.then_inc(state_ok, 1)
                dve.wait_ge(state_ok, c + 1)
            dve_ahead("gla_o")
            dve.wait_ge(osq_ok, TT)
            nc.vector.tensor_scalar(stat[:, 48:56], stat[:, 32:40], 1.0 / GDV, EPS, ALU.mult, ALU.add).then_inc(ovar_ok, 1)
            dve.wait_ge(osd_ok, 1)
            dlink(dve, nc.vector.reciprocal(stat[:, 56:64], stat[:, 40:48]))
            OB = [6, 7, 0, 1]
            dve.wait_ge(act_rows, 2)
            for t in range(TT):
                for h in range(GH):
                    cols = slice(h * GDV, (h + 1) * GDV)
                    last = nc.vector.scalar_tensor_tensor(v3(ytok, D)[:, t, cols],
                                                          ps[:, OB[2 * t + h // 2], (h % 2) * GDV:(h % 2 + 1) * GDV],
                                                          stat[:, 56 + t * GH + h:57 + t * GH + h],
                                                          v3(rtok, D)[:, t, cols], ALU.mult, ALU.mult)
                last.then_inc(tok_ready, 1)
            dve_transpose(dve, "gla", own_cols, [(v3(yT, SEQ), "g_gla")])
            dve_input(dve, "gla", gla_y_hi, gla_y_lo, v3(yT, SEQ))
            for tile in range(HI, KC):
                split_lo(dve, "gla_o", tile)
            dve_residual(dve, "gla_o")

            dve_ahead("ffn0")
            dve_norm(dve, "ffn0")
            dve_transpose(dve, "ffn0", own_cols, [(xn, "g_ffn0")])
            dve_ffn(0)
            dve_residual(dve, "ffn0")

            dve_norm(dve, "mix1")
            dve_transpose(dve, "mix1", own_cols, [(xn, "g_mix1"), (v3(xkv, SEQ), "g_kv")])
            split_lo(dve, "nsa_in", 0)
            dve_input(dve, "kv", kv_x_hi, kv_x_lo, v3(xkv, SEQ))
            for tile in range(1, HI):
                split_lo(dve, "nsa_in", tile)
            for j in range(4):
                bank = fm_take(dve)
                nc.vector.tensor_copy(v3(cmpraw, SEQ)[:, j, :], ps[:, bank, 0:SEQ]).then_inc(fm_free, 1)
                split_lo(dve, "nsa_in", j + HI)
                if j == 1:
                    dve_input(dve, "mix1", nsa_x_hi, nsa_x_lo)
            nc.vector.memset(hvr, 0.0)
            nc.vector.memset(pc, 0.0)
            rawv, rotv = v3(raw, SEQ), v3(rot, SEQ)
            for j in range(13):
                if j < 12:
                    bank = fm_take(dve)
                    nc.vector.tensor_copy(rawv[:, j, :], ps[:, bank, 0:SEQ]).then_inc(fm_free, 1)
                    split_lo(dve, "nsa_in", 4 + j + HI)
                if j:
                    i = j - 1
                    dve.wait_ge(rot_done, i + 1)
                    nc.vector.tensor_tensor(rotv[:, i, :], ps[:, 6 + i % 2, 0:SEQ], con("sin"), ALU.mult).then_inc(rot_free, 1)
                    dlink(dve, nc.vector.tensor_tensor(tmp[:, 0:SEQ], rawv[:, i, :], con("cos"), ALU.mult))
                    dlink(dve, nc.vector.tensor_tensor(rotv[:, i, :], rotv[:, i, :], tmp[:, 0:SEQ], ALU.add))
            split_lo(dve, "nsa_in", 19)
            dve.wait_ge(shift_in, 16 * 8)
            blkv = blk.rearrange("p (b l g n) -> p b l g n", b=2, l=CB // 2, g=NKV)
            shv = shifted.rearrange("p (b g t) -> p b g t", b=2, g=NKV)
            for b, pe_ in ((0, "pe_k"), (1, "pe_v")):
                for g in range(NKV):
                    src = shv[:, b, g, :].rearrange("p (n l e) -> p l n e", l=CB // 4, e=2)
                    lo, hi = src[:, :, 0:NCMP, 0], src[:, :, 1:NCMP + 1, 0]
                    for q, half in enumerate((lo, hi)):
                        ls = slice(q * CB // 4, (q + 1) * CB // 4)
                        last = nc.vector.tensor_tensor(blkv[:, b, ls, g, :], half,
                                                       bcast(par(pe_)[:, ls].unsqueeze(2), CB // 4, NCMP), ALU.add)
                last.then_inc(blk_ok, 1)
            NB = NKV * NCMP
            dve.wait_ge(ht_done, 1)
            hb = v3(ps[:, 6, 0:256], 64)
            hvrv = hvr.rearrange("p (c g r n) -> p c g r n", c=2, g=NKV, r=NG)
            nc.vector.tensor_copy(hidT[:, 0:2 * NB].rearrange("p (c n) -> p c n", c=2), hb[:, 0:2, 0:NB])
            for c in range(2):
                last = nc.vector.tensor_copy(hvrv[:, c, :, :, 0:NCMP],
                                             bcast(hb[:, 2 + c, 0:NB].rearrange("p (g n) -> p g n", g=NKV).unsqueeze(2),
                                                   NKV, NG, NCMP))
            last.then_inc(ht_ok, 1)
            dve.wait_ge(kc_done, 1)
            nc.vector.tensor_copy(kcT[:, 0:NB], ps[:, 7, 0:NB])
            nc.vector.tensor_copy(vcr, ps[:, 7, 64:320]).then_inc(kc_ok, 1)
            csv = csc[:, 0:480].rearrange("p (t h n) -> p t h n", t=TT, h=NH)
            for t in range(TT):
                dve.wait_ge(cs_done, t + 1)
                mask = con("cmask")[:, t * NCMP:(t + 1) * NCMP]
                for b in range(2):
                    got = ps[:, CSB[2 * t + b], 0:128].rearrange("p (h n) -> p h n", n=16)[:, :, 0:NCMP]
                    last = nc.vector.scalar_tensor_tensor(csv[:, t, 8 * b:8 * b + 8], got, ND ** -0.5,
                                                          bcast(mask.unsqueeze(1), 8, NCMP), ALU.mult, ALU.add)
            dlink(dve, last)
            cflat = csc[:, 0:480].rearrange("p (h n) -> p h n", n=NCMP)
            dlink(dve, nc.vector.tensor_reduce(tmp[:, 0:32], cflat, AX.X, ALU.max))
            nc.vector.tensor_tensor(cflat, cflat, bcast(tmp[:, 0:32].unsqueeze(2), 32, NCMP), ALU.subtract).then_inc(cs_ok, 1)
            dve.wait_ge(ce_ok, 1)
            dlink(dve, nc.vector.tensor_reduce(tmp[:, 32:64], cflat, AX.X, ALU.add))
            dlink(dve, nc.vector.reciprocal(tmp[:, 64:96], tmp[:, 32:64]))
            dve.wait_ge(gate_ok, 1)
            gsv = gs.rearrange("p (t b h) -> p t b h", t=TT, b=3)
            for t in range(TT):
                for b in range(2):
                    c = t * NH + 8 * b
                    last = nc.vector.scalar_tensor_tensor(
                        v3(tmp[:, 96 + c:104 + c], NG), v3(tmp[:, 64 + c:72 + c], NG), con("cvalid")[:, t:t + 1],
                        gsv[:, t, 0, :].rearrange("p (g b r) -> p g b r", b=2, r=NG)[:, :, b, :], ALU.mult, ALU.mult)
            dlink(dve, last)
            pcv = pc.rearrange("p (h n) -> p h n", n=32)
            nc.vector.tensor_tensor(pcv[:, :, 0:NCMP], cflat, bcast(tmp[:, 96:128].unsqueeze(2), 32, NCMP),
                                    ALU.mult).then_inc(pc_ok, 1)
            scav, scbv = v3(sc_a, 512), v3(sc_b, 256)

            def logits(u):
                dve.wait_ge(s_done, u + 1)
                if u >= 2:
                    dve.wait_ge(pt_done, u - 1)
                a, b, c = v3(scav[:, u % 2, :], SEQ), v3(scbv[:, u % 2, :], P), 8 * (u % 2)
                nc.vector.scalar_tensor_tensor(a, v3(ps[:, 2 * (u % 2), :], SEQ), ND ** -0.5,
                                               bcast(con("mask1").unsqueeze(1), 2, SEQ), ALU.mult, ALU.add)
                dlink(dve, nc.vector.scalar_tensor_tensor(b, v3(ps[:, 2 * (u % 2) + 1, 0:256], P), ND ** -0.5,
                                                          bcast(con("mask0").unsqueeze(1), 2, P), ALU.mult, ALU.add))
                nc.vector.tensor_reduce(stat[:, 32 + c:34 + c], a, AX.X, ALU.max, negate=True)
                nc.vector.tensor_reduce(stat[:, 34 + c:36 + c], b, AX.X, ALU.max, negate=True).then_inc(max_ok, 1)

            def probs(u):
                j, c = u // 2, 8 * (u % 2)
                h = (2 * (j // NG) + u % 2) * NG + j % NG
                dve.wait_ge(exp_ok, u + 1)
                dlink(dve, nc.vector.reciprocal(tmp[:, 0:4], stat[:, 36 + c:40 + c]))
                nc.vector.tensor_tensor(tmp[:, 4:6], tmp[:, 0:2], gsv[:, 1, 1:3, h], ALU.mult)
                dlink(dve, nc.vector.tensor_tensor(tmp[:, 6:8], tmp[:, 2:4], gsv[:, 0, 1:3, h], ALU.mult))
                for b in range(2):
                    a = scav[:, u % 2, b * SEQ:(b + 1) * SEQ]
                    nc.vector.tensor_scalar(a, a, tmp[:, 4 + b:5 + b], None, ALU.mult)
                    a = scbv[:, u % 2, b * P:(b + 1) * P]
                    last = nc.vector.tensor_scalar(a, a, tmp[:, 6 + b:7 + b], None, ALU.mult)
                last.then_inc(p_ok, 1)

            def heads_out(j, need, dst, base):
                dve.wait_ge(pv_done, need)
                nc.vector.tensor_copy(dst, ps[:, 6 + j % 2, 0:SEQ]).then_inc(o_ok, 1)

            for u in range(NH + 2):
                if u < NH:
                    logits(u)
                if 1 <= u <= NH:
                    probs(u - 1)
                if u >= 3 and u % 2 == 1:
                    heads_out((u - 3) // 2, u - 1, v3(oT, SEQ)[:, (u - 3) // 2, :], 0)
            dve_residual(dve, "nsa_o")

            dve_ahead("ffn1")
            dve_norm(dve, "ffn1")
            dve_transpose(dve, "ffn1", own_cols, [(xn, "g_ffn1")])
            dve_ffn(1)
            dve_residual(dve, "ffn1")

            dve.wait_ge(fin_sem, 16)
            dve_norm(dve, "final", gain=gfin)
            dve_norm(dve, "mix2")
            dve_transpose(dve, "mix2", meta_cols, [(xn, "g_mix2")])
            split_lo(dve, "mix_in", 0)
            dve_input(dve, "mix2", mix_x_hi, mix_x_lo, xn[:, :, :])
            for tile in range(1, HI):
                split_lo(dve, "mix_in", tile)
            linv, mqkv = v3(lin, L2), v3(mqk, L2)
            bank = fm_take(dve)
            nc.vector.tensor_scalar(linv[0:12, 0, :], ps[0:12, bank, 0:L2], par("b_forget")[0:12, :], None, ALU.add)
            nc.vector.tensor_scalar(linv[0:4, 7, :], ps[32:36, bank, 0:L2], par("b_input")[32:36, :], None,
                                    ALU.add).then_inc(fm_free, 1)
            dve.wait_ge(fm_free, fmc["dve"])
            last = nc.vector.scalar_tensor_tensor(linv[0:12, 2, :], linv[0:12, 0, :], -1.0, linv[0:12, 0, :], ALU.mult, ALU.max)
            last.then_inc(gab_ok, 1)
            cm = v3(par("conv_m"), MCONV)
            for j in range(2 * MH):
                bank = fm_take(dve)
                dve.wait_ge(mc0, j + 1)
                for tap in range(MCONV - 2, -1, -1):
                    d = MCONV - 1 - tap
                    last = nc.vector.scalar_tensor_tensor(mqkv[:, j, d:L2], ps[:, bank, 0:L2 - d], cm[:, j, tap:tap + 1],
                                                          mqkv[:, j, d:L2], ALU.mult, ALU.add)
                    if tap:
                        dlink(dve, last)
                last.then_inc(fm_free, 1)
                split_lo(dve, "mix_in", j + HI)
            dve.wait_ge(gln_ok, 1)
            dlink(dve, nc.vector.scalar_tensor_tensor(linv[0:12, 0, :], linv[0:12, 0, :], 0.0, linv[0:12, 2, :], ALU.min, ALU.subtract))
            dlink(dve, nc.vector.tensor_tensor_scan(linv[0:12, 1, :], bcast(con("ones")[0:12, 0:1], L2), linv[0:12, 0, :], 0.0,
                                                    ALU.mult, ALU.add))
            dlink(dve, nc.vector.tensor_tensor(linv[0:4, 3, :], linv[0:4, 7, :], linv[0:4, 1, :], ALU.subtract))
            dlink(dve, nc.vector.tensor_tensor_scan(linv[0:4, 8, :], linv[0:4, 3, :], linv[0:4, 3, :], 0.0, ALU.max, ALU.max))
            nc.vector.tensor_tensor(linv[0:4, 5, :], linv[0:4, 8, :], linv[0:4, 1, :], ALU.add)
            nc.vector.tensor_scalar(linv[0:4, 4, :], linv[0:4, 8, :], -1.0, None, ALU.mult)
            nc.vector.tensor_scalar(linv[0:12, 6, :], linv[0:12, 1, :], -1.0, None, ALU.mult).then_inc(row_ok, 1)
            for j in range(12):
                bank = fm_take(dve)
                dst = v3(mo, L2)[:, j, :] if j < 4 else v3(fqk, L2)[:, j - 4, :]
                nc.vector.tensor_copy(dst, ps[:, bank, 0:L2]).then_inc(fm_free, 1)
                split_lo(dve, "mix_in", 2 * MH + j + HI)
            for tile in range(20 + HI, 28):
                split_lo(dve, "mix_in", tile)
            dve.wait_ge(col_done, 1)
            cols = v3(colb[:, :], 16)
            for s, rows in ((0, META), (1, P), (2, P)):
                last = nc.vector.tensor_copy(cols[0:rows, s, :], ps[0:rows, 0, s * 16:(s + 1) * 16])
            last.then_inc(col_ok, 1)
            dve.wait_ge(col_ok, 1)
            dve.wait_ge(fss_done, 1)
            nc.vector.tensor_scalar(v3(fsq, L2), ps[:, :, 0:L2], 1.0 / FD, EPS, ALU.mult, ALU.add).then_inc(fvar_ok, 1)
            wv, stmv = v3(wts, 640), v3(stm, 640)
            mT = con("maskT")

            def weights(h):
                dve.wait_ge(ms_done, h + 1)
                b1 = 2 * (h % 2) + 1
                nc.vector.scalar_tensor_tensor(wv[:, h, 0:256], ps[:, b1, 0:256], cols[:, 1, 12 + h:13 + h], mT, ALU.add, ALU.add)
                nc.vector.scalar_tensor_tensor(wv[:, h, 256:384], ps[:, b1, P:256], cols[:, 2, 12 + h:13 + h], mT[:, 0:P],
                                               ALU.add, ALU.add)
                nc.vector.tensor_scalar(wv[0:META, h, 384:640], ps[0:META, b1, 0:256], cols[0:META, 0, 12 + h:13 + h], None,
                                        ALU.add).then_inc(mw_ok, 1)

            def weighted(h):
                dve.wait_ge(mexp_ok, h + 1)
                b0 = 2 * (h % 2)
                nc.vector.scalar_tensor_tensor(stmv[:, h, 0:384], ps[:, b0, 0:384], MD ** -0.5, wv[:, h, 0:384], ALU.mult, ALU.mult)
                nc.vector.scalar_tensor_tensor(stmv[0:META, h, 384:640], ps[0:META, b0 + 1, 256:512], MD ** -0.5,
                                               wv[0:META, h, 384:640], ALU.mult, ALU.mult).then_inc(mst_ok, 1)

            for h in range(MH + 1):
                if h < MH:
                    weights(h)
                if h:
                    weighted(h - 1)
                    if h == 1:
                        dve.wait_ge(fsd_ok, 1)
                    part = fsq[:, (h - 1) * 544:h * 544]
                    nc.vector.reciprocal(part, part).then_inc(dve_step, 1)
                    cnt["dve"] += 1
            dve.wait_ge(dve_step, cnt["dve"])
            nc.vector.scalar_tensor_tensor(fqk[:, 0:1088], fqk[:, 0:1088], par("g_fq"), fsq[:, 0:1088], ALU.mult, ALU.mult)
            nc.vector.scalar_tensor_tensor(fqk[:, 1088:2176], fqk[:, 1088:2176], par("g_fk"), fsq[:, 1088:2176], ALU.mult,
                                           ALU.mult).then_inc(fn_ok, 1)
            dve.wait_ge(mnum_done, MH)
            dve.wait_ge(em_ok, 1)
            for sign, other in ((-1.0, em), (1.0, dn)):
                for b in range(2):
                    last = nc.vector.scalar_tensor_tensor(dn[:, b * 512:(b + 1) * 512], ps[:, 6 + b, :], sign,
                                                          other[:, b * 512:(b + 1) * 512], ALU.mult, ALU.max)
                dlink(dve, last)
            dlink(dve, nc.vector.reciprocal(dn, dn))
            for b in range(2):
                last = nc.vector.tensor_tensor(hn[:, b * 512:(b + 1) * 512], ps[:, 4 + b, :], dn[:, b * 512:(b + 1) * 512], ALU.mult)
            last.then_inc(hn_ok, 1)
            dve.wait_ge(hss_done, 1)
            for b in range(2):
                last = nc.vector.tensor_scalar(dn[:, b * 512:(b + 1) * 512], ps[:, 2 + b, :], 1.0 / MD, EPS, ALU.mult, ALU.add)
            last.then_inc(hvar_ok, 1)

            def mlstm_out(h):
                c = slice(h * 256, (h + 1) * 256)
                dlink(dve, nc.vector.reciprocal(dn[:, c], dn[:, c]))
                dlink(dve, nc.vector.scalar_tensor_tensor(hn[:, c], hn[:, c], par("g_m")[:, h:h + 1], dn[:, c], ALU.mult, ALU.mult))
                nc.vector.tensor_tensor(v3(y2T, SEQ)[:, h, :], hn[:, c], v3(mo, L2)[:, h, META:L2], ALU.mult).then_inc(y2_ok, 1)

            sfxv = v3(sfx, 512)
            m2 = v3(con("mask2"), L2)

            def flogits(u):
                dve.wait_ge(s_done, NH + u + 1)
                if u >= 2:
                    dve.wait_ge(pt_done, NH + u - 1)
                b0, b1, c = 2 * (u % 2), 2 * (u % 2) + 1, 8 * (u % 2)
                nc.vector.scalar_tensor_tensor(bfx[:, 0:L2], ps[:, b0, 0:L2], cols[:, 2, 4 + u:5 + u], m2[:, 1, :], ALU.add, ALU.add)
                dlink(dve, nc.vector.scalar_tensor_tensor(bfx[:, L2:416], ps[:, b0, 0:META + P], cols[:, 1, 4 + u:5 + u],
                                                          m2[:, 0, 0:META + P], ALU.add, ALU.add))
                a = sfxv[:, u % 2, 0:416]
                dlink(dve, nc.vector.scalar_tensor_tensor(a, ps[:, b1, 0:416], FD ** -0.5, bfx[:, 0:416], ALU.mult, ALU.add))
                nc.vector.tensor_reduce(stat[:, 32 + c:33 + c], a[:, 0:L2], AX.X, ALU.max, negate=True)
                nc.vector.tensor_reduce(stat[:, 33 + c:34 + c], a[:, L2:416], AX.X, ALU.max, negate=True).then_inc(max_ok, 1)

            def fprobs(u):
                c = 8 * (u % 2)
                dve.wait_ge(exp_ok, NH + u + 1)
                dlink(dve, nc.vector.reciprocal(tmp[:, 0:2], stat[:, 34 + c:36 + c]))
                a = sfxv[:, u % 2, 0:L2]
                nc.vector.tensor_scalar(a, a, tmp[:, 0:1], None, ALU.mult)
                a = sfxv[:, u % 2, L2:416]
                nc.vector.tensor_scalar(a, a, tmp[:, 1:2], None, ALU.mult).then_inc(p_ok, 1)

            for u in range(FH + 2):
                if u < FH:
                    flogits(u)
                if 1 <= u <= FH:
                    fprobs(u - 1)
                if 1 <= u <= MH:
                    if u == 1:
                        dve.wait_ge(hsd_ok, 1)
                    mlstm_out(u - 1)
                if u >= 3 and u % 2 == 1:
                    heads_out((u - 3) // 2, NH + u - 1, v3(y2T, SEQ)[:, 4 + (u - 3) // 2, :], 0)
            dve_residual(dve, "mix_o")

            dve_norm(dve, "ffn2")
            dve_transpose(dve, "ffn2", own_cols, [(xpT, "g_ffn2")])
            dve_input(dve, "ffn2", peer_x_hi, peer_x_lo)
            dve_ahead("peer_q")
            for j in range(2 * PH):
                bank = fm_take(dve)
                nc.vector.tensor_copy(v3(qhT, SEQ)[:, j, :], ps[:, bank, 0:SEQ]).then_inc(fm_free, 1)
                if j + HI < 2 * PH:
                    split_lo(dve, "peer_q", j + HI)
                else:
                    split_lo(dve, "peer_u", j + HI - 2 * PH)
            scv = scs.rearrange("p (l n) -> p l n", n=NKEY)
            NL = TT * 2 * PH
            tvv, tiv = v3(tv, PK), v3(ti.bitcast(U32), PK)
            dve.wait_ge(sc_ok, 4)

            UPRE = UMID + HI
            lo_at = {"n": HI}

            def next_lo():
                if lo_at["n"] < UPRE:
                    split_lo(dve, "peer_u", lo_at["n"])
                    lo_at["n"] += 1

            def top16(lists, src, vals, idxs, every):
                for part in range(2):
                    for l in range(lists):
                        last = nc.vector.max(vals[:, l, 8 * part:8 * part + 8], src[:, l, :])
                        if l % every == every - 1 or l == lists - 1:
                            last.then_inc(dve_step, 1)
                            cnt["dve"] += 1
                            next_lo()
                    dve.wait_ge(dve_step, cnt["dve"])
                    for l in range(lists):
                        last = nc.vector.max_index(idxs[:, l, 8 * part:8 * part + 8], vals[:, l, 8 * part:8 * part + 8], src[:, l, :])
                        if l % every == every - 1 or l == lists - 1:
                            last.then_inc(dve_step, 1)
                            cnt["dve"] += 1
                            next_lo()
                    dve.wait_ge(dve_step, cnt["dve"])
                    if part == 0:
                        for l in range(lists):
                            last = nc.vector.match_replace(src[:, l, :], vals[:, l, 0:8], src[:, l, :], -3.0e38)
                            if l % every == every - 1 or l == lists - 1:
                                last.then_inc(dve_step, 1)
                                cnt["dve"] += 1
                                next_lo()
                        dve.wait_ge(dve_step, cnt["dve"])

            top16(NL, scv, tvv, tiv, 8)
            NT = TT * PH
            pairs = tv.rearrange("p (l h k) -> p l h k", h=2, k=PK)
            candv = v3(eq, PK * PK)
            for l in range(NT):
                last = nc.vector.tensor_tensor(candv[:, l, :].rearrange("p (a b) -> p a b", b=PK),
                                               bcast(pairs[:, l, 0, :].unsqueeze(2), PK, PK),
                                               bcast(pairs[:, l, 1, :].unsqueeze(1), PK, PK), ALU.add)
                if l % 4 == 3:
                    last.then_inc(dve_step, 1)
                    cnt["dve"] += 1
                    next_lo()
            dve.wait_ge(dve_step, cnt["dve"])
            topv, topiv = v3(tops, PK), v3(topi.bitcast(U32), PK)
            top16(NT, candv, topv, topiv, 4)
            dlink(dve, nc.vector.tensor_copy(tmp[:, 32:32 + NT], topv[:, :, 0]))
            nc.vector.tensor_tensor(topv, topv, bcast(tmp[:, 32:32 + NT].unsqueeze(2), NT, PK), ALU.subtract).then_inc(gsub_ok, 1)
            next_lo()
            pau, pbu = pa.bitcast(U32), pb.bitcast(U32)
            nc.vector.tensor_scalar(pau, topi.bitcast(U32), 4, None, ALU.logical_shift_right)
            dlink(dve, nc.vector.tensor_scalar(pbu, topi.bitcast(U32), 15, None, ALU.bitwise_and))
            ixf = ix.rearrange("p (a n) -> p a n", a=4)
            nc.vector.tensor_copy(cand, ti.bitcast(U32))
            nc.vector.tensor_copy(tmp2[:, 0:256], pau)
            dlink(dve, nc.vector.tensor_copy(tmp2[:, 256:512], pbu))
            next_lo()
            kf = cand.rearrange("p (l h k) -> p l h k", h=2, k=PK)
            eqv = eq.rearrange("p (l k c) -> p l k c", k=PK, c=PK)
            QL = NT // 4
            io = bcast(iota[:, 0:PK].unsqueeze(1).unsqueeze(1), QL, PK, PK)
            for a in range(2):
                place = tmp2[:, 256 * a:256 * (a + 1)].rearrange("p (l k) -> p l k", k=PK)
                for l in range(0, NT, QL):
                    e = eqv[:, l:l + QL]
                    dlink(dve, nc.vector.tensor_tensor(e, bcast(place[:, l:l + QL].unsqueeze(3), QL, PK, PK), io, ALU.is_equal))
                    dlink(dve, nc.vector.tensor_tensor(e, e, bcast(kf[:, l:l + QL, a, :].unsqueeze(2), QL, PK, PK), ALU.mult))
                    next_lo()
                    dlink(dve, nc.vector.tensor_reduce(ixf[:, a, l * PK:(l + QL) * PK], e, AX.X, ALU.add))
                    next_lo()
            dve.wait_ge(gexp_ok, 1)
            dlink(dve, nc.vector.tensor_reduce(tmp[:, 0:NT], topv, AX.X, ALU.add))
            dlink(dve, nc.vector.reciprocal(tmp[:, 16:16 + NT], tmp[:, 0:NT]))
            nc.vector.tensor_tensor(ixf[:, 2, :].rearrange("p (l k) -> p l k", k=PK), topv,
                                    bcast(tmp[:, 16:16 + NT].unsqueeze(2), NT, PK), ALU.mult).then_inc(rt_ok, 1)
            loops = (UPRE - lo_at["n"]) // RING
            if loops:
                first = lo_at["n"]
                with dve.Fori(0, loops) as i:
                    for k in range(RING):
                        split_lo(dve, "peer_u", first + k, i)
                lo_at["n"] += loops * RING
            while lo_at["n"] < UPRE:
                next_lo()
            dve.wait_ge(rt_done, 1)
            nc.vector.tensor_copy(route[:, 0:2, :], v3(ps[:, 6, :], SEQ))
            nc.vector.tensor_copy(route[:, 2, :], ps[:, 7, 0:SEQ]).then_inc(route_ok, 1)
            rest = (NKEY - UPRE) // RING
            with dve.Fori(0, rest) as i:
                for k in range(RING):
                    split_lo(dve, "peer_u", UPRE + k, i)
            for tile in range(UPRE + rest * RING, NKEY):
                split_lo(dve, "peer_u", tile)

            def onehots(b, t, need):
                if need is not None:
                    dve.wait_ge(g_done, need)
                for a in range(2):
                    last = nc.vector.tensor_tensor(oh_rows[b][:, a], bcast(iota.unsqueeze(1), 4, P),
                                                   bcast(route[:, a, bass.ds(t, 4)].unsqueeze(2), 4, P), ALU.is_equal)
                last.then_inc(eq_ok, 1)

            def gated(b, t, need):
                a = acts[:, :, bass.ds(t, 4)]
                dve.wait_ge(g_done, need)
                nc.vector.tensor_tensor(a, a, ps[:, OHB[b], :].rearrange("p (t j) -> p j t", j=NKEY), ALU.mult).then_inc(g_ok, 1)

            dve.wait_ge(route_ok, 1)
            for b in range(2):
                onehots(b, 4 * b, None)
            for tile in range(2):
                split_lo(dve, "peer_v", tile)
            dve.wait_ge(gelu_ok, NKEY)
            AHEAD = OH - 1
            onehots(2, 8, None)
            onehots(3, 12, None)
            gated(0, 0, 1)
            GROUPS = SEQ // 4
            with dve.Fori(0, GROUPS // OH - 1) as i:
                for k in range(1, OH + 1):
                    onehots((k + AHEAD) % OH, i * (4 * OH) + 4 * (k + AHEAD), i * OH + k)
                    gated(k % OH, i * (4 * OH) + 4 * k, i * OH + (k + 1))
            for g in range(GROUPS - AHEAD, GROUPS):
                gated(g % OH, 4 * g, g + 1)
            dve.wait_ge(g_ok, SEQ // 4)

            v0, d0 = plan["peer_v"][0], cnt["dve"]
            for j in range(2):
                split_hidden(dve, acts[:, j, :], j, d0 + j + 1, ph_ok)
            split_lo(dve, "peer_v", 2)

            def behind(tile, j, done, step, it=None):
                dve.wait_ge(tile_done, done)
                split_hidden(dve, acts[:, j, :], tile % 2, step, ph_ok)
                if tile + HI < NKEY:
                    split_lo(dve, "peer_v", tile + HI, it)

            rest = (NKEY - HI) // RING
            with dve.Fori(0, rest) as i:
                for k in range(RING):
                    behind(k, i * RING + (k + 2), i * RING + (v0 + k + 1), i * RING + (d0 + 3 + k), i)
            for tile in range(rest * RING, NKEY - 2):
                behind(tile, tile + 2, v0 + tile + 1, d0 + 3 + tile)
            cnt["dve"] = d0 + NKEY
            rows_wait(dve, "peer_v")
            for t in range(TT):
                for half in range(2):
                    part = x[:, t, half * 512:(half + 1) * 512]
                    last = nc.vector.tensor_tensor(part, ps[:, ROWB[t][half], :], part, ALU.add)
                last.then_inc(fin_ok, 1)


def column_tiles(w, dst):
    k, n = w.shape
    dst[...] = w.reshape(k // P, P, n // P, P).transpose(2, 1, 0, 3).reshape(n // P, P, -1)


def pack_stream(a):
    plan, total = stream_plan()
    out = np.empty((total, P, D), np.float32)

    def part(name):
        at, n = plan[name]
        return out[at:at + n]

    w = a["gla_w_in"][0]
    column_tiles(w[:, 0:512], part("gla_q"))
    column_tiles(w[:, 512:1024], part("gla_k"))
    part("gla_v")[...] = w[:, 1024:2048].reshape(KC, P, D)
    part("gla_r")[...] = w[:, 2048:3072].reshape(KC, P, D)
    part("gla_o")[...] = a["gla_w_o"][0].reshape(KC, P, D)
    for layer in range(2):
        dst = part(f"ffn{layer}")
        up, down = a["ffn_w_up"][layer], a["ffn_w_down"][layer].reshape(FT, P, D)
        cols = np.empty((2 * FT, P, D), np.float32)
        column_tiles(up, cols)
        dst[0], dst[1] = cols[0], cols[FT]
        for f in range(1, FT):
            dst[3 * f - 1], dst[3 * f], dst[3 * f + 1] = cols[f], cols[FT + f], down[f - 1]
        dst[3 * FT - 1] = down[FT - 1]
    w = a["nsa_w_kv"]
    column_tiles(w[:, 0:512], part("nsa_raw"))
    column_tiles(np.concatenate([w[:, 512:768], w[:, 1024:1280]], 1), part("nsa_rot_k"))
    v = np.concatenate([w[:, 768:1024], w[:, 1280:1536]], 1)
    part("nsa_v")[...] = v.reshape(4, 2, P, 512).transpose(0, 2, 1, 3).reshape(4, P, D)
    w = a["nsa_w_in"][0][:, 0:D].reshape(D, 2, 2, NG, ND).transpose(0, 1, 3, 2, 4).reshape(D, D)
    column_tiles(w, part("nsa_q"))
    part("nsa_o")[...] = a["nsa_w_o"][0].reshape(2, 2, NG, ND, D).transpose(0, 2, 1, 3, 4).reshape(KC, P, D)
    for name, key in (("cmp_k", "cmp_k_w1"), ("cmp_v", "cmp_v_w1")):
        part(name)[...] = a[key].reshape(4, 4, P, CHID).transpose(0, 2, 1, 3).reshape(4, P, D)
    w = a["w_in_2"][0]
    column_tiles(w[:, 0:512], part("mix_q"))
    column_tiles(w[:, 512:1024], part("mix_k"))
    column_tiles(w[:, 1536:2048], part("mix_og"))
    column_tiles(w[:, 2056:2568], part("mix_fq"))
    column_tiles(w[:, 2568:3080], part("mix_fk"))
    part("mix_v")[:, :, 0:512] = w[:, 1024:1536].reshape(KC, P, 512)
    part("mix_v")[:, :, 512:1024] = w[:, 3080:3592].reshape(KC, P, 512)
    part("mix_o")[...] = a["w_out_2"][0].reshape(KC, P, D)
    column_tiles(a["peer_query_2"][0], part("peer_q"))
    u = a["peer_u_2"][0].reshape(NKEY, NKEY, KC, P).transpose(1, 3, 2, 0)
    part("peer_u")[...] = u.reshape(NKEY, P, D)
    part("peer_v")[...] = a["peer_v_2"][0].reshape(NKEY, NKEY, D).transpose(1, 0, 2)
    return out


def pack_params(a):
    plan, width = param_plan()
    out = np.zeros((P, width), np.float32)

    def put(name, v, row=0):
        at, w = plan[name]
        v = v.reshape(v.shape[0], -1)
        out[row:row + v.shape[0], at:at + v.shape[1]] = v

    def rows(v):
        return v.reshape(-1, P).T

    for name, v in (("g_mix0", a["norm_mix"][0]), ("g_ffn0", a["norm_ffn"][0]), ("g_kv", a["kv_norm"]),
                    ("g_mix1", a["norm_mix"][1]), ("g_ffn1", a["norm_ffn"][1]), ("g_mix2", a["norm_mix_2"][0]),
                    ("g_ffn2", a["norm_ffn_2"][0]), ("g_gla", a["gla_norm"][0]), ("b_alpha", a["gla_b_alpha"][0]),
                    ("g_m", a["m_out_norm_2"][0])):
        put(name, rows(v))
    for layer in range(2):
        taps = a["ffn_conv_w"][layer].reshape(3, 2, FT, P)
        bias = a["ffn_conv_b"][layer].reshape(1, 2, FT, P)
        put(f"conv{layer}", np.concatenate([taps, bias], 0).transpose(3, 2, 1, 0))
    put("conv_m", a["conv_qk_2"][0].reshape(MCONV, 2 * MH, P).transpose(2, 1, 0))
    put("g_fq", np.concatenate([a["f_q_norm_2"][0]] * 2)[:, None])
    put("g_fk", np.concatenate([a["f_k_norm_2"][0]] * 2)[:, None])
    put("b_forget", np.concatenate([a["b_fgate_m_2"][0], a["b_fgate_f_2"][0]])[:, None])
    put("b_input", a["b_igate_2"][0][:, None], row=32)
    put("pe_k", a["cmp_pe_k"].reshape(CB // 2, P).T)
    put("pe_v", a["cmp_pe_v"].reshape(CB // 2, P).T)
    w2 = a["cmp_k_w2"].reshape(2, P, ND).transpose(1, 0, 2)
    put("w2_k", np.concatenate([w2, w2], 2))
    put("w2_v", a["cmp_v_w2"].reshape(2, P, ND).transpose(1, 0, 2))

    def chunks(w):
        return w.reshape(KC, P, -1).transpose(1, 0, 2)

    put("w_alow", chunks(a["gla_w_in"][0][:, 3072:3088]))
    put("w_aup", a["gla_w_alpha_up"][0])
    put("w_gates", chunks(a["nsa_w_in"][0][:, D:D + 3 * NH]))
    g = np.zeros((D, 36), np.float32)
    w = a["w_in_2"][0]
    g[:, 0:4], g[:, 4:12], g[:, 32:36] = w[:, 2052:2056], w[:, 3592:3600], w[:, 2048:2052]
    put("w_gates2", chunks(g))
    return out


def kernel(**inputs):
    import concourse.bacc as bacc
    from concourse.bass_utils import run_bass_kernel_spmd

    a = {k: np.asarray(v) for k, v in inputs.items()}
    arrays = {
        "stream": pack_stream(a),
        "params": pack_params(a),
        "consts": constants(),
        "keys": np.ascontiguousarray(a["peer_sub_keys_2"][0].reshape(2 * PH, NKEY, PQ).transpose(2, 0, 1)),
        "g_final": np.ascontiguousarray(a["norm_final"]),
        "x_in": np.ascontiguousarray(a["x"][0]),
        "meta_in": np.ascontiguousarray(a["meta_tokens_2"]),
    }
    nc = bacc.Bacc("TRN2", target_bir_lowering=False, num_devices=1)
    args = [nc.dram_tensor(n, v.shape, F32, kind="ExternalInput").ap() for n, v in arrays.items()]
    out = nc.dram_tensor("out", (SEQ, D), F32, kind="ExternalOutput").ap()
    build(nc, *args, out)
    r = run_bass_kernel_spmd(nc, [arrays], core_ids=[0])
    return r.results[0]["out"].reshape(1, SEQ, D)
```
